# Optimizing a Trainium2 kernel written in Bass

```python
import math
import jax, jax.numpy as jnp
from jax import lax
import numpy as np

D_MODEL = 1024
BATCH = 1
SEQ = 512
DEPTH = 2
DEC_BATCH = 8
DEC_SEQ = 1
PAST_LEN = 2048
PAGE_SIZE = 128

N_EVEN = (DEPTH + 1) // 2
N_ODD = DEPTH // 2
D_FF = ((8 * D_MODEL // 3 + 127) // 128) * 128
RMS_EPS = 1e-6
ROPE_THETA = 10000.0
CHUNK = 128
Q_BLOCK = 128
RET_HEADS = 4
RET_DK = D_MODEL // 8
RET_DV = D_MODEL // 4
SSM_HEADS = 16
SSM_HEAD_DIM = 64
SSM_D_INNER = SSM_HEADS * SSM_HEAD_DIM
SSM_STATE = 64
SSM_GROUPS = 2
CONV_W = 4
CONV_DIM = SSM_D_INNER + 2 * SSM_GROUPS * SSM_STATE
HYB_IN = 2 * RET_HEADS * RET_DK + 2 * RET_HEADS * RET_DV + SSM_D_INNER + CONV_DIM + SSM_HEADS
HYB_MIX = RET_HEADS * RET_DV + SSM_D_INNER
MLA_HEADS = 16
Q_LORA = 512
KV_LORA = 256
QK_NOPE = 64
QK_ROPE = 32
V_DIM = 64
MLA_IN = Q_LORA + KV_LORA + QK_ROPE
MLA_SCALE = (QK_NOPE + QK_ROPE) ** -0.5

kernel_name = 'hybrid_retention_ssd_mla_macaron_step'

def rms_norm(x, w):
    xf = x.astype(jnp.float32)
    y = xf * lax.rsqrt(jnp.mean(xf * xf, axis=-1, keepdims=True) + RMS_EPS)
    return (y * w.astype(jnp.float32)).astype(x.dtype)

def swiglu(h, w_in, w_out):
    gate, up = jnp.split(h @ w_in, 2, axis=-1)
    return (jax.nn.silu(gate) * up) @ w_out

def rope(x, pos):
    half = x.shape[-1] // 2
    inv = ROPE_THETA ** (-jnp.arange(half, dtype=jnp.float32) / half)
    ang = pos.astype(jnp.float32)[:, None] * inv[None, :]
    cos = jnp.cos(ang)[None, :, None, :]
    sin = jnp.sin(ang)[None, :, None, :]
    xf = x.astype(jnp.float32)
    x1, x2 = xf[..., :half], xf[..., half:]
    return jnp.concatenate([x1 * cos - x2 * sin, x1 * sin + x2 * cos], axis=-1).astype(x.dtype)

def chunked_decay_recurrence(q, k, v, log_a, state0):
    f32 = jnp.float32
    b, L, h, dk = q.shape
    dv = v.shape[-1]
    c = math.gcd(L, CHUNK)
    n = L // c
    q = q.astype(f32).reshape(b, n, c, h, dk)
    k = k.astype(f32).reshape(b, n, c, h, dk)
    v = v.astype(f32).reshape(b, n, c, h, dv)
    cum = jnp.cumsum(log_a.astype(f32).reshape(b, n, c, h), axis=2).swapaxes(2, 3)
    causal = jnp.tril(jnp.ones((c, c), dtype=bool))
    seg = jnp.exp(jnp.where(causal, cum[..., :, None] - cum[..., None, :], -jnp.inf))
    scores = jnp.einsum('bnihd,bnjhd->bnhij', q, k) * seg
    y_intra = jnp.einsum('bnhij,bnjhe->bnihe', scores, v)
    k_end = k * jnp.exp(cum[..., -1:] - cum).swapaxes(2, 3)[..., None]
    chunk_kv = jnp.einsum('bnjhd,bnjhe->bnhde', k_end, v)
    chunk_decay = jnp.exp(cum[..., -1])

    def step(s, inp):
        dec, kv = inp
        return dec[..., None, None] * s + kv, s

    s_final, s_prev = lax.scan(step, state0.astype(f32),
                               (chunk_decay.swapaxes(0, 1), chunk_kv.swapaxes(0, 1)))
    s_prev = s_prev.swapaxes(0, 1)
    q_in = q * jnp.exp(cum).swapaxes(2, 3)[..., None]
    y_inter = jnp.einsum('bnihd,bnhde->bnihe', q_in, s_prev)
    return (y_intra + y_inter).reshape(b, L, h, dv), s_final

def causal_depthwise_conv(x_full, w, bias):
    y = lax.conv_general_dilated(x_full, w[:, None, :].astype(x_full.dtype), window_strides=(1,),
                                 padding='VALID', dimension_numbers=('NWC', 'WIO', 'NWC'),
                                 feature_group_count=x_full.shape[-1])
    return y + bias.astype(x_full.dtype)

def hybrid_mixer(h, pos, ret_s0, ssm_s0, conv_s0, w_in, w_out, conv_w, conv_b, dt_bias, a_log,
                 d_skip, norm_w):
    f32 = jnp.float32
    b, L, _ = h.shape
    qk = RET_HEADS * RET_DK
    vv = RET_HEADS * RET_DV
    cuts = [qk, 2 * qk, 2 * qk + vv, 2 * qk + 2 * vv, 2 * qk + 2 * vv + SSM_D_INNER,
            2 * qk + 2 * vv + SSM_D_INNER + CONV_DIM]
    q, k, v, g, z, xbc_raw, dt_raw = jnp.split(h @ w_in, cuts, axis=-1)
    q = rope(q.reshape(b, L, RET_HEADS, RET_DK), pos)
    k = rope(k.reshape(b, L, RET_HEADS, RET_DK), pos) * (RET_DK ** -0.5)
    v = v.reshape(b, L, RET_HEADS, RET_DV)
    log_gamma = jnp.log1p(-jnp.exp2(-5.0 - jnp.arange(RET_HEADS, dtype=f32)))
    o_ret, ret_s = chunked_decay_recurrence(q, k, v, jnp.broadcast_to(log_gamma, (b, L, RET_HEADS)),
                                            ret_s0)
    o_ret = o_ret * lax.rsqrt(jnp.mean(o_ret * o_ret, axis=-1, keepdims=True) + RMS_EPS)
    o_ret = o_ret.reshape(b, L, vv) * jax.nn.silu(g.astype(f32))
    xbc_full = jnp.concatenate([conv_s0.astype(h.dtype), xbc_raw], axis=1)
    new_conv = xbc_full[:, L:]
    xbc = jax.nn.silu(causal_depthwise_conv(xbc_full, conv_w, conv_b))
    xs, bm, cm = jnp.split(xbc, [SSM_D_INNER, SSM_D_INNER + SSM_GROUPS * SSM_STATE], axis=-1)
    xs = xs.reshape(b, L, SSM_HEADS, SSM_HEAD_DIM).astype(f32)
    rep = SSM_HEADS // SSM_GROUPS
    bm = jnp.repeat(bm.reshape(b, L, SSM_GROUPS, SSM_STATE), rep, axis=2)
    cm = jnp.repeat(cm.reshape(b, L, SSM_GROUPS, SSM_STATE), rep, axis=2)
    dt = jax.nn.softplus(dt_raw.astype(f32) + dt_bias.astype(f32))
    a = -jnp.exp(a_log.astype(f32))
    y, ssm_s = chunked_decay_recurrence(cm, bm, xs * dt[..., None], dt * a, ssm_s0)
    y = y + d_skip.astype(f32)[:, None] * xs
    yg = (y.reshape(b, L, SSM_D_INNER) * jax.nn.silu(z.astype(f32))).reshape(b, L, SSM_GROUPS, -1)
    yg = yg * lax.rsqrt(jnp.mean(yg * yg, axis=-1, keepdims=True) + RMS_EPS)
    y = yg.reshape(b, L, SSM_D_INNER) * norm_w.astype(f32)
    mixed = jnp.concatenate([o_ret, y], axis=-1).astype(h.dtype)
    return (mixed @ w_out, ret_s.astype(ret_s0.dtype), ssm_s.astype(ssm_s0.dtype), new_conv)

def mla_project(h, pos, w_in, q_norm_w, kv_norm_w, w_uq):
    b, L, _ = h.shape
    cq, ckv, kr = jnp.split(h @ w_in, [Q_LORA, Q_LORA + KV_LORA], axis=-1)
    q = (rms_norm(cq, q_norm_w) @ w_uq).reshape(b, L, MLA_HEADS, QK_NOPE + QK_ROPE)
    q_nope = q[..., :QK_NOPE]
    q_rope = rope(q[..., QK_NOPE:], pos)
    ckv = rms_norm(ckv, kv_norm_w)
    kr = rope(kr[:, :, None, :], pos)[:, :, 0, :]
    return q_nope, q_rope, ckv, kr

def mla_prompt_attend(q_nope, q_rope, ckv, kr, w_uk, w_uv):
    b, S, H, _ = q_nope.shape
    k_nope = jnp.einsum('bsc,chd->bshd', ckv, w_uk)
    v = jnp.einsum('bsc,chv->bshv', ckv, w_uv)
    nb = S // Q_BLOCK
    kpos = jnp.arange(S)

    def blocks(t):
        return t.reshape(b, nb, Q_BLOCK, *t.shape[2:]).swapaxes(0, 1)

    def attend(args):
        qn, qr, i = args
        s = (jnp.einsum('bqhd,bkhd->bhqk', qn, k_nope)
             + jnp.einsum('bqhr,bkr->bhqk', qr, kr)).astype(jnp.float32) * MLA_SCALE
        qpos = i * Q_BLOCK + jnp.arange(Q_BLOCK)
        s = jnp.where(kpos[None, :] <= qpos[:, None], s, -jnp.inf)
        p = jax.nn.softmax(s, axis=-1).astype(v.dtype)
        return jnp.einsum('bhqk,bkhv->bqhv', p, v)

    o = lax.map(attend, (blocks(q_nope), blocks(q_rope), jnp.arange(nb)))
    return o.swapaxes(0, 1).reshape(b, S, H, V_DIM)

def mla_sample_attend(q_nope, q_rope, ckv_new, kr_new, page_table, cache_ckv, cache_krope, layer_idx,
                      w_uk, w_uv):
    f32 = jnp.float32
    q_lat = jnp.einsum('bthd,chd->bthc', q_nope.astype(f32), w_uk.astype(f32)) * MLA_SCALE
    q_r = q_rope.astype(f32) * MLA_SCALE
    b, T, H, _ = q_lat.shape

    def scores(ckv, kr):
        return jnp.einsum('bthc,bpc->bhtp', q_lat, ckv) + jnp.einsum('bthr,bpr->bhtp', q_r, kr)

    def merge(carry, s, ckv):
        m, l, acc = carry
        m_new = jnp.maximum(m, jnp.max(s, axis=-1))
        corr = jnp.exp(m - m_new)
        p = jnp.exp(s - m_new[..., None])
        return (m_new, l * corr + jnp.sum(p, axis=-1),
                acc * corr[..., None] + jnp.einsum('bhtp,bpc->bhtc', p, ckv))

    def page_step(carry, pages):
        ckv = cache_ckv[layer_idx, pages].astype(f32)
        kr = cache_krope[layer_idx, pages].astype(f32)
        return merge(carry, scores(ckv, kr), ckv), None

    init = (jnp.full((b, H, T), -jnp.inf, f32), jnp.zeros((b, H, T), f32),
            jnp.zeros((b, H, T, KV_LORA), f32))
    carry, _ = lax.scan(page_step, init, page_table.T)
    ckv_n = ckv_new.astype(f32)
    s_new = scores(ckv_n, kr_new.astype(f32))
    s_new = jnp.where(jnp.tril(jnp.ones((T, T), dtype=bool)), s_new, -jnp.inf)
    m, l, acc = merge(carry, s_new, ckv_n)
    o_lat = (acc / l[..., None]).swapaxes(1, 2)
    return jnp.einsum('bthc,chv->bthv', o_lat, w_uv.astype(f32)).astype(q_nope.dtype)

def setup_inputs(seed: int = 0) -> dict:
    key = jax.random.key(seed)
    keys = jax.random.split(key, 40)
    f32 = jnp.float32

    def nrm(i, shape, scale):
        return jax.random.normal(keys[i], shape, f32) * scale

    n_pages = PAST_LEN // PAGE_SIZE
    n_used = DEC_BATCH * n_pages
    n_phys = n_used + (n_used + 3) // 4
    x_prompt = nrm(0, (BATCH, SEQ, D_MODEL), 1.0)
    x_sample = nrm(1, (DEC_BATCH, DEC_SEQ, D_MODEL), 1.0)
    state_ret = nrm(2, (N_EVEN, DEC_BATCH, RET_HEADS, RET_DK, RET_DV), 1.0)
    state_ssm = nrm(3, (N_EVEN, DEC_BATCH, SSM_HEADS, SSM_STATE, SSM_HEAD_DIM), 0.5)
    state_conv = nrm(4, (N_EVEN, DEC_BATCH, CONV_W - 1, CONV_DIM), 1.0)
    cache_ckv = nrm(5, (N_ODD, n_phys, PAGE_SIZE, KV_LORA), 1.0)
    cache_krope = nrm(6, (N_ODD, n_phys, PAGE_SIZE, QK_ROPE), 1.0)
    page_table = jax.random.permutation(keys[7], n_phys)[:n_used].reshape(DEC_BATCH, n_pages).astype(jnp.int32)
    norm_ffn1 = 1.0 + nrm(8, (DEPTH, D_MODEL), 0.05)
    ffn1_w_in = nrm(9, (DEPTH, D_MODEL, 2 * D_FF), D_MODEL ** -0.5)
    ffn1_w_out = nrm(10, (DEPTH, D_FF, D_MODEL), D_FF ** -0.5)
    norm_mix = 1.0 + nrm(11, (DEPTH, D_MODEL), 0.05)
    norm_ffn2 = 1.0 + nrm(12, (DEPTH, D_MODEL), 0.05)
    ffn2_w_in = nrm(13, (DEPTH, D_MODEL, 2 * D_FF), D_MODEL ** -0.5)
    ffn2_w_out = nrm(14, (DEPTH, D_FF, D_MODEL), D_FF ** -0.5)
    hyb_w_in = nrm(15, (N_EVEN, D_MODEL, HYB_IN), D_MODEL ** -0.5)
    hyb_w_out = nrm(16, (N_EVEN, HYB_MIX, D_MODEL), HYB_MIX ** -0.5)
    hyb_conv_w = nrm(17, (N_EVEN, CONV_W, CONV_DIM), CONV_W ** -0.5)
    hyb_conv_b = nrm(18, (N_EVEN, CONV_DIM), 0.02)
    dt0 = jnp.exp(jax.random.uniform(keys[19], (N_EVEN, SSM_HEADS), f32,
                                     minval=math.log(1e-3), maxval=math.log(1e-1)))
    hyb_dt_bias = dt0 + jnp.log(-jnp.expm1(-dt0))
    hyb_a_log = jnp.log(jax.random.uniform(keys[20], (N_EVEN, SSM_HEADS), f32, minval=1.0, maxval=16.0))
    hyb_d_skip = 1.0 + nrm(21, (N_EVEN, SSM_HEADS), 0.1)
    hyb_norm_w = 1.0 + nrm(22, (N_EVEN, SSM_D_INNER), 0.05)
    mla_w_in = nrm(23, (N_ODD, D_MODEL, MLA_IN), D_MODEL ** -0.5)
    mla_q_norm_w = 1.0 + nrm(24, (N_ODD, Q_LORA), 0.05)
    mla_kv_norm_w = 1.0 + nrm(25, (N_ODD, KV_LORA), 0.05)
    mla_w_uq = nrm(26, (N_ODD, Q_LORA, MLA_HEADS * (QK_NOPE + QK_ROPE)), Q_LORA ** -0.5)
    mla_w_uk = nrm(27, (N_ODD, KV_LORA, MLA_HEADS, QK_NOPE), KV_LORA ** -0.5)
    mla_w_uv = nrm(28, (N_ODD, KV_LORA, MLA_HEADS, V_DIM), KV_LORA ** -0.5)
    mla_w_o = nrm(29, (N_ODD, MLA_HEADS * V_DIM, D_MODEL), (MLA_HEADS * V_DIM) ** -0.5)
    final_norm_w = 1.0 + nrm(30, (D_MODEL,), 0.05)
    return {'x_prompt': x_prompt, 'x_sample': x_sample, 'state_ret': state_ret, 'state_ssm': state_ssm,
            'state_conv': state_conv, 'cache_ckv': cache_ckv, 'cache_krope': cache_krope,
            'page_table': page_table, 'norm_ffn1': norm_ffn1, 'ffn1_w_in': ffn1_w_in,
            'ffn1_w_out': ffn1_w_out, 'norm_mix': norm_mix, 'norm_ffn2': norm_ffn2,
            'ffn2_w_in': ffn2_w_in, 'ffn2_w_out': ffn2_w_out, 'hyb_w_in': hyb_w_in,
            'hyb_w_out': hyb_w_out, 'hyb_conv_w': hyb_conv_w, 'hyb_conv_b': hyb_conv_b,
            'hyb_dt_bias': hyb_dt_bias, 'hyb_a_log': hyb_a_log, 'hyb_d_skip': hyb_d_skip,
            'hyb_norm_w': hyb_norm_w, 'mla_w_in': mla_w_in, 'mla_q_norm_w': mla_q_norm_w,
            'mla_kv_norm_w': mla_kv_norm_w, 'mla_w_uq': mla_w_uq, 'mla_w_uk': mla_w_uk,
            'mla_w_uv': mla_w_uv, 'mla_w_o': mla_w_o, 'final_norm_w': final_norm_w}

def reference(x_prompt, x_sample, state_ret, state_ssm, state_conv, cache_ckv, cache_krope, page_table,
              norm_ffn1, ffn1_w_in, ffn1_w_out, norm_mix, norm_ffn2, ffn2_w_in, ffn2_w_out,
              hyb_w_in, hyb_w_out, hyb_conv_w, hyb_conv_b, hyb_dt_bias, hyb_a_log, hyb_d_skip,
              hyb_norm_w, mla_w_in, mla_q_norm_w, mla_kv_norm_w, mla_w_uq, mla_w_uk, mla_w_uv,
              mla_w_o, final_norm_w):
    xp, xs = x_prompt, x_sample
    bp, sp = xp.shape[0], xp.shape[1]
    pos_p = jnp.arange(sp)
    pos_s = PAST_LEN + jnp.arange(xs.shape[1])
    ret_p, ret_s, ssm_p, ssm_s, conv_p, conv_s = [], [], [], [], [], []
    ckv_p, ckv_s, kr_p, kr_s = [], [], [], []
    for layer in range(DEPTH):
        j = layer // 2
        xp = xp + 0.5 * swiglu(rms_norm(xp, norm_ffn1[layer]), ffn1_w_in[layer], ffn1_w_out[layer])
        xs = xs + 0.5 * swiglu(rms_norm(xs, norm_ffn1[layer]), ffn1_w_in[layer], ffn1_w_out[layer])
        hp = rms_norm(xp, norm_mix[layer])
        hs = rms_norm(xs, norm_mix[layer])
        if layer % 2 == 0:
            wts = (hyb_w_in[j], hyb_w_out[j], hyb_conv_w[j], hyb_conv_b[j], hyb_dt_bias[j],
                   hyb_a_log[j], hyb_d_skip[j], hyb_norm_w[j])
            mp, r_p, s_p, c_p = hybrid_mixer(
                hp, pos_p, jnp.zeros((bp, RET_HEADS, RET_DK, RET_DV), hp.dtype),
                jnp.zeros((bp, SSM_HEADS, SSM_STATE, SSM_HEAD_DIM), hp.dtype),
                jnp.zeros((bp, CONV_W - 1, CONV_DIM), hp.dtype), *wts)
            ms, r_s, s_s, c_s = hybrid_mixer(hs, pos_s, state_ret[j], state_ssm[j], state_conv[j], *wts)
            ret_p.append(r_p); ret_s.append(r_s); ssm_p.append(s_p); ssm_s.append(s_s)
            conv_p.append(c_p); conv_s.append(c_s)
        else:
            qn, qr, ck, kr = mla_project(hp, pos_p, mla_w_in[j], mla_q_norm_w[j], mla_kv_norm_w[j], mla_w_uq[j])
            op = mla_prompt_attend(qn, qr, ck, kr, mla_w_uk[j], mla_w_uv[j])
            mp = op.reshape(bp, sp, MLA_HEADS * V_DIM) @ mla_w_o[j]
            ckv_p.append(ck); kr_p.append(kr)
            qn, qr, ck, kr = mla_project(hs, pos_s, mla_w_in[j], mla_q_norm_w[j], mla_kv_norm_w[j], mla_w_uq[j])
            os_ = mla_sample_attend(qn, qr, ck, kr, page_table, cache_ckv, cache_krope, j,
                                    mla_w_uk[j], mla_w_uv[j])
            ms = os_.reshape(xs.shape[0], xs.shape[1], MLA_HEADS * V_DIM) @ mla_w_o[j]
            ckv_s.append(ck); kr_s.append(kr)
        xp = xp + mp
        xs = xs + ms
        xp = xp + 0.5 * swiglu(rms_norm(xp, norm_ffn2[layer]), ffn2_w_in[layer], ffn2_w_out[layer])
        xs = xs + 0.5 * swiglu(rms_norm(xs, norm_ffn2[layer]), ffn2_w_in[layer], ffn2_w_out[layer])
    y_prompt = rms_norm(xp, final_norm_w)
    y_sample = rms_norm(xs, final_norm_w)
    return (y_prompt, y_sample, jnp.stack(ret_p), jnp.stack(ret_s), jnp.stack(ssm_p), jnp.stack(ssm_s),
            jnp.stack(conv_p), jnp.stack(conv_s), jnp.stack(ckv_p), jnp.stack(ckv_s),
            jnp.stack(kr_p), jnp.stack(kr_s))


_drawn_inputs = setup_inputs


def setup_inputs(seed=0):
    import zlib

    import numpy as np

    out = dict(_drawn_inputs(seed))
    spreads = {}
    factors = {'cache_krope': 3.903, 'mla_q_norm_w': 8.0}
    for name, (base, spread) in spreads.items():
        noise = np.random.default_rng([zlib.crc32(name.encode()), seed]).standard_normal(out[name].shape)
        drawn = base * np.exp(spread * noise) if base else spread * noise
        out[name] = __import__('jax').numpy.asarray(drawn.astype(out[name].dtype))
    for name, factor in factors.items():
        out[name] = (out[name] * factor).astype(out[name].dtype)
    return out
```

```python
import numpy as np
import concourse.bass as bass
from concourse import mybir
from contextlib import ExitStack

F32 = mybir.dt.float32
F32R = mybir.dt.float32r
I32 = mybir.dt.int32
ALU = mybir.AluOpType
ACT = mybir.ActivationFunctionType
AX = mybir.AxisListType
RMAX = bass.bass_isa.ReduceOp.max

P = 128
D = 1024
KD = D // P
NP_ = 512
NS = 8
T = NP_ + NS
TH = T // 2
NTT = NP_ // P
FF = 2816
KF = FF // P
EPS = 1e-6
PAST, PAGE = 2048, 128
NPG = PAST // PAGE
N_PHYS = 160
RH, RDK, RDV = 4, 128, 256
SH, SHD = 16, 64
CONV_W = 4
XBC = 10
MH, NOPE, ROPE, VD = 16, 64, 32, 64
QL, KVL = 512, 256
MLA_SCALE = (NOPE + ROPE) ** -0.5
NEG = -1e30

R = 4
CW = 4 * P

V_FFN1, V_MIX, V_FFN2 = (0, 24), (8, 32), (16, 40)
V_FINAL, V_CONVW, V_CONVB, V_DSKIP, V_HNORM, V_QNORM, V_KVNORM, V_DTB, V_ALOG, V_KEND = 48, 56, 96, 106, 114, 122, 126, 128, 144, 160
V_COLS = 176
NORM_COL = [V_FFN1[0], V_MIX[0], V_FFN2[0], V_FFN1[1], V_MIX[1], V_FFN2[1], V_FINAL]


class Shared:
    pass


class Plan:

    def __init__(self):
        self.n, self.turns = 0, [0, 0]
        self.set_of, self.turn_of = {}, {}
        self.first, self.count = {}, {}
        self.chunks = []
        self.order = []

    def step(self, name, chunks=0, unused=0):
        s = self.n % 2
        self.set_of[name], self.turn_of[name] = s, self.turns[s]
        self.turns[s] += 1
        self.n += 1
        self.first[name], self.count[name] = len(self.chunks), chunks + unused
        for c in range(chunks):
            self.chunks.append((name, c == chunks - 1, True))
        for c in range(unused):
            self.chunks.append((name, False, False))
        self.order.append(name)

    def used_through(self, n):
        return sum(1 for _, last, used in self.chunks[:n + 1] if used and not last)


def ffn_steps(plan, f):
    for g in range(KF):
        plan.step((f, "in", g), 4)
        if g == 0:
            plan.step((f, "stats"))
    for g in range(4):
        plan.step((f, "out", g), 11, 1)


def make_plan(phases):
    plan = Plan()
    for ph in phases:
        if ph in FFNS:
            ffn_steps(plan, ph)
        elif ph == "hyb":
            hyb_steps(plan)
        else:
            mla_steps(plan)
    plan.step("final stats")
    while len(plan.chunks) % R or len(plan.chunks) < 0:
        plan.chunks.append(("pad", False, False))
    for _ in range(R):
        plan.chunks.append(("pad", False, False))
    return plan


STORES = {"hyb": 5, "mla": 2}
FFNS = ("a0", "b0", "a1", "b1")
PHASES = ("a0", "hyb", "b0", "a1", "mla", "b1")


def hyb_steps(plan):
    for g in range(8):
        plan.step(("hin", g), 4)
        if g == 0:
            plan.step("hyb stats")
    for g in range(8, 12):
        plan.step(("hin", g), 4)
    plan.step("ret kT")
    plan.step("ret vT0")
    plan.step("ret vT1")
    for h in range(RH):
        plan.step(("ret S", h))
        plan.step(("ret O", h))
    plan.step("ret sT")
    for p in range(NS // 2):
        plan.step(("ret outer", p))
        plan.step(("ret y", p))
    plan.step(("ret norm", 0))
    plan.step(("ret norm", 1))
    for g in range(12, 21):
        plan.step(("hin", g), 4)
    plan.step(("hin", 21), 2)
    plan.step("ssm dtT")
    plan.step("ssm xT0")
    plan.step("ssm xT1")
    plan.step("ssm BT")
    plan.step("ssm sums")
    for c in range(NTT):
        plan.step(("ssm sc", c))
        plan.step(("ssm D", c))
        plan.step(("ssm y", c))
    plan.step("ssm sT")
    plan.step("ssm dec")
    plan.step(("ssm outer", 0))
    plan.step(("ssm outer", 1))
    plan.step("ssm ys")
    plan.step("ssm norm")
    for g in range(4):
        plan.step(("hout", g), 8)


def mla_steps(plan):
    plan.step(("min", 0), 4)
    plan.step("mla stats")
    plan.step(("min", 1), 4)
    plan.step(("min", 2), 4)
    plan.step(("min", 3), 2)
    plan.step("mla cnorm")
    for g in range(8):
        plan.step(("uq", g), 2)
    plan.step("smp qlat")
    for b in range(NS):
        plan.step(("smp S", b))
        plan.step(("smp PV", b))
    plan.step("smp O")
    for g in range(4):
        plan.step(("uk", g), 1)
    for g in range(2):
        plan.step(("uv", g), 2)
    plan.step(("att S", 0))
    for h in range(MH):
        if h + 1 < MH:
            plan.step(("att S", h + 1))
        plan.step(("att T", h))
        plan.step(("att O", h))
    plan.step("att OT0")
    plan.step("att OT1")
    for g in range(4):
        plan.step(("wo", g), 4)


def program(nc, io, phases=PHASES):
    plan = make_plan(phases)
    NCH = len(plan.chunks)

    BASE = 16512
    cursor = [BASE]

    def at(name, shape, offset, dtype=F32):
        return nc.alloc_sbuf_tensor_at(name, shape, dtype, offset=offset)

    def sb(name, shape, dtype=F32):
        off = cursor[0]
        cursor[0] += (int(np.prod(shape[1:])) * 4 + 31) // 32 * 32
        return at(name, shape, off, dtype), off

    XT, _ = sb("residual", [P, KD, T])
    XH, XH_OFF = sb("x_high", [P, KD, T], F32R)
    XL, XL_OFF = sb("x_low", [P, KD, T], F32R)
    WRAW, _ = sb("w_raw", [P, R, CW])
    WH, _ = sb("w_high", [P, R, CW], F32R)
    WL, _ = sb("w_low", [P, R, CW], F32R)
    RSTD, _ = sb("rstd", [P, T])
    SQS, SQS_OFF = sb("square_sums", [P, 2, T])
    SQT, SQT_OFF = sb("squares", [P, 2, T])
    RCP = at("rcp", [P, T], SQT_OFF)
    VT, VT_OFF = sb("variance", [P, T])
    GU, GU_OFF = sb("gate_up", [P, 2, 2, T])
    SGT, SG_OFF = sb("silu_gate", [P, 2, T])
    HT, HT_OFF = sb("hidden", [P, 2, T])
    PV, _ = sb("vectors", [P, V_COLS])
    CON, _ = sb("constants", [P, 5, P])
    REGION = cursor[0]
    IDENT, ONES, UPTO, AFTER, NEGM = (CON[:, i, :] for i in range(5))
    HH = at("hidden_high", [P, KF, T], REGION, F32R)
    HL = at("hidden_low", [P, KF, T], REGION + KF * T * 4, F32R)

    PS = nc.alloc_psum_tensor("psum", [P, 8, 512], F32)

    stack = ExitStack()
    sem = lambda name: stack.enter_context(nc.semaphore(name))
    w_loaded = [sem(f"w_loaded{i}") for i in range(R)]
    w_high = sem("w_high_done")
    w_split = sem("w_split_done")
    w_used = sem("w_used")
    acc_full = [sem(f"acc_full{i}") for i in range(2)]
    acc_free = [sem(f"acc_free{i}") for i in range(2)]
    x_loaded, v_loaded = sem("x_loaded"), sem("vectors_loaded")
    squares_done, squares_added = sem("squares_done"), sem("squares_added")
    xh_done, xl_done = sem("x_high_done"), sem("x_low_done")
    rcp_done, rstd_done = sem("rcp_done"), sem("rstd_done")
    silu_done, hid_done = sem("silu_done"), sem("hidden_done")
    hh_done, hl_done = sem("hidden_high_done"), sem("hidden_low_done")
    dve_seq, act_seq, pool_seq = sem("dve_seq"), sem("act_seq"), sem("pool_seq")
    out_stored = sem("outputs_stored")
    y_done = sem("y_done")

    def bank0(step):
        return 4 * plan.set_of[step]

    def acc(step, banks=4):
        return PS[:, bank0(step):bank0(step) + banks, 0:TH]

    def halves(ap):
        return ap.rearrange("p (b t) -> p b t", b=2)

    def wait_full(eng, step, i=None):
        n = plan.turn_of[step] + 1
        eng.wait_ge(acc_full[plan.set_of[step]], n if i is None else n + i)

    def wait_free(eng, step, i=None):
        n = plan.turn_of[step] + 1
        eng.wait_ge(acc_free[plan.set_of[step]], n if i is None else n + i)

    def acquire(pe, step, i=None):
        n = plan.turn_of[step]
        if n:
            pe.wait_ge(acc_free[plan.set_of[step]], n if i is None else n + i)

    nn_of = {}
    for n, ph in enumerate(phases):
        nn_of[ph] = n
    NN = len(phases)
    norm_col = [NORM_COL[PHASES.index(ph)] for ph in phases] + [V_FINAL]

    ffn_index = {f: n for n, f in enumerate(ph for ph in phases if ph in FFNS)}

    def wait_stored(eng, f):
        n = nn_of[f]
        if n and phases[n - 1] in STORES:
            eng.wait_ge(out_stored, 16 * sum(STORES[ph] for ph in phases[:n] if ph in STORES))

    def slot_free(eng, n, i=None, used=0, split=0):
        if n < R:
            return
        step, last, real = plan.chunks[n - R]
        if not real:
            eng.wait_ge(w_split, n - R + 1 if i is None else split * i + (n - R + 1))
        elif last:
            wait_full(eng, step, i)
        else:
            k = plan.used_through(n - R)
            eng.wait_ge(w_used, k if i is None else used * i + k)

    def split_high(act, n, i=None, used=0, split=0, per_slot=0):
        slot = n % R
        k = 16 * (n // R + 1)
        act.wait_ge(w_loaded[slot], k if i is None else 16 * per_slot * i + k)
        slot_free(act, n, i, used, split)
        nc.scalar.activation(WH[:, slot, :], WRAW[:, slot, :], ACT.Copy).then_inc(w_high, 1)

    def split_low(dve, n, i=None, per=0):
        slot = n % R
        dve.wait_ge(w_high, n + 1 if i is None else per * i + (n + 1))
        nc.vector.tensor_tensor(WL[:, slot, :], WRAW[:, slot, :], WH[:, slot, :].bitcast(F32),
                                ALU.subtract).then_inc(w_split, 1)

    def gemm(pe, step, mtiles, ktiles, rhs, i=None, split=0, before_k=None, cols=TH):
        acquire(pe, step, i)
        first, b0 = plan.first[step], bank0(step)
        blocks = [(k, m) for k in range(ktiles) for m in range(mtiles)]
        for c in range((len(blocks) + 3) // 4):
            n = first + c
            slot = n % R
            pe.wait_ge(w_split, n + 1 if i is None else split * i + (n + 1))
            for j, (k, m) in enumerate(blocks[4 * c:4 * c + 4]):
                if before_k and m == 0:
                    before_k(k)
                wh, wl = (w[:, slot, j * P:(j + 1) * P] for w in (WH, WL))
                xh, xl = rhs(k)
                for w, x, start, stop in ((wh, xh, k == 0, False), (wh, xl, False, False),
                                          (wl, xh, False, k == ktiles - 1)):
                    for half in range(2):
                        mm = nc.tensor.matmul(PS[:, b0 + 2 * m + half, 0:cols], w,
                                              x[:, half * cols:(half + 1) * cols], start=start, stop=stop)
            if 4 * c + 4 >= len(blocks):
                mm.then_inc(acc_full[plan.set_of[step]], 1)
            else:
                mm.then_inc(w_used, 1)

    def x_rhs(k):
        return XH[:, k, :], XL[:, k, :]

    def pe_stats(pe, step, nn):
        acquire(pe, step)
        pe.wait_ge(squares_added, 4 * (nn + 1))
        b0 = bank0(step)
        for half in range(2):
            for j in range(2):
                mm = nc.tensor.matmul(PS[:, b0 + half, 0:TH], ONES, SQS[:, j, half * TH:(half + 1) * TH],
                                      start=j == 0, stop=j == 1)
        mm.then_inc(acc_full[plan.set_of[step]], 1)

    def first_wait(pe, nn):
        return lambda k: pe.wait_ge(xl_done, KD * nn + k + 1)

    e = Shared()
    e.AFTER, e.GU, e.GU_OFF, e.IDENT, e.NEGM, e.ONES = AFTER, GU, GU_OFF, IDENT, NEGM, ONES
    e.PS, e.PV, e.REGION, e.RSTD, e.SQS_OFF = PS, PV, REGION, RSTD, SQS_OFF
    e.SQT_OFF, e.UPTO, e.VT_OFF, e.WH, e.WL = SQT_OFF, UPTO, VT_OFF, WH, WL
    e.XH, e.XH_OFF, e.XL, e.acc, e.acc_free = XH, XH_OFF, XL, acc, acc_free
    e.acc_full, e.acquire, e.at, e.bank0, e.first_wait = acc_full, acquire, at, bank0, first_wait
    e.gemm, e.halves, e.io, e.nc, e.nn_of = gemm, halves, io, nc, nn_of
    e.out_stored, e.pe_stats, e.phases, e.plan, e.sem = out_stored, pe_stats, phases, plan, sem
    e.w_split, e.w_used, e.wait_free, e.wait_full, e.x_rhs = w_split, w_used, wait_free, wait_full, x_rhs
    hy = hyb_parts(e) if "hyb" in phases else None
    ml = mla_parts(e) if "mla" in phases else None

    block = stack.enter_context(nc.Block())

    @block.sync
    def _(sp):
        def chunk(n):
            if n >= R:
                sp.wait_ge(w_split, n + 1 - R)
            sp.dma_start(WRAW[:, n % R, :], io["weights"][n]).then_inc(w_loaded[n % R], 16)

        def weight_chunks(n0, n1):
            n1 = NCH if n1 is None else n1
            while n0 < n1 and (n0 < R or n0 % R):
                chunk(n0)
                n0 += 1
            if n1 // R - n0 // R > 1:
                with sp.Fori(n0 // R, n1 // R) as i:
                    for s in range(R):
                        sp.wait_ge(w_split, R * i + (s + 1 - R))
                        sp.dma_start(WRAW[:, s, :], io["weights"][bass.ds(R * i + s, 1)]
                                     .rearrange("a p n -> (a p) n")).then_inc(w_loaded[s], 16)
                n0 = n1 // R * R
            for n in range(n0, n1):
                chunk(n)

        if ml:
            ml.sp(sp, weight_chunks)
        else:
            weight_chunks(0, None)
        for s in range(R):
            sp.wait_ge(w_loaded[s], 16 * (NCH // R))

    @block.tensor
    def _(pe):
        def ffn(f):
            nn = nn_of[f]
            gemm(pe, (f, "in", 0), 2, KD, x_rhs, before_k=first_wait(pe, nn))
            pe_stats(pe, (f, "stats"), nn)
            gemm(pe, (f, "in", 1), 2, KD, x_rhs)
            with pe.Fori(0, (KF - 2) // 2) as i:
                for g in (2, 3):
                    gemm(pe, (f, "in", g), 2, KD, x_rhs, i, 8)
            done = KF * (ffn_index[f] + 1)
            h_rhs = lambda k: (HH[:, k, :], HL[:, k, :])
            for g in (0, 1):
                gemm(pe, (f, "out", g), 2, KF, h_rhs,
                     before_k=(lambda k: pe.wait_ge(hl_done, done - KF + k + 1)) if g == 0 else None)
            for g in (2, 3):
                gemm(pe, (f, "out", g), 2, KF, h_rhs)

        pe.wait_ge(v_loaded, 32)
        for ph in phases:
            if ph in FFNS:
                ffn(ph)
            elif ph == "hyb":
                hy.pe(pe)
            else:
                ml.pe(pe)
        pe_stats(pe, "final stats", NN)

    @block.scalar
    def _(act):
        ahead = [0]

        def splits(k):
            for _ in range(k):
                split_high(act, ahead[0])
                ahead[0] += 1

        def norm_pair(nn, pair):
            q = 4 * nn + pair
            squares(nn, pair)
            highs(nn, pair)

        def squares(nn, pair):
            q = 4 * nn + pair
            if q:
                act.wait_ge(squares_added, q)
            if nn and pair == 0:
                act.wait_ge(rstd_done, nn)
            nc.scalar.activation(SQT[:], XT[:, 2 * pair:2 * pair + 2, :], ACT.Square).then_inc(squares_done, 1)

        def highs(nn, pair):
            for m in range(2):
                t = 2 * pair + m
                nc.scalar.activation(XH[:, t, :], XT[:, t, :], ACT.Copy,
                                     scale=PV[:, norm_col[nn] + t:norm_col[nn] + t + 1]).then_inc(xh_done, 1)

        def stats(nn):
            act.wait_ge(rcp_done, nn + 1)
            nc.scalar.activation(RSTD[:], RCP[:], ACT.Sqrt).then_inc(rstd_done, 1)

        def silu(f, g, i=None):
            wait_free(act, (f, "in", g), i)
            nc.scalar.activation(SGT[:, g % 2, :], GU[:, g % 2, 0, :], ACT.Silu).then_inc(silu_done, 1)

        def hidden_high(f, g, i=None):
            n = KF * ffn_index[f] + g + 1
            act.wait_ge(hid_done, n if i is None else 2 * i + n)
            out = HH[:, g, :] if i is None else HH[:, bass.ds(2 * i + g, 1), :]
            src = HT[:, g % 2, :] if i is None else HT[:, g % 2:g % 2 + 1, :]
            nc.scalar.activation(out, src, ACT.Copy).then_inc(hh_done, 1)

        def ffn(f):
            nn = nn_of[f]
            for g in (0, 1):
                splits(2)
                if g == 0:
                    stats(nn)
                silu(f, g)
                splits(1)
                if g == 0:
                    wait_stored(act, f)
                hidden_high(f, g)
                splits(1)
            base = ahead[0]
            with act.Fori(0, (KF - 2) // 2) as i:
                for g in (2, 3):
                    n = base + 4 * (g - 2)
                    go = lambda m: split_high(act, m, i, 6, 8, 2)
                    go(n)
                    go(n + 1)
                    silu(f, g, i)
                    go(n + 2)
                    hidden_high(f, g, i)
                    go(n + 3)
            ahead[0] += 4 * (KF - 2)
            for g in range(4):
                splits(10)
                wait_free(act, (f, "out", g))
                squares(nn + 1, g)
                splits(1)
                highs(nn + 1, g)
                splits(1)

        act.wait_ge(v_loaded, 32)
        for pair in range(4):
            act.wait_ge(x_loaded, 16)
            norm_pair(0, pair)
        splits(R)
        env = Shared()
        env.splits, env.squares, env.highs, env.stats = splits, squares, highs, stats
        for ph in phases:
            if ph in FFNS:
                ffn(ph)
            elif ph == "hyb":
                hy.act(act, env)
            else:
                ml.act(act, env)
        stats(NN)

    @block.vector
    def _(dve):
        ahead = [0]
        seq = [0]

        def splits(k):
            for _ in range(k):
                split_low(dve, ahead[0])
                ahead[0] += 1

        def link(ins):
            seq[0] += 1
            ins.then_inc(dve_seq, 1)
            dve.wait_ge(dve_seq, seq[0])

        def lows(nn, pair):
            for m in range(2):
                t = 2 * pair + m
                dve.wait_ge(xh_done, KD * nn + t + 1)
                nc.vector.scalar_tensor_tensor(XL[:, t, :], XT[:, t, :],
                                               PV[:, norm_col[nn] + t:norm_col[nn] + t + 1],
                                               XH[:, t, :].bitcast(F32), ALU.mult,
                                               ALU.subtract).then_inc(xl_done, 1)

        def stats(step, nn):
            wait_full(dve, step)
            nc.vector.tensor_scalar(halves(VT[:]), acc(step, 2), 1.0 / D, EPS, ALU.mult,
                                    ALU.add).then_inc(acc_free[plan.set_of[step]], 1)
            wait_free(dve, step)
            nc.vector.reciprocal(RCP[:], VT[:]).then_inc(rcp_done, 1)
            dve.wait_ge(rstd_done, nn + 1)

        def rstd4():
            return halves(RSTD[:]).unsqueeze(1).broadcast_to([P, 2, 2, TH])

        def gate_up(f, g, i=None):
            step = (f, "in", g)
            wait_full(dve, step, i)
            out = GU[:, g % 2].rearrange("p m (b t) -> p (m b) t", b=2)
            for m in range(2):
                ins = nc.vector.tensor_tensor(out[:, 2 * m:2 * m + 2, :], acc(step)[:, 2 * m:2 * m + 2, :],
                                              halves(RSTD[:]), ALU.mult)
            ins.then_inc(acc_free[plan.set_of[step]], 1)

        def product(f, g, i=None):
            n = KF * ffn_index[f] + g + 1
            dve.wait_ge(silu_done, n if i is None else 2 * i + n)
            nc.vector.tensor_tensor(HT[:, g % 2, :], SGT[:, g % 2, :], GU[:, g % 2, 1, :],
                                    ALU.mult).then_inc(hid_done, 1)

        def hidden_low(f, g, i=None):
            n = KF * ffn_index[f] + g + 1
            dve.wait_ge(hh_done, n if i is None else 2 * i + n)
            if i is None:
                out, hi, src = HL[:, g, :], HH[:, g, :], HT[:, g % 2, :]
            else:
                tile = bass.ds(2 * i + g, 1)
                out, hi, src = HL[:, tile, :], HH[:, tile, :], HT[:, g % 2:g % 2 + 1, :]
            nc.vector.tensor_tensor(out, src, hi.bitcast(F32), ALU.subtract).then_inc(hl_done, 1)

        def residual(step, pair, scale):
            wait_full(dve, step)
            x = XT[:, 2 * pair:2 * pair + 2, :].rearrange("p m (b t) -> p (m b) t", b=2)
            nc.vector.scalar_tensor_tensor(x, acc(step), scale, x, ALU.mult,
                                           ALU.add).then_inc(acc_free[plan.set_of[step]], 1)

        def ffn(f):
            nn = nn_of[f]
            for g in (0, 1):
                splits(2)
                if g == 0:
                    stats((f, "stats"), nn)
                gate_up(f, g)
                splits(1)
                product(f, g)
                splits(1)
                if g == 0:
                    wait_stored(dve, f)
                hidden_low(f, g)
            base = ahead[0]
            with dve.Fori(0, (KF - 2) // 2) as i:
                for g in (2, 3):
                    n = base + 4 * (g - 2)
                    split_low(dve, n, i, 8)
                    split_low(dve, n + 1, i, 8)
                    gate_up(f, g, i)
                    split_low(dve, n + 2, i, 8)
                    product(f, g, i)
                    split_low(dve, n + 3, i, 8)
                    hidden_low(f, g, i)
            ahead[0] += 4 * (KF - 2)
            for g in range(4):
                splits(10)
                residual((f, "out", g), g, 0.5)
                splits(1)
                splits(1)
                lows(nn + 1, g)

        dve.wait_ge(v_loaded, 32)
        for pair in range(4):
            dve.wait_ge(x_loaded, 16)
            lows(0, pair)
        splits(R)
        env = Shared()
        env.splits, env.lows, env.stats, env.residual, env.link, env.seq = splits, lows, stats, residual, link, seq
        for ph in phases:
            if ph in FFNS:
                ffn(ph)
            elif ph == "hyb":
                hy.dve(dve, env)
            else:
                ml.dve(dve, env)
        stats("final stats", NN)
        for t in range(KD):
            nc.vector.scalar_tensor_tensor(XT[:, t, :], XT[:, t, :], PV[:, V_FINAL + t:V_FINAL + t + 1],
                                           RSTD[:], ALU.mult, ALU.mult).then_inc(y_done, 1)

    @block.gpsimd
    def _(pool):
        pool.dma_start(PV[:], io["vectors"]).then_inc(v_loaded, 16)
        pool.dma_start(CON[:], io["constants"]).then_inc(v_loaded, 16)
        pool.dma_start(XT[:], io["x"]).then_inc(x_loaded, 16)

        def norm_sums(nn):
            for pair in range(4):
                q = 4 * nn + pair
                if pair == 0:
                    pool.wait_ge(squares_done, q + 1)
                    nc.gpsimd.tensor_copy(SQS[:], SQT[:]).then_inc(squares_added, 1)
                else:
                    pool.wait_ge(squares_done, q + 1)
                    pool.wait_ge(squares_added, q)
                    nc.gpsimd.tensor_tensor(SQS[:], SQS[:], SQT[:], ALU.add).then_inc(squares_added, 1)

        norm_sums(0)
        stores = [0]
        env = Shared()
        env.norm_sums, env.stores = norm_sums, stores
        for ph in phases:
            if ph in FFNS:
                norm_sums(nn_of[ph] + 1)
            elif ph == "hyb":
                hy.pool(pool, env)
            else:
                ml.pool(pool, env)
        for t in range(KD):
            pool.wait_ge(y_done, t + 1)
            pool.dma_start(io["y"][:, t, :], XT[:, t, :]).then_inc(out_stored, 16)
            stores[0] += 1
        pool.wait_ge(out_stored, 16 * stores[0])

    stack.close()


def ffn_chunks(w_in, w_out):
    a = w_in.reshape(4, 2, P, 2, KF, P).transpose(4, 0, 2, 1, 3, 5).reshape(-1, P, CW)
    b = w_out.reshape(11, 2, P, 4, 2, P).transpose(3, 0, 2, 1, 4, 5).reshape(4, 11, P, CW)
    b = np.concatenate([b, np.zeros((4, 1, P, CW), b.dtype)], 1).reshape(-1, P, CW)
    return [a, b]


def pairs(w):
    k, n = w.shape
    return w.reshape(k // 256, 2, P, n // 256, 2, P).transpose(3, 0, 2, 1, 4, 5).reshape(-1, P, CW)


def single(w):
    k = w.shape[0]
    return w.reshape(k // 512, 4, P, P).transpose(0, 2, 1, 3).reshape(-1, P, CW)


def columns(v):
    return v.reshape(-1, P).T


def lay_out(q, phases=PHASES):
    a = {k: np.asarray(v) for k, v in q.items()}
    f = np.float32
    w = []
    for ph in phases:
        if ph in FFNS:
            l, which = int(ph[1]), {"a": 1, "b": 2}[ph[0]]
            w += ffn_chunks(a[f"ffn{which}_w_in"][l], a[f"ffn{which}_w_out"][l])
        elif ph == "hyb":
            wi = a["hyb_w_in"][0]
            w += [pairs(wi[:, :5376]),
                  single(np.concatenate([wi[:, 5376:], np.zeros((D, P - SH), f)], 1)),
                  pairs(a["hyb_w_out"][0])]
        else:
            wi = a["mla_w_in"][0]
            kr = wi[:, 768:]
            kr = np.concatenate([np.zeros((D, 64), f), kr, kr[:, 16:], kr[:, :16]], 1)
            uq = a["mla_w_uq"][0].reshape(QL, MH, NOPE + ROPE)
            uq = np.concatenate([uq, uq[:, :, 80:], uq[:, :, 64:80]], 2).reshape(QL, MH * P)
            uv = a["mla_w_uv"][0].reshape(2, P, 2, CW).transpose(2, 0, 1, 3).reshape(-1, P, CW)
            w += [pairs(wi[:, :768]), single(kr), pairs(uq), pairs(a["mla_w_uk"][0].reshape(KVL, D)), uv,
                  pairs(a["mla_w_o"][0])]
    n = sum(len(x) for x in w)
    w.append(np.zeros(((-n) % R + R, P, CW), f))
    x = np.concatenate([a["x_prompt"][0], a["x_sample"][:, 0]], 0)
    rows = lambda v: np.broadcast_to(v, (P, SH))
    jj = np.arange(P)
    gamma = np.log1p(-np.exp2(-5.0 - np.arange(RH)))
    kend = np.stack([np.exp(gamma[h] * (NP_ - 1 - P * jt - jj)) for h in range(RH) for jt in range(NTT)], 1)
    vec = [a["norm_ffn1"][0], a["norm_mix"][0], a["norm_ffn2"][0], a["norm_ffn1"][1], a["norm_mix"][1],
           a["norm_ffn2"][1], a["final_norm_w"], a["hyb_conv_w"][0].reshape(-1), a["hyb_conv_b"][0],
           np.repeat(a["hyb_d_skip"][0], SHD), a["hyb_norm_w"][0], a["mla_q_norm_w"][0], a["mla_kv_norm_w"][0]]
    vectors = np.concatenate([columns(v) for v in vec] + [rows(a["hyb_dt_bias"][0]), rows(a["hyb_a_log"][0]),
                                                          kend.astype(f)], 1)
    i = np.arange(P)
    constants = np.stack([np.eye(P), np.ones((P, P)), i[:, None] <= i[None], i[:, None] > i[None],
                          np.where(i[None] <= i[:, None], 0.0, NEG)], 1).astype(f)
    tile = lambda m: np.ascontiguousarray(m.reshape(-1, P, m.shape[-1]).transpose(1, 0, 2))
    out = {"weights": np.concatenate(w, 0), "x": tile(x.T), "vectors": vectors, "constants": constants}
    if "hyb" in phases:
        out.update(lay_out_hyb(a, tile, gamma))
    if "mla" in phases:
        out.update(lay_out_mla(a, tile))
    return {k: np.ascontiguousarray(v) for k, v in out.items()}


def outputs(phases=PHASES):
    out = {"y": (P, KD, T)}
    if "hyb" in phases:
        out.update(OUT_HYB)
    if "mla" in phases:
        out.update(OUT_MLA)
    return out




def hyb_parts(e):
    nc, io, plan, at, sem, PS = e.nc, e.io, e.plan, e.at, e.sem, e.PS
    REGION, GU_OFF = e.REGION, e.GU_OFF
    IDENT, ONES, UPTO, AFTER, PV, RSTD = e.IDENT, e.ONES, e.UPTO, e.AFTER, e.PV, e.RSTD
    acc, bank0, halves = e.acc, e.bank0, e.halves
    wait_full, wait_free, acquire = e.wait_full, e.wait_free, e.acquire
    full = lambda step: e.acc_full[plan.set_of[step]]
    free = lambda step: e.acc_free[plan.set_of[step]]
    nn = e.nn_of["hyb"]
    before = e.phases[nn - 1] if nn else None

    M1H = at("ret_out_high", [P, 8, T], REGION, F32R)
    M1L = at("ret_out_low", [P, 8, T], REGION + 16640, F32R)
    VTF = at("v_features", [P, 8, T], REGION)
    OB = at("ret_out", [P, 8, T], REGION + 16640)
    QT = at("q_features", [P, 4, T], REGION + 33280)
    KT = at("k_features", [P, 4, T], REGION + 41600)
    VTOK = at("v_tokens", [P, NTT, 1024], REGION + 49920)
    KM = at("k_samples_masked", [NS, NS, 512], REGION + 49920)
    GS = at("silu_g", [P, 8, T], REGION + 66304)
    KTOK = at("k_tokens", [P, RH * NTT, P], REGION + 82944)
    SEG = at("decays", [P, RH, NP_], REGION + 91136)
    S0 = [at("sample_state0", [P, 2, RH, RDV], REGION + 91136), at("sample_state1", [P, 2, RH, RDV], REGION + 82944)]
    CT = at("rope_cos", [P, T], REGION + 99328)
    SN = at("rope_sin", [P, T], REGION + 101408)
    RST = at("ret_state", [P, RH, RDV], REGION + 99328)
    ST = [at("ret_scores0", [P, 1280], GU_OFF), at("ret_scores1", [P, 1280], GU_OFF + 8320)]
    VS = at("v_samples", [NS, 1024], GU_OFF)
    SQB = at("ret_squares", [P, 8, T], GU_OFF)
    ROT = at("rotated", [P, 2, T], GU_OFF + 12480)
    ZS = at("silu_z", [P, 8, T], REGION + 33280)
    XS = at("ssm_x", [P, 8, T], REGION + 49920)
    BC = at("ssm_bc", [P, 2, T], REGION + 66560)
    XTOK = at("ssm_x_tokens", [P, NTT, 1024], REGION + 70720)
    SSS = at("ssm_sample_state", [P, NS, 512], REGION + 70720)
    BTOK = at("ssm_b_tokens", [P, NTT, P], REGION + 87104)
    EM = at("ssm_weights", [P, SH, P], REGION + 89152)
    CS = at("ssm_c_decayed", [P, 8, P], REGION + 97344)
    DTR = at("dt_features", [SH, T], REGION + 97344)
    XDS = at("ssm_x_samples", [NS, 1024], REGION + 97344)
    SST = at("ssm_state", [P, 512], REGION + 101440)
    CBE = at("ssm_c_decay", [P, 1024], GU_OFF)
    BM = at("ssm_b_masked", [NS, NS, P], GU_OFF)
    XEND = at("ssm_x_end", [P, 1024], GU_OFF + 4096)
    LM = at("ssm_masked_log", [P, SH, P], GU_OFF + 8448)
    LAW = at("ssm_log_wide", [P, 8, 2, 64], e.SQS_OFF)
    SM = at("ssm_scores", [P, 2, P], e.VT_OFF)
    DECX = at("ssm_decay_masked", [NS, NS, SH], e.VT_OFF + 1024)
    V2 = at("ssm_variance", [P, 2, T], REGION + 89152)
    RT2 = at("ssm_rstd", [P, 2, T], REGION + 89152 + 4160)
    CR = at("conv_in", [P, 4, 524], GU_OFF)
    CACC = at("conv_sum", [P, 2, T], GU_OFF + 8448)
    SCI = at("conv_state", [P, XBC, 3, NS], GU_OFF + 12608)
    CSO = at("conv_sample_out", [P, XBC, 3, NS], GU_OFF + 13568)
    CPO = at("conv_prompt_out", [P, XBC, 3], GU_OFF + 14528)
    small = [at(f"dt_work{i}", [P, 5, SH], e.SQT_OFF + 320 * i) for i in range(9)]
    DX, DP, DE, DS_, DS2, DH, DT, LA, DA = small
    DEX = at("ssm_decays", [P, 2, 64], e.SQT_OFF + 2880)
    DECB = at("ssm_sample_decay", [P, 64], e.SQT_OFF + 3392)
    soff = [0, 512, 896, 1152]

    loaded = sem("hyb_tables_loaded")
    conv_loaded = sem("conv_state_loaded")
    rot_done, gs_done = sem("rotated_done"), sem("silu_gz_done")
    s0_loaded = [sem("ret_state_loaded0"), sem("ret_state_loaded1")]
    s0_stored = [sem("ret_state_stored0"), sem("ret_state_stored1")]
    sss_loaded = sem("ssm_state_loaded")
    sq_done, v2_done, rt_done = sem("ret_squares_done"), sem("ret_rcp_done"), sem("ret_rstd_done")
    o_done, m1h_done, m1l_done = sem("ret_gated_done"), sem("ret_high_done"), sem("ret_low_done")
    conv_done, convs_done = sem("conv_sum_done"), sem("conv_silu_done")
    dt_abs, dt_exp, dt_done = sem("dt_abs_done"), sem("dt_exp_done"), sem("dt_done")
    law_done, cbe_done, l_done, m_done, xend_done = sem("log_wide_done"), sem("c_decay_done"), sem("masked_log_done"), sem("weights_done"), sem("x_end_done")
    yg_done, ysq_done, yv_done, yr_done = sem("y_gated_done"), sem("y_squares_done"), sem("y_rcp_done"), sem("y_rstd_done")
    yn_done, yh_done, yl_done = sem("y_normed_done"), sem("y_high_done"), sem("y_low_done")
    out_ready = sem("hyb_out_ready")


    def pe(pe):
        last = None

        def transposes(step, items, waits):
            acquire(pe, step)
            for w in waits:
                w()
            for out, src in items:
                k = src.shape[0]
                mm = nc.tensor.transpose(out, src, IDENT[0:k, 0:k])
            mm.then_inc(full(step), 1)

        def hin(g, **kw):
            e.gemm(pe, ("hin", g), 2 if g < 21 else 1, KD, e.x_rhs, **kw)

        hin(0, before_k=e.first_wait(pe, nn))
        e.pe_stats(pe, "hyb stats", nn)
        for g in range(1, 12):
            hin(g)
        b = bank0("ret kT")
        transposes("ret kT", [(PS[:, b + h, jt * P:(jt + 1) * P], KT[:, h, jt * P:(jt + 1) * P])
                              for h in range(RH) for jt in range(NTT)],
                   [lambda: pe.wait_ge(rot_done, 8)])
        for v in range(2):
            b = bank0(f"ret vT{v}")
            transposes(f"ret vT{v}", [(PS[:, b + t, jt * P:(jt + 1) * P], VTF[:, 4 * v + t, jt * P:(jt + 1) * P])
                                      for t in range(4) for jt in range(NTT)],
                       [lambda: wait_free(pe, ("hin", 7))])
        for h in range(RH):
            step = ("ret S", h)
            acquire(pe, step)
            b = bank0(step)
            for jt in range(NTT):
                mm = nc.tensor.matmul(PS[:, b + jt, 0:NP_ - jt * P], KT[:, h, jt * P:(jt + 1) * P],
                                      QT[:, h, jt * P:NP_], start=True, stop=True)
            mm.then_inc(full(step), 1)
            step2 = ("ret O", h)
            acquire(pe, step2)
            wait_free(pe, step)
            if h == 0:
                wait_free(pe, "ret vT1")
                wait_free(pe, "ret kT")
            b = bank0(step2)
            for m in range(2):
                for jt in range(NTT):
                    n = NP_ - jt * P
                    nc.tensor.matmul(PS[:, b + m, jt * P:NP_],
                                     VTOK[:, jt, h * RDV + m * P:h * RDV + (m + 1) * P],
                                     ST[h % 2][:, soff[jt]:soff[jt] + n], start=jt == 0, stop=jt == NTT - 1)
            for jt in range(NTT):
                mm = nc.tensor.matmul(PS[:, b + 2, 0:RDV], KTOK[:, h * NTT + jt, :],
                                      VTOK[:, jt, h * RDV:(h + 1) * RDV], start=jt == 0, stop=jt == NTT - 1)
            mm.then_inc(full(step2), 1)
        b = bank0("ret sT")
        transposes("ret sT", [(PS[0:NS, b, h * P:(h + 1) * P], KT[:, h, NP_:T]) for h in range(RH)] +
                   [(PS[0:NS, b + 1 + t // 4, (t % 4) * P:(t % 4 + 1) * P], VTF[:, t, NP_:T]) for t in range(8)], [])
        for p in range(NS // 2):
            step = ("ret outer", p)
            acquire(pe, step)
            if p == 0:
                wait_free(pe, "ret sT")
            b = bank0(step)
            for j in range(2):
                for h in range(RH):
                    mm = nc.tensor.matmul(PS[:, b + 2 * j + h // 2, (h % 2) * RDV:(h % 2 + 1) * RDV],
                                          KM[:, 2 * p + j, h * P:(h + 1) * P], VS[:, h * RDV:(h + 1) * RDV],
                                          start=True, stop=True)
            mm.then_inc(full(step), 1)
            step2 = ("ret y", p)
            acquire(pe, step2)
            wait_free(pe, step)
            b = bank0(step2)
            for j in range(2):
                for t in range(8):
                    h = t // 2
                    mm = nc.tensor.matmul(PS[:, b, j * 8 + t:j * 8 + t + 1],
                                          S0[p % 2][:, j, h, (t % 2) * P:(t % 2 + 1) * P],
                                          QT[:, h, NP_ + 2 * p + j:NP_ + 2 * p + j + 1], start=True, stop=True)
            mm.then_inc(full(step2), 1)
        for n in range(2):
            step = ("ret norm", n)
            acquire(pe, step)
            pe.wait_ge(sq_done, n + 1)
            b = bank0(step)
            for hh in range(2):
                for half in range(2):
                    for m in range(2):
                        mm = nc.tensor.matmul(PS[:, b + 2 * hh + half, 0:TH], ONES,
                                              SQB[:, 4 * n + 2 * hh + m, half * TH:(half + 1) * TH],
                                              start=m == 0, stop=m == 1)
            mm.then_inc(full(step), 1)
        for g in range(12, 22):
            hin(g)
        b = bank0("ssm dtT")
        transposes("ssm dtT", [(PS[:, b, c * SH:(c + 1) * SH], DTR[:, c * P:(c + 1) * P]) for c in range(NTT)] +
                   [(PS[0:NS, b, 64:80], DTR[:, NP_:T])], [lambda: wait_free(pe, ("hin", 21))])
        for v in range(2):
            b = bank0(f"ssm xT{v}")
            transposes(f"ssm xT{v}", [(PS[:, b + t, jt * P:(jt + 1) * P], XS[:, 4 * v + t, jt * P:(jt + 1) * P])
                                      for t in range(4) for jt in range(NTT)],
                       [lambda: pe.wait_ge(convs_done, 4 * v + 4)])
        b = bank0("ssm BT")
        transposes("ssm BT", [(PS[:, b, c * P:(c + 1) * P], BC[:, 0, c * P:(c + 1) * P]) for c in range(NTT)],
                   [lambda: pe.wait_ge(convs_done, XBC)])
        step = "ssm sums"
        acquire(pe, step)
        pe.wait_ge(dt_done, 1)
        b = bank0(step)
        la = LA[:, 0:NTT, :].rearrange("p c h -> p (c h)")
        nc.tensor.matmul(PS[:, b, 0:64], AFTER, la, start=True, stop=True)
        nc.tensor.matmul(PS[:, b, 64:128], ONES, la, start=True, stop=True).then_inc(full(step), 1)
        for c in range(NTT):
            tok = slice(c * P, (c + 1) * P)
            step = ("ssm sc", c)
            acquire(pe, step)
            b = bank0(step)
            for g in range(2):
                rows = slice(64 * g, 64 * g + 64)
                nc.tensor.matmul(PS[:, b + g, 0:P], BC[rows, 0, tok], BC[rows, 1, tok], start=True, stop=True)
            pe.wait_ge(law_done, c + 1)
            for h8 in range(8):
                mm = nc.tensor.matmul(PS[:, b + 2 + h8 // 4, (h8 % 4) * P:(h8 % 4 + 1) * P], LAW[:, h8].rearrange("p g s -> p (g s)"),
                                      UPTO, start=True, stop=True)
            mm.then_inc(full(step), 1)
            step = ("ssm D", c)
            acquire(pe, step)
            pe.wait_ge(l_done, c + 1)
            b = bank0(step)
            for h in range(SH):
                mm = nc.tensor.matmul(PS[:, b + h // 4, (h % 4) * P:(h % 4 + 1) * P], LM[:, h, :], UPTO,
                                      start=True, stop=True)
            mm.then_inc(full(step), 1)
            step = ("ssm y", c)
            acquire(pe, step)
            pe.wait_ge(xend_done, c + 1)
            pe.wait_ge(m_done, 2 * (c + 1))
            wait_free(pe, ("ssm sc", c))
            b = bank0(step)
            for g in range(2):
                mm = nc.tensor.matmul(PS[64 * g:64 * g + 64, b + 2, :], BTOK[:, c, 64 * g:64 * g + 64],
                                      XEND[:, g * 512:(g + 1) * 512], start=True, stop=True)
            for h in range(SH):
                g, t = h // 8, h // 2
                out = PS[64 * (h % 2):64 * (h % 2) + 64, b + g, (t % 4) * P:(t % 4 + 1) * P]
                mm = nc.tensor.matmul(out, XTOK[:, c, h * SHD:(h + 1) * SHD], EM[:, h, :], start=True, stop=c == 0)
                if c:
                    rows = slice(64 * g, 64 * g + 64)
                    mm = nc.tensor.matmul(out, SST[rows, (h % 8) * SHD:(h % 8 + 1) * SHD], CS[rows, h % 8, :],
                                          start=False, stop=True)
            mm.then_inc(full(step), 1)
        b = bank0("ssm sT")
        transposes("ssm sT", [(PS[0:NS, b + t // 4, (t % 4) * P:(t % 4 + 1) * P], XS[:, t, NP_:T]) for t in range(8)] +
                   [(PS[0:NS, b + 2, 0:P], BC[:, 0, NP_:T])], [])
        step = "ssm dec"
        acquire(pe, step)
        wait_free(pe, "ssm sT")
        b = bank0(step)
        for g in range(2):
            mm = nc.tensor.matmul(PS[64 * g:64 * g + 64, b, 0:64].rearrange("p (b h) -> p b h", b=8),
                                  ONES[0:NS, 0:64], DECX[:, :, 8 * g:8 * g + 8], start=True, stop=True)
        mm.then_inc(full(step), 1)
        for k in range(2):
            step = ("ssm outer", k)
            acquire(pe, step)
            b = bank0(step)
            for j in range(4):
                for g in range(2):
                    mm = nc.tensor.matmul(PS[64 * g:64 * g + 64, b + j, :], BM[:, 4 * k + j, 64 * g:64 * g + 64],
                                          XDS[:, g * 512:(g + 1) * 512], start=True, stop=True)
            mm.then_inc(full(step), 1)
        step = "ssm ys"
        acquire(pe, step)
        wait_free(pe, ("ssm outer", 1))
        b = bank0(step)
        for q in range(8):
            g = q // 4
            rows = slice(64 * g, 64 * g + 64)
            for s in range(NS):
                mm = nc.tensor.matmul(PS[:, b + g, (q % 4) * 8 + s:(q % 4) * 8 + s + 1],
                                      SSS[rows, s, (q % 4) * P:(q % 4 + 1) * P], BC[rows, 1, NP_ + s:NP_ + s + 1],
                                      start=True, stop=True)
        mm.then_inc(full(step), 1)
        step = "ssm norm"
        acquire(pe, step)
        pe.wait_ge(ysq_done, 1)
        b = bank0(step)
        for g in range(2):
            for half in range(2):
                for t in range(4):
                    mm = nc.tensor.matmul(PS[:, b + 2 * g + half, 0:TH], ONES,
                                          SQB[:, 4 * g + t, half * TH:(half + 1) * TH], start=t == 0, stop=t == 3)
        mm.then_inc(full(step), 1)

        def mixed(k):
            return (M1H[:, k, :], M1L[:, k, :]) if k < 8 else (e.XH[:, k - 8, :], e.XL[:, k - 8, :])

        def ready(k):
            if k == 0:
                pe.wait_ge(m1l_done, 2)
            if k >= 8:
                pe.wait_ge(yl_done, k - 7)

        for g in range(4):
            e.gemm(pe, ("hout", g), 2, 16, mixed, before_k=ready if g == 0 else None)

    def act(act, a):
        def silu_pair(step, dst, src):
            wait_free(act, step)
            nc.scalar.activation(dst, src, ACT.Silu).then_inc(gs_done, 1)

        for g in range(12):
            a.splits(2)
            if g == 0:
                a.stats(nn)
            if g >= 8:
                silu_pair(("hin", g), GS[:, 2 * (g - 8):2 * (g - 8) + 2, :], e.GU[:, g % 2])
            a.splits(2)
        for v in range(2):
            step = f"ret vT{v}"
            wait_full(act, step)
            b = bank0(step)
            for t in range(4):
                ins = nc.scalar.activation(VTOK[:, :, (4 * v + t) * P:(4 * v + t + 1) * P],
                                           PS[:, b + t, :].rearrange("p (j e) -> p j e", j=NTT), ACT.Copy)
            ins.then_inc(free(step), 1)
        for h in range(RH):
            step = ("ret O", h)
            wait_full(act, step)
            b = bank0(step)
            nc.scalar.activation(OB[:, 2 * h:2 * h + 2, 0:NP_], PS[:, b:b + 2, :], ACT.Copy)
            nc.scalar.activation(RST[:, h, :], PS[:, b + 2, 0:RDV], ACT.Copy).then_inc(free(step), 1)
        for n in range(2):
            wait_free(act, ("ret y", 3))
            nc.scalar.activation(SQB[:, 4 * n:4 * n + 4, :], OB[:, 4 * n:4 * n + 4, :], ACT.Square).then_inc(sq_done, 1)
        for n in range(2):
            act.wait_ge(v2_done, n + 1)
            nc.scalar.activation(KT[:, 2 * n:2 * n + 2, :], QT[:, 2 * n:2 * n + 2, :], ACT.Sqrt).then_inc(rt_done, 1)
        for n in range(2):
            act.wait_ge(o_done, n + 1)
            nc.scalar.activation(M1H[:, 4 * n:4 * n + 4, :], OB[:, 4 * n:4 * n + 4, :], ACT.Copy).then_inc(m1h_done, 1)
        for g in range(12, 21):
            a.splits(2)
            if g < 16:
                silu_pair(("hin", g), ZS[:, 2 * (g - 12):2 * (g - 12) + 2, :], e.GU[:, g % 2])
                a.splits(2)
            else:
                for m in range(2):
                    c = 2 * (g - 16) + m
                    act.wait_ge(conv_done, c + 1)
                    dst = XS[:, c, :] if c < 8 else BC[:, c - 8, :]
                    nc.scalar.activation(dst, CACC[:, m, :], ACT.Silu).then_inc(convs_done, 1)
                    a.splits(1)
        a.splits(2)
        nc.scalar.activation(DA[:, 0, :], PV[:, V_ALOG:V_ALOG + SH], ACT.Exp)
        act.wait_ge(dt_abs, 1)
        nc.scalar.activation(DE[:], DE[:], ACT.Exp, scale=-1.0).then_inc(dt_exp, 1)
        step = "ssm sums"
        wait_full(act, step)
        nc.scalar.activation(DX[:, 0, :], LA[:, 4, :], ACT.Exp)
        nc.scalar.activation(DEX[:].rearrange("p a b -> p (a b)"), PS[:, bank0(step), 0:128],
                             ACT.Exp).then_inc(free(step), 1)
        for c in range(NTT):
            step = ("ssm sc", c)
            wait_full(act, step)
            b = bank0(step)
            nc.scalar.activation(CBE[:], PS[:, b + 2:b + 4, :].rearrange("p a b -> p (a b)"),
                                 ACT.Exp).then_inc(cbe_done, 1)
            step = ("ssm D", c)
            wait_full(act, step)
            b = bank0(step)
            nc.scalar.activation(EM[:].rearrange("p h i -> p (h i)"), PS[:, b:b + 4, :].rearrange("p a b -> p (a b)"),
                                 ACT.Exp).then_inc(free(step), 1)
        act.wait_ge(yg_done, 1)
        nc.scalar.activation(SQB[:], XS[:], ACT.Square).then_inc(ysq_done, 1)
        act.wait_ge(yv_done, 1)
        nc.scalar.activation(RT2[:], V2[:], ACT.Sqrt).then_inc(yr_done, 1)
        for t in range(8):
            act.wait_ge(yn_done, t // 4 + 1)
            nc.scalar.activation(e.XH[:, t, :], XS[:, t, :], ACT.Copy,
                                 scale=PV[:, V_HNORM + t:V_HNORM + t + 1]).then_inc(yh_done, 1)
        for g in range(4):
            a.splits(6)
            wait_free(act, ("hout", g))
            a.squares(nn + 1, g)
            a.splits(2)
        wait_full(act, ("hout", 3))
        for g in range(4):
            a.highs(nn + 1, g)

    def dve(dve, a):
        link = a.link

        def rstd_pair(step, out, signal=True):
            wait_full(dve, step)
            for m in range(2):
                ins = nc.vector.tensor_tensor(halves(out[:, m, :]), acc(step)[:, 2 * m:2 * m + 2, :], halves(RSTD[:]), ALU.mult)
            ins.then_inc(free(step), 1)

        def rotate(g):
            step = ("hin", g)
            wait_full(dve, step)
            for m in range(2):
                t = 2 * g + m
                dst = (QT if t < 4 else KT)[:, t % 4, :]
                scale = 1.0 if t < 4 else RDK ** -0.5
                src = acc(step)[:, 2 * m:2 * m + 2, :]
                stt = lambda out, i0, i1: nc.vector.scalar_tensor_tensor(halves(out), i0, scale, halves(i1),
                                                                         ALU.mult, ALU.mult)
                if t >= 2:
                    dve.wait_ge(rot_done, t - 1)
                stt(dst, src, CT[:])
                stt(ROT[0:64, m, :], src[64:128], SN[64:128, :])
                ins = stt(ROT[64:128, m, :], src[0:64], SN[0:64, :])
                if m == 0:
                    link(ins)
                else:
                    ins.then_inc(free(step), 1)
                    wait_free(dve, step)
                nc.vector.tensor_tensor(dst, dst, ROT[:, m, :], ALU.add).then_inc(rot_done, 1)

        for g in range(12):
            a.splits(2)
            if g == 0:
                a.stats("hyb stats", nn)
                dve.wait_ge(loaded, 16 * 3)
                nc.vector.tensor_tensor(CT[:], CT[:], RSTD[:], ALU.mult)
                link(nc.vector.tensor_tensor(SN[:], SN[:], RSTD[:], ALU.mult))
            if g < 4:
                rotate(g)
            elif g < 8:
                rstd_pair(("hin", g), VTF[:, 2 * (g - 4):2 * (g - 4) + 2, :])
            else:
                if g >= 10:
                    dve.wait_ge(gs_done, g - 9)
                rstd_pair(("hin", g), e.GU[:, g % 2])
            a.splits(2)
        step = "ret kT"
        wait_full(dve, step)
        b = bank0(step)
        nc.vector.tensor_tensor(KTOK[:], PS[:, b:b + 4, :].rearrange("p a (j d) -> p (a j) d", d=P),
                                PV[:, V_KEND:V_KEND + 16].unsqueeze(2).broadcast_to([P, 16, P]),
                                ALU.mult).then_inc(free(step), 1)
        dve.wait_ge(gs_done, 4)
        for h in range(RH):
            step = ("ret S", h)
            wait_full(dve, step)
            b = bank0(step)
            for jt in range(NTT):
                n = NP_ - jt * P
                ins = nc.vector.tensor_tensor(ST[h % 2][:, soff[jt]:soff[jt] + n], PS[:, b + jt, 0:n],
                                              SEG[:, h, 0:n], ALU.mult)
            ins.then_inc(free(step), 1)
        step = "ret sT"
        wait_full(dve, step)
        b = bank0(step)
        nc.vector.tensor_copy(VS[:], PS[0:NS, b + 1:b + 3, :].rearrange("p a b -> p (a b)"))
        nc.vector.tensor_tensor(KM[:], PS[0:NS, b, :].unsqueeze(1).broadcast_to([NS, NS, 512]),
                                IDENT[0:NS, 0:NS].unsqueeze(2).broadcast_to([NS, NS, 512]),
                                ALU.mult).then_inc(free(step), 1)
        for p in range(NS // 2):
            step = ("ret outer", p)
            wait_full(dve, step)
            dve.wait_ge(s0_loaded[p % 2], 16 * (p // 2 + 1))
            b = bank0(step)
            for h in range(RH):
                s = S0[p % 2][:, :, h, :]
                ps = PS[:, b + h // 2:b + h // 2 + 3:2, (h % 2) * RDV:(h % 2 + 1) * RDV]
                ins = nc.vector.scalar_tensor_tensor(s, s, float(1.0 - 2.0 ** (-5 - h)), ps, ALU.mult, ALU.add)
            ins.then_inc(free(step), 1)
            step = ("ret y", p)
            wait_full(dve, step)
            b = bank0(step)
            nc.vector.tensor_copy(OB[:, :, NP_ + 2 * p:NP_ + 2 * p + 2],
                                  PS[:, b, 0:16].rearrange("p (j t) -> p t j", j=2)).then_inc(free(step), 1)
        for n in range(2):
            step = ("ret norm", n)
            wait_full(dve, step)
            v = QT[:, 2 * n:2 * n + 2, :]
            nc.vector.tensor_scalar(v.rearrange("p m (b t) -> p (m b) t", b=2), acc(step), 1.0 / RDV, EPS,
                                    ALU.mult, ALU.add).then_inc(free(step), 1)
            wait_free(dve, step)
            nc.vector.reciprocal(v, v).then_inc(v2_done, 1)
        for n in range(2):
            dve.wait_ge(rt_done, n + 1)
            for hh in range(2):
                h = 2 * n + hh
                o = OB[:, 2 * h:2 * h + 2, :]
                ins = nc.vector.tensor_tensor(o, o, KT[:, h, :].unsqueeze(1).broadcast_to([P, 2, T]), ALU.mult)
            link(ins)
            o = OB[:, 4 * n:4 * n + 4, :]
            nc.vector.tensor_tensor(o, o, GS[:, 4 * n:4 * n + 4, :], ALU.mult).then_inc(o_done, 1)
        for n in range(2):
            dve.wait_ge(m1h_done, n + 1)
            nc.vector.tensor_tensor(M1L[:, 4 * n:4 * n + 4, :], OB[:, 4 * n:4 * n + 4, :],
                                    M1H[:, 4 * n:4 * n + 4, :].bitcast(F32), ALU.subtract).then_inc(m1l_done, 1)
        for g in range(12, 16):
            a.splits(2)
            if g >= 14:
                dve.wait_ge(gs_done, g - 9)
            rstd_pair(("hin", g), e.GU[:, g % 2])
            a.splits(2)
        dve.wait_ge(gs_done, 8)
        link(nc.vector.memset(CR[:, :, 0:3], 0.0))
        dve.wait_ge(conv_loaded, 16)
        nc.vector.tensor_copy(CSO[:, :, 0:2, :], SCI[:, :, 1:3, :])
        for g in range(16, 21):
            a.splits(2)
            step = ("hin", g)
            wait_full(dve, step)
            for m in range(2):
                cr = CR[:, 2 * (g % 2) + m, 3:523]
                ins = nc.vector.tensor_tensor(halves(cr), acc(step)[:, 2 * m:2 * m + 2, :], halves(RSTD[:]), ALU.mult)
                if m == 0:
                    link(ins)
            ins.then_inc(free(step), 1)
            wait_free(dve, step)
            for m in range(2):
                c = 2 * (g - 16) + m
                cr = CR[:, 2 * (g % 2) + m, :]
                w = [PV[:, V_CONVW + XBC * k + c:V_CONVW + XBC * k + c + 1] for k in range(CONV_W)]
                bias = PV[:, V_CONVB + c:V_CONVB + c + 1]
                if g > 16:
                    dve.wait_ge(convs_done, c - 1)
                nc.vector.tensor_scalar(CACC[:, m, 0:NP_], cr[:, 0:NP_], w[0], bias, ALU.mult, ALU.add)
                link(nc.vector.tensor_scalar(CACC[:, m, NP_:T], SCI[:, c, 0, :], w[0], bias, ALU.mult, ALU.add))
                for k in range(1, CONV_W):
                    nc.vector.scalar_tensor_tensor(CACC[:, m, 0:NP_], cr[:, k:k + NP_], w[k], CACC[:, m, 0:NP_],
                                                   ALU.mult, ALU.add)
                    xs = SCI[:, c, k, :] if k < 3 else cr[:, 515:523]
                    ins = nc.vector.scalar_tensor_tensor(CACC[:, m, NP_:T], xs, w[k], CACC[:, m, NP_:T],
                                                         ALU.mult, ALU.add)
                    if k < 3:
                        link(ins)
                    else:
                        ins.then_inc(conv_done, 1)
                nc.vector.tensor_copy(CPO[:, c, :], cr[:, 512:515])
                ins = nc.vector.tensor_copy(CSO[:, c, 2, :], cr[:, 515:523])
            if g == 20:
                ins.then_inc(out_ready, 1)
            a.splits(2)
        step = ("hin", 21)
        wait_full(dve, step)
        nc.vector.tensor_tensor(halves(DTR[:]), PS[0:SH, bank0(step):bank0(step) + 2, 0:TH], halves(RSTD[0:SH, :]),
                                ALU.mult).then_inc(free(step), 1)
        a.splits(2)
        step = "ssm dtT"
        link(nc.vector.memset(DX[:], 0.0))
        wait_full(dve, step)
        b = bank0(step)
        bias = PV[:, V_DTB:V_DTB + SH]
        nc.vector.tensor_tensor(DX[:, 0:NTT, :], PS[:, b, 0:64].rearrange("p (c h) -> p c h", c=NTT),
                                bias.unsqueeze(1).broadcast_to([P, NTT, SH]), ALU.add)
        nc.vector.tensor_tensor(DX[0:NS, NTT, :], PS[0:NS, b, 64:80], bias[0:NS], ALU.add).then_inc(free(step), 1)
        wait_free(dve, step)
        nc.vector.scalar_tensor_tensor(DE[:], DX[:], -1.0, DX[:], ALU.mult, ALU.max).then_inc(dt_abs, 1)
        nc.vector.tensor_scalar(DP[:], DX[:], 0.0, None, ALU.max)
        dve.wait_ge(dt_exp, 1)
        link(nc.vector.tensor_scalar(DS_[:], DE[:], 2.0, None, ALU.add))
        link(nc.vector.reciprocal(DS_[:], DS_[:]))
        link(nc.vector.tensor_tensor(DS_[:], DS_[:], DE[:], ALU.mult))
        link(nc.vector.tensor_tensor(DS2[:], DS_[:], DS_[:], ALU.mult))
        link(nc.vector.tensor_scalar(DH[:], DS2[:], 1.0 / 17, None, ALU.mult))
        for k in range(15, 1, -2):
            link(nc.vector.scalar_tensor_tensor(DH[:], DH[:], 1.0 / k, DS2[:], ALU.add, ALU.mult))
        link(nc.vector.scalar_tensor_tensor(DH[:], DH[:], 1.0, DS_[:], ALU.add, ALU.mult))
        link(nc.vector.scalar_tensor_tensor(DT[:], DH[:], 2.0, DP[:], ALU.mult, ALU.add))
        nc.vector.scalar_tensor_tensor(LA[:], DT[:], -1.0, DA[:, 0:1, :].broadcast_to([P, 5, SH]), ALU.mult,
                                       ALU.mult).then_inc(dt_done, 1)
        for v in range(2):
            step = f"ssm xT{v}"
            wait_full(dve, step)
            b = bank0(step)
            for jt in range(NTT):
                out = XTOK[:, jt, v * 512:(v + 1) * 512].rearrange("p (t h d) -> p t h d", t=4, h=2)
                ins = nc.vector.tensor_tensor(out, PS[:, b:b + 4, jt * P:(jt + 1) * P].rearrange("p t (h d) -> p t h d", h=2),
                                              DT[:, jt, 8 * v:8 * v + 8].rearrange("p (t h) -> p t h", t=4)
                                              .unsqueeze(3).broadcast_to([P, 4, 2, SHD]), ALU.mult)
            ins.then_inc(free(step), 1)
        step = "ssm BT"
        wait_full(dve, step)
        nc.vector.tensor_copy(BTOK[:].rearrange("p c n -> p (c n)"), PS[:, bank0(step), :]).then_inc(free(step), 1)
        for c in range(NTT):
            tok = slice(c * P, (c + 1) * P)
            step = ("ssm sc", c)
            wait_full(dve, step)
            b = bank0(step)
            nc.vector.tensor_tensor(SM[:], PS[:, b:b + 2, 0:P], UPTO.unsqueeze(1).broadcast_to([P, 2, P]), ALU.mult)
            dve.wait_ge(cbe_done, c + 1)
            nc.vector.tensor_tensor(CS[:], BC[:, 1, tok].unsqueeze(1).broadcast_to([P, 8, P]),
                                    CBE[:].rearrange("p (h i) -> p h i", h=8), ALU.mult).then_inc(free(step), 1)
            wait_free(dve, ("ssm D", c))
            wait_free(dve, ("ssm sc", c))
            for g in range(2):
                em = EM[:, 8 * g:8 * g + 8, :]
                nc.vector.tensor_tensor(em, em, SM[:, g:g + 1, :].broadcast_to([P, 8, P]), ALU.mult).then_inc(m_done, 1)
            step = ("ssm y", c)
            wait_full(dve, step)
            b = bank0(step)
            for t in range(8):
                nc.vector.scalar_tensor_tensor(XS[:, t, tok], XS[:, t, tok], PV[:, V_DSKIP + t:V_DSKIP + t + 1],
                                               PS[:, b + t // 4, (t % 4) * P:(t % 4 + 1) * P], ALU.mult, ALU.add)
            if c == 0:
                nc.vector.tensor_copy(SST[:], PS[:, b + 2, :]).then_inc(free(step), 1)
            else:
                for g in range(2):
                    rows = slice(64 * g, 64 * g + 64)
                    s = SST[rows, :].rearrange("p (h d) -> p h d", h=8)
                    ins = nc.vector.tensor_tensor(s, s, DEX[rows, 1, c * SH + 8 * g:c * SH + 8 * g + 8]
                                                  .unsqueeze(2).broadcast_to([64, 8, SHD]), ALU.mult)
                    link(ins)
                nc.vector.tensor_tensor(SST[:], SST[:], PS[:, b + 2, :], ALU.add).then_inc(free(step), 1)
            wait_free(dve, step)
        step = "ssm sT"
        wait_full(dve, step)
        b = bank0(step)
        nc.vector.tensor_tensor(DECX[:], DX[0:NS, 0:1, :].broadcast_to([NS, NS, SH]),
                                IDENT[0:NS, 0:NS].unsqueeze(2).broadcast_to([NS, NS, SH]), ALU.mult)
        nc.vector.tensor_tensor(XDS[:].rearrange("p (h d) -> p h d", d=SHD),
                                PS[0:NS, b:b + 2, :].rearrange("p a (h d) -> p (a h) d", d=SHD),
                                DT[0:NS, NTT, :].unsqueeze(2).broadcast_to([NS, SH, SHD]), ALU.mult)
        nc.vector.tensor_tensor(BM[:], PS[0:NS, b + 2, 0:P].unsqueeze(1).broadcast_to([NS, NS, P]),
                                IDENT[0:NS, 0:NS].unsqueeze(2).broadcast_to([NS, NS, P]),
                                ALU.mult).then_inc(free(step), 1)
        step = "ssm dec"
        wait_full(dve, step)
        nc.vector.tensor_copy(DECB[:], PS[:, bank0(step), 0:64]).then_inc(free(step), 1)
        wait_free(dve, step)
        dve.wait_ge(sss_loaded, 16)
        for k in range(2):
            s = SSS[:, 4 * k:4 * k + 4, :].rearrange("p b (h d) -> p (b h) d", d=SHD)
            link(nc.vector.tensor_tensor(s, s, DECB[:, 32 * k:32 * k + 32].unsqueeze(2).broadcast_to([P, 32, SHD]), ALU.mult))
        for k in range(2):
            step = ("ssm outer", k)
            wait_full(dve, step)
            s = SSS[:, 4 * k:4 * k + 4, :]
            nc.vector.tensor_tensor(s, s, PS[:, bank0(step):bank0(step) + 4, :], ALU.add).then_inc(free(step), 1)
        step = "ssm ys"
        wait_full(dve, step)
        b = bank0(step)
        for t in range(8):
            ins = nc.vector.scalar_tensor_tensor(XS[:, t, NP_:T], XS[:, t, NP_:T], PV[:, V_DSKIP + t:V_DSKIP + t + 1],
                                                 PS[:, b + t // 4, (t % 4) * 8:(t % 4) * 8 + 8], ALU.mult, ALU.add)
        ins.then_inc(free(step), 1)
        wait_free(dve, step)
        nc.vector.tensor_tensor(XS[:], XS[:], ZS[:], ALU.mult).then_inc(yg_done, 1)
        step = "ssm norm"
        wait_full(dve, step)
        nc.vector.tensor_scalar(V2[:].rearrange("p m (b t) -> p (m b) t", b=2), acc(step), 1.0 / 512, EPS, ALU.mult,
                                ALU.add).then_inc(free(step), 1)
        wait_free(dve, step)
        nc.vector.reciprocal(V2[:], V2[:]).then_inc(yv_done, 1)
        dve.wait_ge(yr_done, 1)
        for g in range(2):
            y = XS[:, 4 * g:4 * g + 4, :]
            nc.vector.tensor_tensor(y, y, RT2[:, g:g + 1, :].broadcast_to([P, 4, T]), ALU.mult).then_inc(yn_done, 1)
        for t in range(8):
            dve.wait_ge(yh_done, t + 1)
            nc.vector.scalar_tensor_tensor(e.XL[:, t, :], XS[:, t, :], PV[:, V_HNORM + t:V_HNORM + t + 1],
                                           e.XH[:, t, :].bitcast(F32), ALU.mult, ALU.subtract).then_inc(yl_done, 1)
        for g in range(4):
            a.splits(6)
            a.residual(("hout", g), g, 1.0)
            a.splits(2)
        for g in range(4):
            a.lows(nn + 1, g)

    def pool(pool, a):
        def store(dst, src):
            pool.dma_start(dst, src).then_inc(e.out_stored, 16)
            a.stores[0] += 1

        if before:
            wait_full(pool, (before, "out", 3))
        pool.dma_start(CT[:], io["ret_cos"]).then_inc(loaded, 16)
        pool.dma_start(SN[:], io["ret_sin"]).then_inc(loaded, 16)
        pool.dma_start(SEG[:], io["ret_decays"]).then_inc(loaded, 16)
        wait_free(pool, ("ret S", 3))
        pool.dma_start(S0[0][:], io["state_ret"][:, 0:2]).then_inc(s0_loaded[0], 16)
        wait_free(pool, ("ret O", 3))
        pool.dma_start(S0[1][:], io["state_ret"][:, 2:4]).then_inc(s0_loaded[1], 16)
        store(io["ret_p"], RST[:])
        for p in range(NS // 2):
            wait_free(pool, ("ret outer", p))
            pool.dma_start(io["ret_s"][:, 2 * p:2 * p + 2], S0[p % 2][:]).then_inc(s0_stored[p % 2], 16)
            if p < 2:
                pool.wait_ge(s0_stored[p % 2], 16)
                wait_full(pool, ("ret y", p))
                pool.dma_start(S0[p % 2][:], io["state_ret"][:, 2 * p + 4:2 * p + 6]).then_inc(s0_loaded[p % 2], 16)
        for s in range(2):
            pool.wait_ge(s0_stored[s], 32)
        pool.wait_ge(gs_done, 8)
        pool.dma_start(SCI[:], io["state_conv"]).then_inc(conv_loaded, 16)
        pool.wait_ge(out_ready, 1)
        store(io["conv_p"], CPO[:])
        store(io["conv_s"], CSO[:])
        pool.wait_ge(e.out_stored, 16 * a.stores[0])
        pool.wait_ge(dt_done, 1)
        for c in range(NTT):
            if c:
                wait_full(pool, ("ssm sc", c - 1))
            nc.gpsimd.tensor_copy(LAW[:], LA[:, c, :].rearrange("p (g h) -> p h g", g=2).unsqueeze(3)
                                  .broadcast_to([P, 8, 2, 64])).then_inc(law_done, 1)
            if c:
                wait_full(pool, ("ssm D", c - 1))
            nc.gpsimd.tensor_tensor(LM[:], AFTER.unsqueeze(1).broadcast_to([P, SH, P]),
                                    LA[:, c, :].unsqueeze(2).broadcast_to([P, SH, P]), ALU.mult).then_inc(l_done, 1)
            if c:
                wait_full(pool, ("ssm y", c - 1))
            else:
                wait_free(pool, "ssm xT1")
                wait_free(pool, "ssm sums")
            nc.gpsimd.tensor_tensor(XEND[:].rearrange("p (h d) -> p h d", d=SHD),
                                    XTOK[:, c, :].rearrange("p (h d) -> p h d", d=SHD),
                                    DEX[:, 0, c * SH:(c + 1) * SH].unsqueeze(2).broadcast_to([P, SH, SHD]),
                                    ALU.mult).then_inc(xend_done, 1)
        wait_full(pool, ("ssm y", 3))
        pool.dma_start(SSS[:], io["state_ssm"]).then_inc(sss_loaded, 16)
        wait_free(pool, ("ssm y", 3))
        store(io["ssm_p"], SST[:])
        wait_free(pool, ("ssm outer", 1))
        store(io["ssm_s"], SSS[:])
        a.norm_sums(nn + 1)
        pool.wait_ge(e.out_stored, 16 * a.stores[0])

    parts = Shared()
    parts.pe, parts.act, parts.dve, parts.pool = pe, act, dve, pool
    return parts


def lay_out_hyb(a, tile, gamma):
    f = np.float32
    i = np.arange(P)
    dist = np.arange(NP_)[None, :] - i[:, None]
    decays = np.stack([np.where(dist >= 0, np.exp(g * np.maximum(dist, 0)), 0.0) for g in gamma], 1).astype(f)
    pos = np.concatenate([np.arange(NP_), np.full(NS, PAST)]).astype(f)
    inv = (np.float32(10000.0) ** (-np.arange(64, dtype=f) / 64)).astype(f)
    ang = (inv[:, None] * pos[None]).astype(f)
    cos, sin = np.cos(ang.astype(np.float64)), np.sin(ang.astype(np.float64))
    return {
        "ret_decays": decays,
        "ret_cos": np.concatenate([cos, cos], 0).astype(f),
        "ret_sin": np.concatenate([sin, -sin], 0).astype(f),
        "state_ret": a["state_ret"][0].transpose(2, 0, 1, 3),
        "state_conv": a["state_conv"][0].reshape(NS, 3, XBC, P).transpose(3, 2, 1, 0),
        "state_ssm": a["state_ssm"][0].reshape(NS, 2, 8, SST_N, SHD).transpose(1, 3, 0, 2, 4).reshape(P, NS, 512),
    }


SST_N = 64
OUT_HYB = {"ret_p": (P, RH, RDV), "ret_s": (P, NS, RH, RDV), "conv_p": (P, XBC, 3), "conv_s": (P, XBC, 3, NS),
           "ssm_p": (P, 512), "ssm_s": (P, NS, 512)}


def hyb_results(o):
    ssm = lambda s, n: s.reshape(2, SST_N, n, 8, SHD).transpose(2, 0, 3, 1, 4).reshape(1, n, SH, SST_N, SHD)
    return (o["ret_p"].transpose(1, 0, 2)[None, None], o["ret_s"].transpose(1, 2, 0, 3)[None],
            ssm(o["ssm_p"], 1), ssm(o["ssm_s"], NS),
            o["conv_p"].transpose(2, 1, 0).reshape(1, 1, 3, XBC * P),
            o["conv_s"].transpose(3, 2, 1, 0).reshape(1, NS, 3, XBC * P))


def mla_parts(e):
    nc, io, plan, at, sem, PS = e.nc, e.io, e.plan, e.at, e.sem, e.PS
    REGION, GU_OFF = e.REGION, e.GU_OFF
    IDENT, ONES, NEGM, PV, RSTD = e.IDENT, e.ONES, e.NEGM, e.PV, e.RSTD
    acc, bank0, halves = e.acc, e.bank0, e.halves
    wait_full, wait_free, acquire = e.wait_full, e.wait_free, e.acquire
    full = lambda step: e.acc_full[plan.set_of[step]]
    free = lambda step: e.acc_free[plan.set_of[step]]
    nn = e.nn_of["mla"]
    before = e.phases[nn - 1] if nn else None
    XH, XL = e.XH, e.XL

    CQF = at("q_latent", [P, 4, T], REGION)
    XQH = at("q_latent_high", [P, 4, T], REGION + 8320, F32R)
    XQL = at("q_latent_low", [P, 4, T], REGION + 16640, F32R)
    WUKT = at("w_uk_by_head", [NOPE, MH, KVL], REGION)
    WUV = at("w_uv_f32", [P, 2, MH * VD], REGION + 16384)
    OTOK = at("attention_tokens", [P, NTT, MH * VD], REGION)
    CKF = at("kv_latent", [P, 2, T], REGION + 24960)
    CKH = at("kv_latent_high", [P, 2, T], REGION + 29120, F32R)
    CKL = at("kv_latent_low", [P, 2, T], REGION + 33280, F32R)
    KRT = at("rotary_key", [P, T], REGION + 37440)
    Q = at("queries", [P, MH, T], REGION + 39520)
    TAB = at("query_scale", [P, T], REGION + 72800)
    TABR = at("rope_table", [P, T], REGION + 74880)
    TB = [at(f"cache_by_feature{i}", [P, 8, 3 * P], REGION + 76960 + 12288 * i) for i in range(2)]
    NAT = [at(f"cache_by_row{i}", [P, NPG, KVL], e.XH_OFF + 16384 * i) for i in range(2)]
    KTT = at("keys", [P, MH, NP_], e.XH_OFF)
    V = at("values", [P, NTT, MH * VD], REGION + 76960)
    PB = [at(f"probs{i}", [P, 1280], REGION + 93344 + 5120 * i) for i in range(2)]
    KRX = at("rotary_parts", [P, T], REGION + 93344 + 0)
    KRB = at("rotary_second", [P, T], REGION + 93344 + 2080)
    TABK = at("key_table", [P, T], REGION + 93344 + 4160)
    PT = [at(f"probs_by_key{i}", [P, 1280], GU_OFF + 5120 * i) for i in range(2)]
    SQC = at("latent_squares", [P, 6, T], GU_OFF)
    V2 = at("latent_variance", [P, 2, T], GU_OFF + 12480)
    R2 = at("latent_rstd", [P, 2, T], e.SQT_OFF)
    SSB = [at(f"sample_scores{i}", [P, (NPG + 1) * MH], GU_OFF + 1088 * i) for i in range(2)]
    SPB = [at(f"sample_probs{i}", [P, NPG + 1, MH], GU_OFF + 2176 + 1088 * i) for i in range(2)]
    MXP = at("sample_max", [P, MH], GU_OFF + 4352)
    MXA = at("sample_max_all", [P, MH], GU_OFF + 4416)
    LSUM = at("sample_sum", [P, MH], GU_OFF + 4480)
    LPN = at("sample_sum_all", [P, 2 * MH], GU_OFF + 4544)
    O2 = at("sample_out_part", [P, 2, MH], GU_OFF + 4672)
    QLAT = at("sample_q_latent", [P, 2, NS, MH], GU_OFF + 4800)
    OLAT = at("sample_out_latent", [P, 2, MH, NS], GU_OFF + 5824)
    OTS = at("sample_out", [P, 8, NS], GU_OFF + 14848)
    MX = at("row_max", [P, 2, NTT], GU_OFF + 15104)
    LS = at("row_sum", [P, 2, NTT], GU_OFF + 15136)
    RL = at("row_rcp", [P, 2, NTT], GU_OFF + 15168)
    PGT = at("page_numbers", [1, NS * NPG], REGION + 103584, I32)

    loaded, wuk_loaded = sem("mla_tables_loaded"), sem("sample_weights_loaded")
    t_loaded = [sem("cache_features_loaded0"), sem("cache_features_loaded1")]
    n_loaded = [sem("cache_rows_loaded0"), sem("cache_rows_loaded1")]
    t_used = sem("cache_features_used")
    lsq_done, xqh_done, xq_done = sem("latent_squares_done"), sem("q_high_done"), sem("q_low_done")
    lv_done, lr_done = sem("latent_rcp_done"), sem("latent_rstd_done")
    ckn_done, ckh_done, ck_done = sem("kv_normed_done"), sem("kv_high_done"), sem("kv_low_done")
    kr_done, krr_done = sem("rotary_key_done"), sem("keys_rotary_done")
    smx_done, sall_done, sd_done, sp_done, sl_done = (sem(n) for n in (
        "sample_max_done", "sample_max_all_done", "sample_scores_less_max", "sample_probs_done", "sample_sum_done"))
    mx_done, oh_done, ol_done = sem("row_max_done"), sem("out_high_done"), sem("out_low_done")
    block_of = lambda it, jt: it * (it + 1) // 2 + jt
    PAGE_LOADS_FROM = plan.first[("uq", 0)] + 2 * R
    STOP = plan.first[("uk", 0)] + 2 * R

    def sp(sp, weight_chunks):
        def page_load(b, pg, what, i=None, wait=None):
            at_ = b * NPG + pg
            idx = sp.value_load(PGT[0:1, at_:at_ + 1] if i is None else PGT[0:1, bass.ds(2 * NPG * i + at_, 1)],
                                min_val=0, max_val=N_PHYS - 1)
            if wait:
                wait()
            if what == "rows":
                sp.dma_start(NAT[b % 2][:, pg, :], io["cache_rows"][bass.ds(idx, 1)]
                             .rearrange("a p n -> (a p) n")).then_inc(n_loaded[b % 2], 16)
            else:
                sp.dma_start(TB[pg // 8][:, pg % 8, :], io["cache_features"][bass.ds(idx, 1)]
                             .rearrange("a p n -> (a p) n")).then_inc(t_loaded[pg // 8], 16)

        weight_chunks(0, PAGE_LOADS_FROM)
        sp.wait_ge(loaded, 32)
        if before:
            wait_full(sp, (before, "out", 3))
        wait_full(sp, ("min", 3))
        sp.wait_ge(kr_done, 2)
        todo = [(0, pg, "features") for pg in range(NPG)] + [(b, pg, "rows") for b in range(2) for pg in range(NPG)]
        per = -(-len(todo) // (STOP - PAGE_LOADS_FROM))
        for n in range(PAGE_LOADS_FROM, STOP):
            weight_chunks(n, n + 1)
            for item in todo[:per]:
                page_load(*item)
            todo = todo[per:]

        def features(b, i=None):
            for u in range(2):
                waits = [lambda: sp.wait_ge(t_used, b if i is None else 2 * i + b),
                         lambda: wait_full(sp, ("smp S", b - 1), None if i is None else 2 * i)]
                for pg in range(8 * u, 8 * u + 8):
                    page_load(b, pg, "features", i, waits[u] if pg % 8 == 0 else None)

        features(1)
        with sp.Fori(0, (NS - 2) // 2) as i:
            for b in (2, 3):
                for pg in range(NPG):
                    page_load(b, pg, "rows", i, (lambda: wait_full(sp, ("smp PV", b - 2), 2 * i)) if pg == 0 else None)
                features(b, i)
        weight_chunks(STOP, None)

    def pe(pe):
        def transposes(step, items, waits=()):
            acquire(pe, step)
            for w in waits:
                w()
            for out, src in items:
                k = src.shape[0]
                mm = nc.tensor.transpose(out, src, IDENT[0:k, 0:k])
            mm.then_inc(full(step), 1)

        e.gemm(pe, ("min", 0), 2, KD, e.x_rhs, before_k=e.first_wait(pe, nn))
        e.pe_stats(pe, "mla stats", nn)
        e.gemm(pe, ("min", 1), 2, KD, e.x_rhs)
        e.gemm(pe, ("min", 2), 2, KD, e.x_rhs)
        e.gemm(pe, ("min", 3), 1, KD, e.x_rhs)
        step = "mla cnorm"
        acquire(pe, step)
        pe.wait_ge(lsq_done, 3)
        b = bank0(step)
        for which, tiles in enumerate((range(4), range(4, 6))):
            for half in range(2):
                for t in tiles:
                    mm = nc.tensor.matmul(PS[:, b + 2 * which + half, 0:TH], ONES, SQC[:, t, half * TH:(half + 1) * TH],
                                          start=t == tiles[0], stop=t == tiles[-1])
        mm.then_inc(full(step), 1)
        for g in range(8):
            e.gemm(pe, ("uq", g), 2, 4, lambda k: (XQH[:, k, :], XQL[:, k, :]),
                   before_k=(lambda k: pe.wait_ge(xq_done, k + 1)) if g == 0 else None)
        step = "smp qlat"
        acquire(pe, step)
        wait_free(pe, ("uq", 7))
        pe.wait_ge(wuk_loaded, 32)
        b = bank0(step)
        for h in range(MH):
            for ct in range(2):
                mm = nc.tensor.matmul(PS[:, b + ct, h * NS:(h + 1) * NS], WUKT[:, h, ct * P:(ct + 1) * P],
                                      Q[0:NOPE, h, NP_:T], start=True, stop=True)
        mm.then_inc(full(step), 1)
        for s in range(NS):
            step = ("smp S", s)
            acquire(pe, step)
            if s == 0:
                wait_free(pe, "smp qlat")
                pe.wait_ge(kr_done, 2)
                pe.wait_ge(ckn_done, 2)
            b = bank0(step)
            qr = Q[64:128, :, NP_ + s]
            for pg in range(NPG):
                u = pg // 8
                if pg % 8 == 0:
                    pe.wait_ge(t_loaded[u], 16 * 8 * (s + 1))
                out = PS[:, b, pg * MH:(pg + 1) * MH]
                for ct in range(2):
                    nc.tensor.matmul(out, TB[u][:, pg % 8, ct * P:(ct + 1) * P], QLAT[:, ct, s, :], start=ct == 0, stop=False)
                mm = nc.tensor.matmul(out, TB[u][64:128, pg % 8, 2 * P:3 * P], qr, start=False, stop=True)
                if pg == 7:
                    mm.then_inc(t_used, 1)
            out = PS[0:1, b + 1, 0:MH]
            for ct in range(2):
                nc.tensor.matmul(out, CKF[:, ct, NP_ + s:NP_ + s + 1], QLAT[:, ct, s, :], start=ct == 0, stop=False)
            nc.tensor.matmul(out, KRT[64:128, NP_ + s:NP_ + s + 1], qr, start=False, stop=True).then_inc(full(step), 1)
            step = ("smp PV", s)
            acquire(pe, step)
            pe.wait_ge(sp_done, s + 1)
            pe.wait_ge(sl_done, s + 1)
            pe.wait_ge(n_loaded[s % 2], 16 * NPG * (s // 2 + 1))
            b = bank0(step)
            nc.tensor.matmul(PS[:, b + 1, 0:MH], ONES, LSUM[:], start=True, stop=True)
            nc.tensor.matmul(PS[:, b + 1, MH:2 * MH], ONES[0:1, :], SPB[s % 2][0:1, NPG, :], start=True, stop=True)
            for ct in range(2):
                for pg in range(NPG):
                    mm = nc.tensor.matmul(PS[:, b, ct * MH:(ct + 1) * MH], NAT[s % 2][:, pg, ct * P:(ct + 1) * P],
                                          SPB[s % 2][:, pg, :], start=pg == 0, stop=pg == NPG - 1)
            mm.then_inc(full(step), 1)
        step = "smp O"
        acquire(pe, step)
        wait_free(pe, ("smp PV", NS - 1))
        b = bank0(step)
        for h in range(MH):
            for ct in range(2):
                mm = nc.tensor.matmul(PS[64 * (h % 2):64 * (h % 2) + 64, b, (h // 2) * NS:(h // 2 + 1) * NS],
                                      WUV[:, ct, h * VD:(h + 1) * VD], OLAT[:, ct, h, :], start=ct == 0, stop=ct == 1)
        mm.then_inc(full(step), 1)
        for g in range(4):
            e.gemm(pe, ("uk", g), 2, 2, lambda k: (CKH[:, k, :], CKL[:, k, :]), cols=NP_ // 2,
                   before_k=(lambda k: pe.wait_ge(ck_done, k + 1)) if g == 0 else None)
        for g in range(2):
            step = ("uv", g)
            acquire(pe, step)
            b = bank0(step)
            for ct in range(2):
                n = plan.first[step] + ct
                pe.wait_ge(e.w_split, n + 1)
                for tt in range(NTT):
                    kh, kl = (k[:, ct, tt * P:(tt + 1) * P] for k in (CKH, CKL))
                    wh, wl = e.WH[:, n % R, :], e.WL[:, n % R, :]
                    for k, w, st, sp_ in ((kh, wh, ct == 0, False), (kh, wl, False, False), (kl, wh, False, ct == 1)):
                        mm = nc.tensor.matmul(PS[:, b + tt, :], k, w, start=st, stop=sp_)
                mm.then_inc(e.w_used if ct == 0 else full(step), 1)

        def scores(h):
            step = ("att S", h)
            acquire(pe, step)
            if h == 0:
                wait_free(pe, ("uk", 3))
                pe.wait_ge(krr_done, 1)
            b = bank0(step)
            for it in range(NTT):
                n = (it + 1) * P
                nc.tensor.matmul(PS[:, b + it, 0:n], Q[:, h, it * P:n], KTT[:, h, 0:n], start=True, stop=False)
                mm = nc.tensor.matmul(PS[:, b + it, it * P:n], IDENT, NEGM, start=False, stop=True)
            mm.then_inc(full(step), 1)

        scores(0)
        for h in range(MH):
            if h + 1 < MH:
                scores(h + 1)
            step = ("att T", h)
            b = bank0(step)
            transposes(step, [(PS[:, b + n // 4, (n % 4) * P:(n % 4 + 1) * P], PB[h % 2][:, n * P:(n + 1) * P])
                              for n in range(10)], [lambda: wait_free(pe, ("att S", h))])
            step = ("att O", h)
            acquire(pe, step)
            wait_free(pe, ("att T", h))
            if h == 0:
                wait_free(pe, ("uv", 1))
            b = bank0(step)
            for it in range(NTT):
                for jt in range(it + 1):
                    n = block_of(it, jt)
                    mm = nc.tensor.matmul(PS[:, b, it * VD:(it + 1) * VD], PT[h % 2][:, n * P:(n + 1) * P],
                                          V[:, jt, h * VD:(h + 1) * VD], start=jt == 0, stop=jt == it)
            mm.then_inc(full(step), 1)
        for v in range(2):
            b = bank0(f"att OT{v}")
            transposes(f"att OT{v}", [(PS[:, b + t, it * P:(it + 1) * P], OTOK[:, it, (4 * v + t) * P:(4 * v + t + 1) * P])
                                      for t in range(4) for it in range(NTT)],
                       [lambda: wait_free(pe, ("att O", MH - 1))])
        for g in range(4):
            e.gemm(pe, ("wo", g), 2, KD, e.x_rhs,
                   before_k=(lambda k: pe.wait_ge(ol_done, 1)) if g == 0 else None)

    def act(act, a):
        for g in range(2):
            a.splits(2)
            if g == 0:
                a.stats(nn)
            wait_free(act, ("min", g))
            nc.scalar.activation(SQC[:, 2 * g:2 * g + 2, :], CQF[:, 2 * g:2 * g + 2, :], ACT.Square).then_inc(lsq_done, 1)
            for m in range(2):
                t = 2 * g + m
                nc.scalar.activation(XQH[:, t, :], CQF[:, t, :], ACT.Copy,
                                     scale=PV[:, V_QNORM + t:V_QNORM + t + 1]).then_inc(xqh_done, 1)
            a.splits(2)
        a.splits(2)
        wait_free(act, ("min", 2))
        nc.scalar.activation(SQC[:, 4:6, :], CKF[:], ACT.Square).then_inc(lsq_done, 1)
        a.splits(2)
        a.splits(2)
        act.wait_ge(lv_done, 1)
        nc.scalar.activation(R2[:], V2[:], ACT.Sqrt).then_inc(lr_done, 1)
        act.wait_ge(ckn_done, 2)
        for t in range(2):
            nc.scalar.activation(CKH[:, t, :], CKF[:, t, :], ACT.Copy).then_inc(ckh_done, 1)
        for g in range(8):
            a.splits(2)
        for s in range(NS):
            act.wait_ge(sd_done, s + 1)
            nc.scalar.activation(SPB[s % 2][:], SPB[s % 2][:], ACT.Exp, scale=MLA_SCALE).then_inc(sp_done, 1)
        for g in range(4):
            a.splits(1)
        for g in range(2):
            step = ("uv", g)
            wait_full(act, step)
            b = bank0(step)
            nc.scalar.activation(V[:, :, g * 512:(g + 1) * 512], PS[:, b:b + 4, :], ACT.Copy).then_inc(free(step), 1)
            a.splits(2)

        def exps(h):
            step = ("att S", h)
            act.wait_ge(mx_done, h + 1)
            if h >= 2:
                wait_full(act, ("att T", h - 2))
                wait_free(act, ("att O", h - 2))
            b = bank0(step)
            for it in range(NTT):
                n0 = block_of(it, 0) * P
                ins = nc.scalar.activation(PB[h % 2][:, n0:n0 + (it + 1) * P], PS[:, b + it, 0:(it + 1) * P], ACT.Exp,
                                           bias=MX[:, h % 2, it:it + 1], scale=MLA_SCALE,
                                           accum_out=LS[:, h % 2, it:it + 1])
            ins.then_inc(free(step), 1)

        exps(0)
        for h in range(MH):
            if h + 1 < MH:
                exps(h + 1)
        for v in range(2):
            step = f"att OT{v}"
            wait_full(act, step)
            b = bank0(step)
            nc.scalar.activation(XH[:, 4 * v:4 * v + 4, 0:NP_], PS[:, b:b + 4, :], ACT.Copy).then_inc(oh_done, 1)
        nc.scalar.activation(XH[:, :, NP_:T], OTS[:], ACT.Copy).then_inc(oh_done, 1)
        for g in range(4):
            a.splits(2)
            wait_free(act, ("wo", g))
            a.squares(nn + 1, g)
            a.splits(2)
        wait_full(act, ("wo", 3))
        for g in range(4):
            a.highs(nn + 1, g)

    def dve(dve, a):
        link = a.link

        def latent(g, out):
            step = ("min", g)
            wait_full(dve, step)
            nc.vector.tensor_tensor(halves(out[:, 0, :]), acc(step)[:, 0:2, :], halves(RSTD[:]), ALU.mult)
            nc.vector.tensor_tensor(halves(out[:, 1, :]), acc(step)[:, 2:4, :], halves(RSTD[:]),
                                    ALU.mult).then_inc(free(step), 1)
            wait_free(dve, step)

        for g in range(2):
            a.splits(2)
            if g == 0:
                a.stats("mla stats", nn)
                dve.wait_ge(loaded, 32)
                link(nc.vector.tensor_tensor(TABK[64:128, :], TABR[64:128, :], RSTD[64:128, :], ALU.mult))
            latent(g, CQF[:, 2 * g:2 * g + 2, :])
            for m in range(2):
                t = 2 * g + m
                dve.wait_ge(xqh_done, t + 1)
                nc.vector.scalar_tensor_tensor(XQL[:, t, :], CQF[:, t, :], PV[:, V_QNORM + t:V_QNORM + t + 1],
                                               XQH[:, t, :].bitcast(F32), ALU.mult, ALU.subtract).then_inc(
                                                   xq_done, 1)
            a.splits(2)
        a.splits(2)
        latent(2, CKF)
        a.splits(2)
        step = ("min", 3)
        wait_full(dve, step)
        nc.vector.tensor_tensor(halves(KRX[64:128, :]), PS[64:128, bank0(step):bank0(step) + 2, 0:TH],
                                halves(TABK[64:128, :]), ALU.mult).then_inc(free(step), 1)
        wait_free(dve, step)
        link(nc.vector.tensor_copy(KRB[64:96, :], KRX[96:128, :]))
        nc.vector.tensor_tensor(KRT[64:96, :], KRX[64:96, :], KRB[64:96, :], ALU.add).then_inc(kr_done, 1)
        dve.wait_ge(kr_done, 1)
        nc.vector.tensor_copy(KRT[96:128, :], KRT[64:96, :]).then_inc(kr_done, 1)
        a.splits(2)
        step = "mla cnorm"
        wait_full(dve, step)
        b = bank0(step)
        nc.vector.tensor_scalar(halves(V2[:, 0, :]), PS[:, b:b + 2, 0:TH], 1.0 / QL, EPS, ALU.mult, ALU.add)
        nc.vector.tensor_scalar(halves(V2[:, 1, :]), PS[:, b + 2:b + 4, 0:TH], 1.0 / KVL, EPS, ALU.mult,
                                ALU.add).then_inc(free(step), 1)
        wait_free(dve, step)
        nc.vector.reciprocal(V2[:], V2[:]).then_inc(lv_done, 1)
        dve.wait_ge(lr_done, 1)
        for t in range(2):
            nc.vector.scalar_tensor_tensor(CKF[:, t, :], CKF[:, t, :], PV[:, V_KVNORM + t:V_KVNORM + t + 1], R2[:, 1, :],
                                           ALU.mult, ALU.mult).then_inc(ckn_done, 1)
        link(nc.vector.tensor_tensor(TAB[:], TABR[:], R2[:, 0, :], ALU.mult))
        for t in range(2):
            dve.wait_ge(ckh_done, t + 1)
            nc.vector.tensor_tensor(CKL[:, t, :], CKF[:, t, :], CKH[:, t, :].bitcast(F32), ALU.subtract).then_inc(ck_done, 1)
        for g in range(8):
            step = ("uq", g)
            wait_full(dve, step)
            for m in range(2):
                ins = nc.vector.tensor_tensor(halves(Q[:, 2 * g + m, :]), acc(step)[:, 2 * m:2 * m + 2, :], halves(TAB[:]),
                                              ALU.mult)
            ins.then_inc(free(step), 1)
            a.splits(2)
        step = "smp qlat"
        nc.vector.memset(SSB[0][:, NPG * MH:], NEG)
        link(nc.vector.memset(SSB[1][:, NPG * MH:], NEG))
        wait_full(dve, step)
        b = bank0(step)
        for ct in range(2):
            ins = nc.vector.tensor_copy(QLAT[:, ct], PS[:, b + ct, 0:MH * NS].rearrange("p (h b) -> p b h", b=NS))
        ins.then_inc(free(step), 1)
        for s in range(NS):
            step = ("smp S", s)
            wait_full(dve, step)
            b = bank0(step)
            ss = SSB[s % 2]
            nc.vector.tensor_copy(ss[:, 0:NPG * MH], PS[:, b, 0:NPG * MH])
            nc.vector.tensor_copy(ss[0:1, NPG * MH:], PS[0:1, b + 1, 0:MH]).then_inc(free(step), 1)
            wait_free(dve, step)
            by_head = ss[:].rearrange("p (g h) -> p h g", h=MH)
            nc.vector.tensor_reduce(MXP[:], by_head, AX.X, ALU.max).then_inc(smx_done, 1)
            dve.wait_ge(sall_done, s + 1)
            pb = SPB[s % 2]
            nc.vector.tensor_tensor(pb[:], ss[:].rearrange("p (g h) -> p g h", h=MH),
                                    MXA[:].unsqueeze(1).broadcast_to([P, NPG + 1, MH]), ALU.subtract).then_inc(sd_done, 1)
            dve.wait_ge(sp_done, s + 1)
            nc.vector.tensor_reduce(LSUM[:], pb[:].rearrange("p g h -> p h g"), AX.X, ALU.add).then_inc(sl_done, 1)
            step = ("smp PV", s)
            wait_full(dve, step)
            b = bank0(step)
            link(nc.vector.tensor_copy(LPN[:], PS[:, b + 1, 0:2 * MH]))
            nc.vector.reciprocal(LPN[:, 0:MH], LPN[:, 0:MH])
            for ct in range(2):
                ins = nc.vector.scalar_tensor_tensor(O2[:, ct, :], LPN[:, MH:2 * MH], CKF[:, ct, NP_ + s:NP_ + s + 1],
                                                     PS[:, b, ct * MH:(ct + 1) * MH], ALU.mult, ALU.add)
            link(ins)
            nc.vector.tensor_tensor(OLAT[:, :, :, s], O2[:], LPN[:, 0:MH].unsqueeze(1).broadcast_to([P, 2, MH]),
                                    ALU.mult).then_inc(free(step), 1)
            wait_free(dve, step)
        step = "smp O"
        wait_full(dve, step)
        nc.vector.tensor_copy(OTS[:].rearrange("p t b -> p (t b)"), PS[:, bank0(step), 0:64]).then_inc(free(step), 1)
        for g in range(4):
            step = ("uk", g)
            wait_full(dve, step)
            b = bank0(step)
            for m in range(2):
                for hh in range(2):
                    ins = nc.vector.tensor_copy(KTT[0:64, 4 * g + 2 * m + hh, :].rearrange("p (a t) -> p a t", a=2),
                                                PS[64 * hh:64 * hh + 64, b + 2 * m:b + 2 * m + 2, 0:NP_ // 2])
            ins.then_inc(free(step), 1)
            a.splits(1)
        for g in range(2):
            a.splits(2)

        def maxima(h):
            step = ("att S", h)
            wait_full(dve, step)
            if h >= 2:
                wait_free(dve, ("att S", h - 2))
            b = bank0(step)
            for it in range(NTT):
                ins = nc.vector.tensor_reduce(MX[:, h % 2, it:it + 1], PS[:, b + it, 0:(it + 1) * P], AX.X, ALU.max)
            link(ins)
            nc.vector.tensor_scalar(MX[:, h % 2, :], MX[:, h % 2, :], -MLA_SCALE, None, ALU.mult).then_inc(mx_done, 1)

        maxima(0)
        for h in range(MH):
            if h + 1 < MH:
                maxima(h + 1)
            step = ("att T", h)
            wait_full(dve, step)
            if h >= 2:
                wait_full(dve, ("att O", h - 2))
            b = bank0(step)
            nc.vector.tensor_copy(PT[h % 2][:], PS[:, b:b + 3, :].rearrange("p a n -> p (a n)")[:, 0:1280]).then_inc(free(step), 1)
            wait_free(dve, ("att S", h))
            link(nc.vector.reciprocal(RL[:, h % 2, :], LS[:, h % 2, :]))
            step = ("att O", h)
            wait_full(dve, step)
            b = bank0(step)
            nc.vector.tensor_tensor(OTOK[:, :, h * VD:(h + 1) * VD], PS[:, b, 0:NTT * VD].rearrange("p (i d) -> p i d", i=NTT),
                                    RL[:, h % 2, :].unsqueeze(2).broadcast_to([P, NTT, VD]), ALU.mult).then_inc(free(step), 1)
        for v in range(2):
            step = f"att OT{v}"
            dve.wait_ge(oh_done, v + 1)
            b = bank0(step)
            nc.vector.tensor_tensor(XL[:, 4 * v:4 * v + 4, 0:NP_], PS[:, b:b + 4, :], XH[:, 4 * v:4 * v + 4, 0:NP_].bitcast(F32),
                                    ALU.subtract).then_inc(free(step), 1)
        dve.wait_ge(oh_done, 3)
        wait_free(dve, "att OT1")
        nc.vector.tensor_tensor(XL[:, :, NP_:T], OTS[:], XH[:, :, NP_:T].bitcast(F32), ALU.subtract).then_inc(ol_done, 1)
        for g in range(4):
            a.splits(2)
            a.residual(("wo", g), g, 1.0)
            a.splits(2)
        for g in range(4):
            a.lows(nn + 1, g)

    def pool(pool, a):
        def store(dst, src):
            pool.dma_start(dst, src).then_inc(e.out_stored, 16)
            a.stores[0] += 1

        if before:
            wait_full(pool, (before, "out", 3))
            wait_free(pool, (before, "out", 3))
        pool.dma_start(TABR[:], io["mla_rope"]).then_inc(loaded, 16)
        pool.dma_start(PGT[:], io["page_table"]).then_inc(loaded, 16)
        pool.wait_ge(kr_done, 2)
        store(io["kr"], KRT[64:96, :])
        pool.wait_ge(ckn_done, 2)
        store(io["ckv"], CKF[:])
        wait_full(pool, ("uq", 7))
        pool.dma_start(WUKT[:], io["w_uk_by_head"]).then_inc(wuk_loaded, 16)
        pool.dma_start(WUV[:], io["w_uv"]).then_inc(wuk_loaded, 16)
        for s in range(NS):
            pool.wait_ge(smx_done, s + 1)
            nc.gpsimd.partition_all_reduce(MXA[:], MXP[:], P, RMAX).then_inc(sall_done, 1)
        wait_full(pool, ("smp PV", NS - 1))
        nc.gpsimd.tensor_copy(KTT[64:128, :, :], KRT[64:128, 0:NP_].unsqueeze(1).broadcast_to([64, MH, NP_])).then_inc(krr_done, 1)
        a.norm_sums(nn + 1)
        pool.wait_ge(e.out_stored, 16 * a.stores[0])

    parts = Shared()
    parts.pe, parts.act, parts.dve, parts.pool, parts.sp = pe, act, dve, pool, sp
    return parts


def lay_out_mla(a, tile):
    f = np.float32
    pos = np.concatenate([np.arange(NP_), np.full(NS, PAST)]).astype(f)
    half = ROPE // 2
    inv = (np.float32(10000.0) ** (-np.arange(half, dtype=f) / half)).astype(f)
    ang = (inv[:, None] * pos[None]).astype(f).astype(np.float64)
    cos, sin = np.cos(ang), np.sin(ang)
    ckv, kr = a["cache_ckv"][0], a["cache_krope"][0]
    krt = kr.transpose(0, 2, 1)
    features = np.concatenate([ckv.reshape(N_PHYS, PAGE, 2, P).transpose(0, 3, 2, 1).reshape(N_PHYS, P, 2 * PAGE),
                               np.concatenate([np.zeros((N_PHYS, 64, PAGE), f), krt, krt], 1)], 2)
    return {
        "mla_rope": np.concatenate([np.ones((64, T)), cos, cos, -sin, sin], 0).astype(f),
        "cache_rows": ckv,
        "cache_features": features,
        "page_table": a["page_table"].reshape(1, NS * NPG),
        "w_uk_by_head": a["mla_w_uk"][0].transpose(2, 1, 0),
        "w_uv": a["mla_w_uv"][0].reshape(2, P, MH * VD).transpose(1, 0, 2),
    }


OUT_MLA = {"ckv": (P, 2, T), "kr": (ROPE, T)}


def mla_results(o):
    ckv = o["ckv"].transpose(1, 0, 2).reshape(KVL, T).T
    kr = o["kr"].T
    return (ckv[None, None, :NP_], ckv[None, NP_:, None], kr[None, None, :NP_], kr[None, NP_:, None])


def kernel(**inputs):
    import concourse.bacc as bacc
    from concourse.bass_utils import run_bass_kernel_spmd

    nc = bacc.Bacc("TRN2", target_bir_lowering=False, num_devices=1)
    arrays, io = {}, {}
    for name, a in lay_out(inputs).items():
        arrays[f"in_{name}_dram"] = a
        io[name] = nc.dram_tensor(f"in_{name}_dram", a.shape, mybir.dt.from_np(a.dtype), kind="ExternalInput").ap()
    shapes = outputs()
    for name, shape in shapes.items():
        io[name] = nc.dram_tensor(f"out_{name}_dram", shape, F32, kind="ExternalOutput").ap()
    program(nc, io)
    r = run_bass_kernel_spmd(nc, [arrays], core_ids=[0])
    o = {name: np.asarray(r.results[0][f"out_{name}_dram"]) for name in shapes}
    y = o["y"].transpose(1, 0, 2).reshape(D, T).T
    got = (y[None, :NP_], y[NP_:, None]) + tuple(hyb_results(o)) + tuple(mla_results(o))
    return tuple(np.ascontiguousarray(g) for g in got)
```

```python
import numpy as np
import concourse.bass as bass
from concourse import mybir
from contextlib import ExitStack

F32 = mybir.dt.float32
F32R = mybir.dt.float32r
I32 = mybir.dt.int32
ALU = mybir.AluOpType
ACT = mybir.ActivationFunctionType
AX = mybir.AxisListType
RMAX = bass.bass_isa.ReduceOp.max

P = 128
D = 1024
KD = D // P
NP_ = 512
NS = 8
T = NP_ + NS
TH = T // 2
TQ = T // 4
NTT = NP_ // P
FF = 2816
KF = FF // P
EPS = 1e-6
PAST, PAGE = 2048, 128
NPG = PAST // PAGE
N_PHYS = 160
RH, RDK, RDV = 4, 128, 256
SH, SHD = 16, 64
CONV_W = 4
XBC = 10
MH, NOPE, ROPE, VD = 16, 64, 32, 64
QL, KVL = 512, 256
MLA_SCALE = (NOPE + ROPE) ** -0.5
NEG = -1e30

R = 4
CW = 4 * P

V_FFN1, V_MIX, V_FFN2 = (0, 24), (8, 32), (16, 40)
V_FINAL, V_CONVW, V_CONVB, V_DSKIP, V_HNORM, V_QNORM, V_KVNORM, V_DTB, V_ALOG, V_KEND = 48, 56, 96, 106, 114, 122, 126, 128, 144, 160
V_COLS = 176
NORM_COL = [V_FFN1[0], V_MIX[0], V_FFN2[0], V_FFN1[1], V_MIX[1], V_FFN2[1], V_FINAL]


class Shared:
    pass


class Plan:

    def __init__(self):
        self.n, self.turns = 0, [0, 0]
        self.set_of, self.turn_of = {}, {}
        self.first, self.count = {}, {}
        self.chunks = []
        self.order = []

    def step(self, name, chunks=0, unused=0):
        s = self.n % 2
        self.set_of[name], self.turn_of[name] = s, self.turns[s]
        self.turns[s] += 1
        self.n += 1
        self.first[name], self.count[name] = len(self.chunks), chunks + unused
        for c in range(chunks):
            self.chunks.append((name, c == chunks - 1, True))
        for c in range(unused):
            self.chunks.append((name, False, False))
        self.order.append(name)

    def used_through(self, n):
        return sum(1 for _, last, used in self.chunks[:n + 1] if used and not last)


def ffn_steps(plan, f):
    for g in range(KF):
        plan.step((f, "in", g), 4)
    for g in range(4):
        plan.step((f, "out", g), 11, 1)


def make_plan(phases):
    plan = Plan()
    for ph in phases:
        if ph in FFNS:
            ffn_steps(plan, ph)
        elif ph == "hyb":
            hyb_steps(plan)
        else:
            mla_steps(plan)
    plan.step("final stats")
    while len(plan.chunks) % R:
        plan.chunks.append(("pad", False, False))
    for _ in range(R):
        plan.chunks.append(("pad", False, False))
    return plan


STORES = {"hyb": 5, "mla": 2}
FFNS = ("a0", "b0", "a1", "b1")
PHASES = ("a0", "hyb", "b0", "a1", "mla", "b1")


HIN_REST = (12, 13, 16, 14, 17, 18, 21, 19, 20, 15)


def hyb_steps(plan):
    for g in range(8):
        plan.step(("hin", g), 4)
    plan.step("ret kT")
    plan.step("ret vT0")
    plan.step("ret vT1")
    plan.step(("ret S", 0))
    for h in range(RH):
        if h + 1 < RH:
            plan.step(("ret S", h + 1))
        plan.step(("ret O", h))
    plan.step("ret sT")
    for p in range(NS // 2):
        plan.step(("ret outer", p))
        plan.step(("hin", 8 + p), 4)
        plan.step(("ret y", p))
    plan.step(("ret norm", 0))
    plan.step(("ret norm", 1))
    for g in HIN_REST:
        if g == HIN_REST[-1]:
            plan.step("ssm dtT")
        plan.step(("hin", g), 4 if g < 21 else 2)
    plan.step("ssm xT0")
    plan.step("ssm xT1")
    plan.step("ssm BT")
    plan.step("ssm sums")
    plan.step("ssm dec")
    for c in range(NTT):
        plan.step(("ssm sc", c))
        if c:
            plan.step(("ssm y", c - 1))
        plan.step(("ssm D", c))
    plan.step("ssm sT")
    plan.step(("ssm y", NTT - 1))
    plan.step(("ssm outer", 0))
    plan.step(("ssm outer", 1))
    plan.step("ssm ys")
    plan.step("ssm yT")
    plan.step(("hout", 0), 8)
    plan.step("ssm norm")
    for g in range(1, 4):
        plan.step(("hout", g), 8)


def mla_steps(plan):
    plan.step(("min", 0), 4)
    plan.step(("min", 1), 4)
    plan.step(("min", 2), 4)
    plan.step(("min", 3), 2)
    plan.step("mla cnorm")
    for g in range(8):
        plan.step(("uq", g), 2)
    plan.step("smp qlat")
    for g in range(4):
        plan.step(("uk", g), 1)
    plan.step(("smp S", 0))
    for g in range(2):
        plan.step(("uv", g), 2)
    plan.step(("smp S", 1))
    plan.step(("att S", 0))
    for h in range(MH + 1):
        if h + 1 < MH:
            plan.step(("att S", h + 1))
        plan.step(("att TO", h))
    plan.step("smp T")
    plan.step("att OT0")
    plan.step("smp O")
    plan.step("att OT1")
    for g in range(4):
        plan.step(("wo", g), 4)


def program(nc, io, phases=PHASES):
    plan = make_plan(phases)
    NCH = len(plan.chunks)

    BASE = 16512
    cursor = [BASE]

    def at(name, shape, offset, dtype=F32):
        return nc.alloc_sbuf_tensor_at(name, shape, dtype, offset=offset)

    def sb(name, shape, dtype=F32):
        off = cursor[0]
        cursor[0] += (int(np.prod(shape[1:])) * 4 + 31) // 32 * 32
        return at(name, shape, off, dtype), off

    XT, _ = sb("residual", [P, KD, T])
    XH, XH_OFF = sb("x_high", [P, KD, T], F32R)
    XL, XL_OFF = sb("x_low", [P, KD, T], F32R)
    WRAW, _ = sb("w_raw", [P, R, CW])
    WH, WH_OFF = sb("w_high", [P, R, CW], F32R)
    WL, _ = sb("w_low", [P, R, CW], F32R)
    RSTD, _ = sb("rstd", [P, T])
    SQS, SQS_OFF = sb("square_sums", [P, 2, T])
    SQT, SQT_OFF = sb("squares", [P, 2, T])
    RCP = at("rcp", [P, T], SQT_OFF)
    VT, VT_OFF = sb("variance", [P, T])
    GU, GU_OFF = sb("gate_up", [P, 2, 2, T])
    SGT, SG_OFF = sb("silu_gate", [P, 2, T])
    HT, HT_OFF = sb("hidden", [P, 2, T])
    PV, _ = sb("vectors", [P, V_COLS])
    CON, _ = sb("constants", [P, 5, P])
    REGION = cursor[0]
    IDENT, ONES, UPTO, AFTER, NEGM = (CON[:, i, :] for i in range(5))
    HH = at("hidden_high", [P, KF, T], REGION, F32R)
    HL = at("hidden_low", [P, KF, T], REGION + KF * T * 4, F32R)

    PS = nc.alloc_psum_tensor("psum", [P, 8, 512], F32)

    stack = ExitStack()
    sem = lambda name: stack.enter_context(nc.semaphore(name))
    w_loaded = [sem(f"w_loaded{i}") for i in range(R)]
    w_high = sem("w_high_done")
    w_split = sem("w_split_done")
    w_used = sem("w_used")
    acc_full = [sem(f"acc_full{i}") for i in range(2)]
    acc_free = [sem(f"acc_free{i}") for i in range(2)]
    x_loaded = [sem(f"x_loaded{i}") for i in range(4)]
    v_loaded, c_loaded = sem("vectors_loaded"), sem("constants_loaded")
    squares_done, squares_added = sem("squares_done"), sem("squares_added")
    xh_done, xl_done = sem("x_high_done"), sem("x_low_done")
    stats_full = sem("norm_sums_full")
    rcp_done, rstd_done = sem("rcp_done"), sem("rstd_done")
    silu_done, hid_done = sem("silu_done"), sem("hidden_done")
    hh_done, hl_done = sem("hidden_high_done"), sem("hidden_low_done")
    dve_seq, act_seq, pool_seq = sem("dve_seq"), sem("act_seq"), sem("pool_seq")
    out_stored = sem("outputs_stored")
    y_done, y_stored = sem("y_done"), sem("y_stored")

    def bank0(step):
        return 4 * plan.set_of[step]

    def acc(step, banks=4):
        return PS[:, bank0(step):bank0(step) + banks, 0:TH]

    def halves(ap):
        return ap.rearrange("p (b t) -> p b t", b=2)

    def wait_full(eng, step, i=None):
        n = plan.turn_of[step] + 1
        eng.wait_ge(acc_full[plan.set_of[step]], n if i is None else n + i)

    def wait_free(eng, step, i=None):
        n = plan.turn_of[step] + 1
        eng.wait_ge(acc_free[plan.set_of[step]], n if i is None else n + i)

    def acquire(pe, step, i=None):
        n = plan.turn_of[step]
        if n:
            pe.wait_ge(acc_free[plan.set_of[step]], n if i is None else n + i)

    nn_of = {}
    for n, ph in enumerate(phases):
        nn_of[ph] = n
    NN = len(phases)
    norm_col = [NORM_COL[PHASES.index(ph)] for ph in phases] + [V_FINAL]

    ffn_index = {f: n for n, f in enumerate(ph for ph in phases if ph in FFNS)}

    def wait_stored(eng, f):
        n = nn_of[f]
        if n and phases[n - 1] in STORES:
            eng.wait_ge(out_stored, 16 * sum(STORES[ph] for ph in phases[:n] if ph in STORES))

    def slot_free(eng, n, i=None, used=0, split=0):
        if n < R:
            return
        step, last, real = plan.chunks[n - R]
        if not real:
            eng.wait_ge(w_split, n - R + 1 if i is None else split * i + (n - R + 1))
        elif last:
            wait_full(eng, step, i)
        else:
            k = plan.used_through(n - R)
            eng.wait_ge(w_used, k if i is None else used * i + k)

    def split_high(act, n, i=None, used=0, split=0, per_slot=0):
        slot = n % R
        k = 16 * (n // R + 1)
        act.wait_ge(w_loaded[slot], k if i is None else 16 * per_slot * i + k)
        slot_free(act, n, i, used, split)
        nc.scalar.activation(WH[:, slot, :], WRAW[:, slot, :], ACT.Copy).then_inc(w_high, 1)

    def split_low(dve, n, i=None, per=0):
        slot = n % R
        dve.wait_ge(w_high, n + 1 if i is None else per * i + (n + 1))
        nc.vector.tensor_tensor(WL[:, slot, :], WRAW[:, slot, :], WH[:, slot, :].bitcast(F32),
                                ALU.subtract).then_inc(w_split, 1)

    def gemm(pe, step, mtiles, ktiles, rhs, i=None, split=0, before_k=None, cols=TH):
        acquire(pe, step, i)
        first, b0 = plan.first[step], bank0(step)
        blocks = [(k, m) for k in range(ktiles) for m in range(mtiles)]
        for c in range((len(blocks) + 3) // 4):
            n = first + c
            slot = n % R
            for j, (k, m) in enumerate(blocks[4 * c:4 * c + 4]):
                if before_k and m == 0:
                    before_k(k)
                if j == 0:
                    pe.wait_ge(w_split, n + 1 if i is None else split * i + (n + 1))
                wh, wl = (w[:, slot, j * P:(j + 1) * P] for w in (WH, WL))
                xh, xl = rhs(k)
                for w, x, start, stop in ((wh, xh, k == 0, False), (wh, xl, False, False),
                                          (wl, xh, False, k == ktiles - 1)):
                    for half in range(2):
                        mm = nc.tensor.matmul(PS[:, b0 + 2 * m + half, 0:cols], w,
                                              x[:, half * cols:(half + 1) * cols], start=start, stop=stop)
            if 4 * c + 4 >= len(blocks):
                mm.then_inc(acc_full[plan.set_of[step]], 1)
            else:
                mm.then_inc(w_used, 1)

    def x_rhs(k):
        return XH[:, k, :], XL[:, k, :]

    def pe_stats(pe, step, nn):
        pe.wait_ge(squares_added, 4 * (nn + 1))
        b0 = bank0(step)
        for q in range(4):
            for j in range(2):
                mm = nc.tensor.matmul(PS[:, b0 + q, TH:TH + TQ], ONES, SQS[:, j, q * TQ:(q + 1) * TQ],
                                      start=j == 0, stop=j == 1)
        mm.then_inc(stats_full, 1)

    def first_wait(pe, nn):
        return lambda k: pe.wait_ge(xl_done, KD * nn + k + 1)

    e = Shared()
    e.AFTER, e.GU, e.GU_OFF, e.IDENT, e.NEGM, e.ONES = AFTER, GU, GU_OFF, IDENT, NEGM, ONES
    e.PS, e.PV, e.REGION, e.RSTD, e.SQS_OFF = PS, PV, REGION, RSTD, SQS_OFF
    e.SQT_OFF, e.UPTO, e.VT_OFF, e.WH, e.WH_OFF, e.WL = SQT_OFF, UPTO, VT_OFF, WH, WH_OFF, WL
    e.XH, e.XH_OFF, e.XL, e.acc, e.acc_free = XH, XH_OFF, XL, acc, acc_free
    e.acc_full, e.acquire, e.at, e.bank0, e.first_wait = acc_full, acquire, at, bank0, first_wait
    e.gemm, e.halves, e.io, e.nc, e.nn_of = gemm, halves, io, nc, nn_of
    e.out_stored, e.pe_stats, e.phases, e.plan, e.sem = out_stored, pe_stats, phases, plan, sem
    e.w_split, e.w_used, e.wait_free, e.wait_full, e.x_rhs = w_split, w_used, wait_free, wait_full, x_rhs
    hy = hyb_parts(e) if "hyb" in phases else None
    ml = mla_parts(e) if "mla" in phases else None

    block = stack.enter_context(nc.Block())

    @block.sync
    def _(sp):
        def chunk(n):
            if n >= R:
                sp.wait_ge(w_split, n + 1 - R)
            sp.dma_start(WRAW[:, n % R, :], io["weights"][n]).then_inc(w_loaded[n % R], 16)

        def weight_chunks(n0, n1):
            n0, n1 = max(n0, R), NCH if n1 is None else n1
            while n0 < n1 and (n0 < R or n0 % R):
                chunk(n0)
                n0 += 1
            if n1 // R - n0 // R > 1:
                with sp.Fori(n0 // R, n1 // R) as i:
                    for s in range(R):
                        sp.wait_ge(w_split, R * i + (s + 1 - R))
                        sp.dma_start(WRAW[:, s, :], io["weights"][bass.ds(R * i + s, 1)]
                                     .rearrange("a p n -> (a p) n")).then_inc(w_loaded[s], 16)
                n0 = n1 // R * R
            for n in range(n0, n1):
                chunk(n)

        for pair in range(4):
            tiles = slice(2 * pair, 2 * pair + 2)
            sp.dma_start(XT[:, tiles, :], io["x"][:, tiles, :]).then_inc(x_loaded[pair], 16)
            chunk(pair)
        if ml:
            ml.sp(sp, weight_chunks)
        else:
            weight_chunks(0, None)
        for t in range(KD):
            sp.wait_ge(y_done, t + 1)
            sp.dma_start(io["y"][:, t, :], XT[:, t, :]).then_inc(y_stored, 16)
        for s in range(R):
            sp.wait_ge(w_loaded[s], 16 * (NCH // R))
        sp.wait_ge(y_stored, 16 * KD)

    @block.tensor
    def _(pe):
        def ffn(f):
            nn = nn_of[f]
            gemm(pe, (f, "in", 0), 2, KD, x_rhs, before_k=first_wait(pe, nn))
            pe_stats(pe, (f, "in", 0), nn)
            gemm(pe, (f, "in", 1), 2, KD, x_rhs)
            with pe.Fori(0, (KF - 2) // 2) as i:
                for g in (2, 3):
                    gemm(pe, (f, "in", g), 2, KD, x_rhs, i, 8)
            done = KF * (ffn_index[f] + 1)
            h_rhs = lambda k: (HH[:, k, :], HL[:, k, :])
            for g in (0, 1):
                gemm(pe, (f, "out", g), 2, KF, h_rhs,
                     before_k=(lambda k: pe.wait_ge(hl_done, done - KF + k + 1)) if g == 0 else None)
            for g in (2, 3):
                gemm(pe, (f, "out", g), 2, KF, h_rhs)

        pe.wait_ge(c_loaded, 16)
        for ph in phases:
            if ph in FFNS:
                ffn(ph)
            elif ph == "hyb":
                hy.pe(pe)
            else:
                ml.pe(pe)
        acquire(pe, "final stats")
        pe_stats(pe, "final stats", NN)

    @block.scalar
    def _(act):
        ahead = [0]

        def splits(k):
            for _ in range(k):
                split_high(act, ahead[0])
                ahead[0] += 1

        def squares(nn, pair):
            q = 4 * nn + pair
            if q:
                act.wait_ge(squares_added, q)
            if nn and pair == 0:
                act.wait_ge(rstd_done, nn)
            nc.scalar.activation(SQT[:], XT[:, 2 * pair:2 * pair + 2, :], ACT.Square).then_inc(squares_done, 1)

        def highs(nn, pair):
            for m in range(2):
                t = 2 * pair + m
                nc.scalar.activation(XH[:, t, :], XT[:, t, :], ACT.Copy,
                                     scale=PV[:, norm_col[nn] + t:norm_col[nn] + t + 1]).then_inc(xh_done, 1)

        def stats(nn):
            act.wait_ge(rcp_done, nn + 1)
            nc.scalar.activation(RSTD[:], RCP[:], ACT.Sqrt).then_inc(rstd_done, 1)

        def silu(f, g, i=None):
            wait_free(act, (f, "in", g), i)
            nc.scalar.activation(SGT[:, g % 2, :], GU[:, g % 2, 0, :], ACT.Silu).then_inc(silu_done, 1)

        def hidden_high(f, g, i=None):
            n = KF * ffn_index[f] + g + 1
            act.wait_ge(hid_done, n if i is None else 2 * i + n)
            out = HH[:, g, :] if i is None else HH[:, bass.ds(2 * i + g, 1), :]
            src = HT[:, g % 2, :] if i is None else HT[:, g % 2:g % 2 + 1, :]
            nc.scalar.activation(out, src, ACT.Copy).then_inc(hh_done, 1)

        def ffn(f):
            nn = nn_of[f]
            for g in (0, 1):
                splits(2 if g else 4)
                if g == 0:
                    stats(nn)
                silu(f, g)
                if g:
                    splits(1)
                else:
                    wait_stored(act, f)
                hidden_high(f, g)
                if g:
                    splits(1)
            base = ahead[0]
            with act.Fori(0, (KF - 2) // 2) as i:
                for g in (2, 3):
                    n = base + 4 * (g - 2)
                    go = lambda m: split_high(act, m, i, 6, 8, 2)
                    go(n)
                    go(n + 1)
                    silu(f, g, i)
                    go(n + 2)
                    hidden_high(f, g, i)
                    go(n + 3)
            ahead[0] += 4 * (KF - 2)
            for g in range(4):
                splits(10)
                wait_free(act, (f, "out", g))
                squares(nn + 1, g)
                splits(1)
                highs(nn + 1, g)
                splits(1)

        act.dma_start(PV[:], io["vectors"]).then_inc(v_loaded, 16)
        act.wait_ge(v_loaded, 16)
        for pair in range(4):
            act.wait_ge(x_loaded[pair], 16)
            highs(0, pair)
            splits(R // 4)
            squares(0, pair)
        env = Shared()
        env.splits, env.squares, env.highs, env.stats = splits, squares, highs, stats
        for ph in phases:
            if ph in FFNS:
                ffn(ph)
            elif ph == "hyb":
                hy.act(act, env)
            else:
                ml.act(act, env)
        stats(NN)

    @block.vector
    def _(dve):
        ahead = [0]
        seq = [0]

        def splits(k):
            for _ in range(k):
                split_low(dve, ahead[0])
                ahead[0] += 1

        def link(ins):
            seq[0] += 1
            ins.then_inc(dve_seq, 1)
            dve.wait_ge(dve_seq, seq[0])

        def lows(nn, pair):
            for m in range(2):
                t = 2 * pair + m
                dve.wait_ge(xh_done, KD * nn + t + 1)
                nc.vector.scalar_tensor_tensor(XL[:, t, :], XT[:, t, :],
                                               PV[:, norm_col[nn] + t:norm_col[nn] + t + 1],
                                               XH[:, t, :].bitcast(F32), ALU.mult,
                                               ALU.subtract).then_inc(xl_done, 1)

        def stats(step, nn):
            dve.wait_ge(stats_full, nn + 1)
            b0 = bank0(step)
            link(nc.vector.tensor_scalar(VT[:].rearrange("p (q t) -> p q t", q=4), PS[:, b0:b0 + 4, TH:TH + TQ],
                                         1.0 / D, EPS, ALU.mult, ALU.add))
            nc.vector.reciprocal(RCP[:], VT[:]).then_inc(rcp_done, 1)
            dve.wait_ge(rstd_done, nn + 1)

        def rstd4():
            return halves(RSTD[:]).unsqueeze(1).broadcast_to([P, 2, 2, TH])

        def gate_up(f, g, i=None):
            step = (f, "in", g)
            wait_full(dve, step, i)
            out = GU[:, g % 2].rearrange("p m (b t) -> p (m b) t", b=2)
            for m in range(2):
                ins = nc.vector.tensor_tensor(out[:, 2 * m:2 * m + 2, :], acc(step)[:, 2 * m:2 * m + 2, :],
                                              halves(RSTD[:]), ALU.mult)
            ins.then_inc(acc_free[plan.set_of[step]], 1)

        def product(f, g, i=None):
            n = KF * ffn_index[f] + g + 1
            dve.wait_ge(silu_done, n if i is None else 2 * i + n)
            nc.vector.tensor_tensor(HT[:, g % 2, :], SGT[:, g % 2, :], GU[:, g % 2, 1, :],
                                    ALU.mult).then_inc(hid_done, 1)

        def hidden_low(f, g, i=None):
            n = KF * ffn_index[f] + g + 1
            dve.wait_ge(hh_done, n if i is None else 2 * i + n)
            if i is None:
                out, hi, src = HL[:, g, :], HH[:, g, :], HT[:, g % 2, :]
            else:
                tile = bass.ds(2 * i + g, 1)
                out, hi, src = HL[:, tile, :], HH[:, tile, :], HT[:, g % 2:g % 2 + 1, :]
            nc.vector.tensor_tensor(out, src, hi.bitcast(F32), ALU.subtract).then_inc(hl_done, 1)

        def residual(step, pair, scale):
            wait_full(dve, step)
            x = XT[:, 2 * pair:2 * pair + 2, :].rearrange("p m (b t) -> p (m b) t", b=2)
            nc.vector.scalar_tensor_tensor(x, acc(step), scale, x, ALU.mult,
                                           ALU.add).then_inc(acc_free[plan.set_of[step]], 1)

        def ffn(f):
            nn = nn_of[f]
            for g in (0, 1):
                splits(2 if g else 4)
                if g == 0:
                    stats((f, "in", 0), nn)
                gate_up(f, g)
                if g:
                    splits(1)
                product(f, g)
                if g:
                    splits(1)
                else:
                    wait_stored(dve, f)
                hidden_low(f, g)
            base = ahead[0]
            with dve.Fori(0, (KF - 2) // 2) as i:
                for g in (2, 3):
                    n = base + 4 * (g - 2)
                    split_low(dve, n, i, 8)
                    split_low(dve, n + 1, i, 8)
                    gate_up(f, g, i)
                    split_low(dve, n + 2, i, 8)
                    product(f, g, i)
                    split_low(dve, n + 3, i, 8)
                    hidden_low(f, g, i)
            ahead[0] += 4 * (KF - 2)
            for g in range(4):
                splits(10)
                residual((f, "out", g), g, 0.5)
                splits(1)
                splits(1)
                lows(nn + 1, g)

        dve.wait_ge(v_loaded, 16)
        for pair in range(4):
            dve.wait_ge(x_loaded[pair], 16)
            lows(0, pair)
            splits(R // 4)
        env = Shared()
        env.splits, env.lows, env.stats, env.residual, env.link, env.seq = splits, lows, stats, residual, link, seq
        for ph in phases:
            if ph in FFNS:
                ffn(ph)
            elif ph == "hyb":
                hy.dve(dve, env)
            else:
                ml.dve(dve, env)
        stats("final stats", NN)
        for t in range(KD):
            nc.vector.scalar_tensor_tensor(XT[:, t, :], XT[:, t, :], PV[:, V_FINAL + t:V_FINAL + t + 1],
                                           RSTD[:], ALU.mult, ALU.mult).then_inc(y_done, 1)

    @block.gpsimd
    def _(pool):
        pool.dma_start(CON[:], io["constants"]).then_inc(c_loaded, 16)

        def norm_sums(nn):
            for pair in range(4):
                q = 4 * nn + pair
                if pair == 0:
                    pool.wait_ge(squares_done, q + 1)
                    nc.gpsimd.tensor_copy(SQS[:], SQT[:]).then_inc(squares_added, 1)
                else:
                    pool.wait_ge(squares_done, q + 1)
                    pool.wait_ge(squares_added, q)
                    nc.gpsimd.tensor_tensor(SQS[:], SQS[:], SQT[:], ALU.add).then_inc(squares_added, 1)

        norm_sums(0)
        stores = [0]
        env = Shared()
        env.norm_sums, env.stores = norm_sums, stores
        for ph in phases:
            if ph in FFNS:
                norm_sums(nn_of[ph] + 1)
            elif ph == "hyb":
                hy.pool(pool, env)
            else:
                ml.pool(pool, env)

    stack.close()


def ffn_chunks(w_in, w_out):
    a = w_in.reshape(4, 2, P, 2, KF, P).transpose(4, 0, 2, 1, 3, 5).reshape(-1, P, CW)
    b = w_out.reshape(11, 2, P, 4, 2, P).transpose(3, 0, 2, 1, 4, 5).reshape(4, 11, P, CW)
    b = np.concatenate([b, np.zeros((4, 1, P, CW), b.dtype)], 1).reshape(-1, P, CW)
    return [a, b]


def pairs(w):
    k, n = w.shape
    return w.reshape(k // 256, 2, P, n // 256, 2, P).transpose(3, 0, 2, 1, 4, 5).reshape(-1, P, CW)


def single(w):
    k = w.shape[0]
    return w.reshape(k // 512, 4, P, P).transpose(0, 2, 1, 3).reshape(-1, P, CW)


def columns(v):
    return v.reshape(-1, P).T


def lay_out(q, phases=PHASES):
    a = {k: np.asarray(v) for k, v in q.items()}
    f = np.float32
    w = []
    for ph in phases:
        if ph in FFNS:
            l, which = int(ph[1]), {"a": 1, "b": 2}[ph[0]]
            w += ffn_chunks(a[f"ffn{which}_w_in"][l], a[f"ffn{which}_w_out"][l])
        elif ph == "hyb":
            wi = a["hyb_w_in"][0]
            groups = pairs(wi[:, :5376]).reshape(21, 4, P, CW)
            groups = list(groups) + [single(np.concatenate([wi[:, 5376:], np.zeros((D, P - SH), f)], 1))]
            w += [groups[g] for g in list(range(12)) + list(HIN_REST)] + [
                  pairs(a["hyb_w_out"][0])]
        else:
            wi = a["mla_w_in"][0]
            kr = wi[:, 768:]
            kr = np.concatenate([np.zeros((D, 64), f), kr, kr[:, 16:], kr[:, :16]], 1)
            uq = a["mla_w_uq"][0].reshape(QL, MH, NOPE + ROPE)
            uq = np.concatenate([uq, uq[:, :, 80:], uq[:, :, 64:80]], 2).reshape(QL, MH * P)
            uv = a["mla_w_uv"][0].reshape(2, P, 2, CW).transpose(2, 0, 1, 3).reshape(-1, P, CW)
            w += [pairs(wi[:, :768]), single(kr), pairs(uq), pairs(a["mla_w_uk"][0].reshape(KVL, D)), uv,
                  pairs(a["mla_w_o"][0])]
    n = sum(len(x) for x in w)
    w.append(np.zeros(((-n) % R + R, P, CW), f))
    x = np.concatenate([a["x_prompt"][0], a["x_sample"][:, 0]], 0)
    rows = lambda v: np.broadcast_to(v, (P, SH))
    jj = np.arange(P)
    gamma = np.log1p(-np.exp2(-5.0 - np.arange(RH)))
    kend = np.stack([np.exp(gamma[h] * (NP_ - 1 - P * jt - jj)) for h in range(RH) for jt in range(NTT)], 1)
    vec = [a["norm_ffn1"][0], a["norm_mix"][0], a["norm_ffn2"][0], a["norm_ffn1"][1], a["norm_mix"][1],
           a["norm_ffn2"][1], a["final_norm_w"], a["hyb_conv_w"][0].reshape(-1), a["hyb_conv_b"][0],
           np.repeat(a["hyb_d_skip"][0], SHD), a["hyb_norm_w"][0], a["mla_q_norm_w"][0], a["mla_kv_norm_w"][0]]
    vectors = np.concatenate([columns(v) for v in vec] + [rows(a["hyb_dt_bias"][0]), rows(a["hyb_a_log"][0]),
                                                          kend.astype(f)], 1)
    i = np.arange(P)
    constants = np.stack([np.eye(P), np.ones((P, P)), i[:, None] <= i[None], i[:, None] > i[None],
                          np.where(i[None] <= i[:, None], 0.0, NEG)], 1).astype(f)
    tile = lambda m: np.ascontiguousarray(m.reshape(-1, P, m.shape[-1]).transpose(1, 0, 2))
    out = {"weights": np.concatenate(w, 0), "x": tile(x.T), "vectors": vectors, "constants": constants}
    if "hyb" in phases:
        out.update(lay_out_hyb(a, tile, gamma))
    if "mla" in phases:
        out.update(lay_out_mla(a, tile))
    return {k: np.ascontiguousarray(v) for k, v in out.items()}


def outputs(phases=PHASES):
    out = {"y": (P, KD, T)}
    if "hyb" in phases:
        out.update(OUT_HYB)
    if "mla" in phases:
        out.update(OUT_MLA)
    return out




def hyb_parts(e):
    nc, io, plan, at, sem, PS = e.nc, e.io, e.plan, e.at, e.sem, e.PS
    REGION, GU_OFF = e.REGION, e.GU_OFF
    IDENT, ONES, UPTO, AFTER, PV, RSTD = e.IDENT, e.ONES, e.UPTO, e.AFTER, e.PV, e.RSTD
    acc, bank0, halves = e.acc, e.bank0, e.halves
    wait_full, wait_free, acquire = e.wait_full, e.wait_free, e.acquire
    full = lambda step: e.acc_full[plan.set_of[step]]
    free = lambda step: e.acc_free[plan.set_of[step]]
    nn = e.nn_of["hyb"]
    before = e.phases[nn - 1] if nn else None

    M1H = at("ret_out_high", [P, 8, T], REGION, F32R)
    M1L = at("ret_out_low", [P, 8, T], REGION + 16640, F32R)
    VTF = at("v_features", [P, 8, T], REGION)
    OB = at("ret_out", [P, 8, T], REGION + 16640)
    QT = at("q_features", [P, 4, T], REGION + 33280)
    KT = at("k_features", [P, 4, T], REGION + 41600)
    VTOK = at("v_tokens", [P, NTT, 1024], REGION + 49920)
    KM = at("k_samples_masked", [NS, NS, 512], REGION + 49920)
    GS = at("silu_g", [P, 8, T], REGION + 66304)
    KTOK = at("k_tokens", [P, RH * NTT, P], REGION + 82944)
    SEG = at("decays", [P, RH, NP_], REGION + 91136)
    S0 = [at("sample_state0", [P, 2, RH, RDV], REGION + 91136), at("sample_state1", [P, 2, RH, RDV], REGION + 82944)]
    CT = at("rope_cos", [P, T], REGION + 99328)
    SN = at("rope_sin", [P, T], REGION + 101408)
    RST = at("ret_state", [P, RH, RDV], REGION + 99328)
    ST = [at("ret_scores0", [P, 1280], GU_OFF), at("ret_scores1", [P, 1280], GU_OFF + 8320)]
    VS = at("v_samples", [NS, 1024], GU_OFF)
    SQB = at("ret_squares", [P, 8, T], GU_OFF)
    ROT = at("rotated", [P, 2, T], GU_OFF + 12480)
    ZS = at("silu_z", [P, 8, T], REGION + 33280)
    XS = at("ssm_x", [P, 8, T], REGION + 49920)
    BC = at("ssm_bc", [P, 2, T], REGION + 66560)
    XTOK = at("ssm_x_tokens", [P, NTT, 1024], REGION + 70720)
    SSS = at("ssm_sample_state", [P, NS, 512], REGION + 70720)
    BTOK = at("ssm_b_tokens", [P, NTT, P], REGION + 87104)
    EM = at("ssm_weights", [P, SH, P], REGION + 89152)
    CS = at("ssm_c_decayed", [P, 8, P], REGION + 97344)
    DTR = at("dt_features", [SH, T], REGION + 97344)
    XDS = at("ssm_x_samples", [NS, 1024], REGION + 97344)
    SST = at("ssm_state", [P, 512], REGION + 101440)
    CBE = at("ssm_c_decay", [P, 1024], GU_OFF)
    BM = at("ssm_b_masked", [NS, NS, P], GU_OFF)
    XEND = at("ssm_x_end", [P, 1024], GU_OFF + 4096)
    LM = at("ssm_masked_log", [P, SH, P], GU_OFF + 8448)
    LAW = at("ssm_log_wide", [P, 8, 2, 64], e.SQS_OFF)
    SM = at("ssm_scores", [P, 2, P], e.VT_OFF)
    DECX = at("ssm_decay_masked", [NS, NS, SH], e.VT_OFF + 1024)
    YB = at("ssm_y_samples", [2 * NS, 512], GU_OFF + 4096)
    CM = at("ssm_c_masked", [P, NS, 2 * NS], GU_OFF + 6144)
    V2 = at("ssm_variance", [P, 2, T], REGION + 89152)
    RT2 = at("ssm_rstd", [P, 2, T], REGION + 89152 + 4160)
    CR = at("conv_in", [P, 4, 524], GU_OFF)
    CACC = at("conv_sum", [P, 2, T], GU_OFF + 8448)
    SCI = at("conv_state", [P, XBC, 3, NS], GU_OFF + 12608)
    CSO = at("conv_sample_out", [P, XBC, 3, NS], GU_OFF + 13568)
    CPO = at("conv_prompt_out", [P, XBC, 3], GU_OFF + 14528)
    small = [at(f"dt_work{i}", [P, 5, SH], e.SQT_OFF + 320 * i) for i in range(9)]
    DX, DP, DE, DS_, DS2, DH, DT, LA, DA = small
    DEX = at("ssm_decays", [P, 2, 64], e.SQT_OFF + 2880)
    DECB = at("ssm_sample_decay", [P, 64], e.SQT_OFF + 3392)
    soff = [0, 512, 896, 1152]

    loaded = sem("hyb_tables_loaded")
    conv_loaded = sem("conv_state_loaded")
    rot_done, gs_done = sem("rotated_done"), sem("silu_gz_done")
    s0_loaded = [sem("ret_state_loaded0"), sem("ret_state_loaded1")]
    s0_stored = [sem("ret_state_stored0"), sem("ret_state_stored1")]
    sss_loaded = sem("ssm_state_loaded")
    sq_done, v2_done, rt_done = sem("ret_squares_done"), sem("ret_rcp_done"), sem("ret_rstd_done")
    o_done, m1h_done, m1l_done = sem("ret_gated_done"), sem("ret_high_done"), sem("ret_low_done")
    conv_done, convs_done = sem("conv_sum_done"), sem("conv_silu_done")
    dt_abs, dt_exp, dt_done = sem("dt_abs_done"), sem("dt_exp_done"), sem("dt_done")
    law_done, cbe_done, l_done, m_done, xend_done = sem("log_wide_done"), sem("c_decay_done"), sem("masked_log_done"), sem("weights_done"), sem("x_end_done")
    yg_done, ysq_done, yv_done, yr_done = sem("y_gated_done"), sem("y_squares_done"), sem("y_rcp_done"), sem("y_rstd_done")
    yn_done, yh_done, yl_done = sem("y_normed_done"), sem("y_high_done"), sem("y_low_done")
    out_ready = sem("hyb_out_ready")
    dx_done = sem("sample_decays_masked")
    em_done = sem("weights_exp_done")
    vs_done, km_done = sem("v_samples_done"), sem("k_masked_done")
    tap_done = sem("conv_first_tap_done")


    def pe(pe):

        def transposes(step, items, waits):
            acquire(pe, step)
            for w in waits:
                w()
            for out, src in items:
                k = src.shape[0]
                mm = nc.tensor.transpose(out, src, IDENT[0:k, 0:k])
            mm.then_inc(full(step), 1)

        def hin(g, **kw):
            e.gemm(pe, ("hin", g), 2 if g < 21 else 1, KD, e.x_rhs, **kw)

        hin(0, before_k=e.first_wait(pe, nn))
        e.pe_stats(pe, ("hin", 0), nn)
        for g in range(1, 8):
            hin(g)
        b = bank0("ret kT")
        transposes("ret kT", [(PS[:, b + h, jt * P:(jt + 1) * P], KT[:, h, jt * P:(jt + 1) * P])
                              for h in range(RH) for jt in range(NTT)],
                   [lambda: pe.wait_ge(rot_done, 8)])
        for v in range(2):
            b = bank0(f"ret vT{v}")
            transposes(f"ret vT{v}", [(PS[:, b + t, jt * P:(jt + 1) * P], VTF[:, 4 * v + t, jt * P:(jt + 1) * P])
                                      for t in range(4) for jt in range(NTT)],
                       [lambda: wait_free(pe, ("hin", 7))])

        def ret_scores(h):
            step = ("ret S", h)
            acquire(pe, step)
            b = bank0(step)
            for jt in range(NTT):
                mm = nc.tensor.matmul(PS[:, b + jt, 0:NP_ - jt * P], KT[:, h, jt * P:(jt + 1) * P],
                                      QT[:, h, jt * P:NP_], start=True, stop=True)
            mm.then_inc(full(step), 1)

        ret_scores(0)
        for h in range(RH):
            if h + 1 < RH:
                ret_scores(h + 1)
            step2 = ("ret O", h)
            acquire(pe, step2)
            wait_free(pe, ("ret S", h))
            if h == 0:
                wait_free(pe, "ret vT1")
                wait_free(pe, "ret kT")
            b = bank0(step2)
            for m in range(2):
                for jt in range(NTT):
                    n = NP_ - jt * P
                    nc.tensor.matmul(PS[:, b + m, jt * P:NP_],
                                     VTOK[:, jt, h * RDV + m * P:h * RDV + (m + 1) * P],
                                     ST[h % 2][:, soff[jt]:soff[jt] + n], start=jt == 0, stop=jt == NTT - 1)
            for jt in range(NTT):
                mm = nc.tensor.matmul(PS[:, b + 2, 0:RDV], KTOK[:, h * NTT + jt, :],
                                      VTOK[:, jt, h * RDV:(h + 1) * RDV], start=jt == 0, stop=jt == NTT - 1)
            mm.then_inc(full(step2), 1)
        b = bank0("ret sT")
        transposes("ret sT", [(PS[0:NS, b, h * P:(h + 1) * P], KT[:, h, NP_:T]) for h in range(RH)] +
                   [(PS[0:NS, b + 1 + t // 4, (t % 4) * P:(t % 4 + 1) * P], VTF[:, t, NP_:T]) for t in range(8)], [])
        for p in range(NS // 2):
            step = ("ret outer", p)
            acquire(pe, step)
            pe.wait_ge(vs_done, 1)
            if p < NS // 2 - 1:
                pe.wait_ge(km_done, p + 1)
            else:
                wait_free(pe, "ret sT")
            b = bank0(step)
            for j in range(2):
                for h in range(RH):
                    mm = nc.tensor.matmul(PS[:, b + 2 * j + h // 2, (h % 2) * RDV:(h % 2 + 1) * RDV],
                                          KM[:, 2 * p + j, h * P:(h + 1) * P], VS[:, h * RDV:(h + 1) * RDV],
                                          start=True, stop=True)
            mm.then_inc(full(step), 1)
            hin(8 + p)
            step2 = ("ret y", p)
            acquire(pe, step2)
            wait_free(pe, step)
            b = bank0(step2)
            for j in range(2):
                for t in range(8):
                    h = t // 2
                    mm = nc.tensor.matmul(PS[:, b, j * 8 + t:j * 8 + t + 1],
                                          S0[p % 2][:, j, h, (t % 2) * P:(t % 2 + 1) * P],
                                          QT[:, h, NP_ + 2 * p + j:NP_ + 2 * p + j + 1], start=True, stop=True)
            mm.then_inc(full(step2), 1)
        for n in range(2):
            step = ("ret norm", n)
            acquire(pe, step)
            pe.wait_ge(sq_done, n + 1)
            b = bank0(step)
            for hh in range(2):
                for half in range(2):
                    for m in range(2):
                        mm = nc.tensor.matmul(PS[:, b + 2 * hh + half, 0:TH], ONES,
                                              SQB[:, 4 * n + 2 * hh + m, half * TH:(half + 1) * TH],
                                              start=m == 0, stop=m == 1)
            mm.then_inc(full(step), 1)
        for g in HIN_REST:
            if g == HIN_REST[-1]:
                b = bank0("ssm dtT")
                transposes("ssm dtT", [(PS[:, b, c * SH:(c + 1) * SH], DTR[:, c * P:(c + 1) * P]) for c in range(NTT)] +
                           [(PS[0:NS, b, 64:80], DTR[:, NP_:T])], [lambda: wait_free(pe, ("hin", 21))])
            hin(g)
        for v in range(2):
            b = bank0(f"ssm xT{v}")
            transposes(f"ssm xT{v}", [(PS[:, b + t, jt * P:(jt + 1) * P], XS[:, 4 * v + t, jt * P:(jt + 1) * P])
                                      for t in range(4) for jt in range(NTT)],
                       [lambda: pe.wait_ge(convs_done, 4 * v + 4)])
        b = bank0("ssm BT")
        transposes("ssm BT", [(PS[:, b, c * P:(c + 1) * P], BC[:, 0, c * P:(c + 1) * P]) for c in range(NTT)],
                   [lambda: pe.wait_ge(convs_done, XBC)])
        step = "ssm sums"
        acquire(pe, step)
        pe.wait_ge(dt_done, 1)
        b = bank0(step)
        la = LA[:, 0:NTT, :].rearrange("p c h -> p (c h)")
        nc.tensor.matmul(PS[:, b, 0:64], AFTER, la, start=True, stop=True)
        nc.tensor.matmul(PS[:, b, 64:128], ONES, la, start=True, stop=True).then_inc(full(step), 1)

        step = "ssm dec"
        acquire(pe, step)
        pe.wait_ge(dx_done, 1)
        b = bank0(step)
        for g in range(2):
            mm = nc.tensor.matmul(PS[64 * g:64 * g + 64, b, 0:64].rearrange("p (b h) -> p b h", b=8),
                                  ONES[0:NS, 0:64], DECX[:, :, 8 * g:8 * g + 8], start=True, stop=True)
        mm.then_inc(full(step), 1)

        def ssm_scores(c):
            tok = slice(c * P, (c + 1) * P)
            step = ("ssm sc", c)
            acquire(pe, step)
            b = bank0(step)
            for g in range(2):
                rows = slice(64 * g, 64 * g + 64)
                nc.tensor.matmul(PS[:, b + g, 0:P], BC[rows, 0, tok], BC[rows, 1, tok], start=True, stop=True)
            pe.wait_ge(law_done, c + 1)
            for h8 in range(8):
                mm = nc.tensor.matmul(PS[:, b + 2 + h8 // 4, (h8 % 4) * P:(h8 % 4 + 1) * P], LAW[:, h8].rearrange("p g s -> p (g s)"),
                                      UPTO, start=True, stop=True)
            mm.then_inc(full(step), 1)

        def ssm_decays(c):
            step = ("ssm D", c)
            acquire(pe, step)
            pe.wait_ge(l_done, c + 1)
            b = bank0(step)
            for h in range(SH):
                mm = nc.tensor.matmul(PS[:, b + h // 4, (h % 4) * P:(h % 4 + 1) * P], LM[:, h, :], UPTO,
                                      start=True, stop=True)
            mm.then_inc(full(step), 1)

        def ssm_values(c):
            step = ("ssm y", c)
            acquire(pe, step)
            pe.wait_ge(xend_done, c + 1)
            b = bank0(step)
            for g in range(2):
                mm = nc.tensor.matmul(PS[64 * g:64 * g + 64, b + 2, :], BTOK[:, c, 64 * g:64 * g + 64],
                                      XEND[:, g * 512:(g + 1) * 512], start=True, stop=True)
            wait_free(pe, ("ssm sc", c))
            for h in range(SH):
                g, t = h // 8, h // 2
                if h % 8 == 0:
                    pe.wait_ge(m_done, 2 * c + g + 1)
                out = PS[64 * (h % 2):64 * (h % 2) + 64, b + g, (t % 4) * P:(t % 4 + 1) * P]
                mm = nc.tensor.matmul(out, XTOK[:, c, h * SHD:(h + 1) * SHD], EM[:, h, :], start=True, stop=c == 0)
                if c:
                    rows = slice(64 * g, 64 * g + 64)
                    mm = nc.tensor.matmul(out, SST[rows, (h % 8) * SHD:(h % 8 + 1) * SHD], CS[rows, h % 8, :],
                                          start=False, stop=True)
            mm.then_inc(full(step), 1)

        for c in range(NTT):
            ssm_scores(c)
            if c:
                ssm_values(c - 1)
            ssm_decays(c)
        b = bank0("ssm sT")
        transposes("ssm sT", [(PS[0:NS, b + t // 4, (t % 4) * P:(t % 4 + 1) * P], XS[:, t, NP_:T]) for t in range(8)] +
                   [(PS[0:NS, b + 2, 0:P], BC[:, 0, NP_:T])], [])
        ssm_values(NTT - 1)
        for k in range(2):
            step = ("ssm outer", k)
            acquire(pe, step)
            if k == 0:
                wait_free(pe, "ssm sT")
            b = bank0(step)
            for j in range(4):
                for g in range(2):
                    mm = nc.tensor.matmul(PS[64 * g:64 * g + 64, b + j, :], BM[:, 4 * k + j, 64 * g:64 * g + 64],
                                          XDS[:, g * 512:(g + 1) * 512], start=True, stop=True)
            mm.then_inc(full(step), 1)
        step = "ssm ys"
        acquire(pe, step)
        wait_free(pe, ("ssm outer", 1))
        b = bank0(step)
        for k in range(NS):
            mm = nc.tensor.matmul(PS[0:2 * NS, b, :], CM[:, k, :], SSS[:, k, :], start=k == 0, stop=k == NS - 1)
        mm.then_inc(full(step), 1)
        b = bank0("ssm yT")
        transposes("ssm yT", [(PS[:, b, 2 * NS * t:2 * NS * (t + 1)], YB[:, t * P:(t + 1) * P]) for t in range(4)],
                   [lambda: wait_free(pe, "ssm ys")])
        def ssm_norm():
            step = "ssm norm"
            acquire(pe, step)
            pe.wait_ge(ysq_done, 1)
            b = bank0(step)
            for g in range(2):
                for half in range(2):
                    for t in range(4):
                        mm = nc.tensor.matmul(PS[:, b + 2 * g + half, 0:TH], ONES,
                                              SQB[:, 4 * g + t, half * TH:(half + 1) * TH], start=t == 0, stop=t == 3)
            mm.then_inc(full(step), 1)

        def mixed(k):
            return (M1H[:, k, :], M1L[:, k, :]) if k < 8 else (e.XH[:, k - 8, :], e.XL[:, k - 8, :])

        def ready(k):
            if k == 0:
                pe.wait_ge(m1l_done, 2)
            if k == 8:
                ssm_norm()
            if k >= 8:
                pe.wait_ge(yl_done, k - 7)

        for g in range(4):
            e.gemm(pe, ("hout", g), 2, 16, mixed, before_k=ready if g == 0 else None)

    def act(act, a):
        def silu_pair(step, x):
            wait_free(act, step)
            nc.scalar.activation(x, x, ACT.Silu).then_inc(gs_done, 1)

        a.splits(4)
        a.stats(nn)
        for g in range(1, 8):
            a.splits(4)
        for v in range(2):
            step = f"ret vT{v}"
            wait_full(act, step)
            b = bank0(step)
            for t in range(4):
                ins = nc.scalar.activation(VTOK[:, :, (4 * v + t) * P:(4 * v + t + 1) * P],
                                           PS[:, b + t, :].rearrange("p (j e) -> p j e", j=NTT), ACT.Copy)
            ins.then_inc(free(step), 1)
        for h in range(RH):
            step = ("ret O", h)
            wait_full(act, step)
            b = bank0(step)
            nc.scalar.activation(OB[:, 2 * h:2 * h + 2, 0:NP_], PS[:, b:b + 2, :], ACT.Copy)
            nc.scalar.activation(RST[:, h, :], PS[:, b + 2, 0:RDV], ACT.Copy).then_inc(free(step), 1)
        step = "ret sT"
        wait_full(act, step)
        nc.scalar.activation(VS[:], PS[0:NS, bank0(step) + 1:bank0(step) + 3, :].rearrange("p a b -> p (a b)"),
                             ACT.Copy).then_inc(vs_done, 1)
        for g in range(8, 12):
            a.splits(2)
            silu_pair(("hin", g), GS[:, 2 * (g - 8):2 * (g - 8) + 2, :])
            a.splits(2)
        for n in range(2):
            wait_free(act, ("ret y", 3))
            nc.scalar.activation(SQB[:, 4 * n:4 * n + 4, :], OB[:, 4 * n:4 * n + 4, :], ACT.Square).then_inc(sq_done, 1)
        for n in range(2):
            act.wait_ge(v2_done, n + 1)
            nc.scalar.activation(KT[:, 2 * n:2 * n + 2, :], QT[:, 2 * n:2 * n + 2, :], ACT.Sqrt).then_inc(rt_done, 1)

        def ret_high(n):
            act.wait_ge(o_done, n + 1)
            nc.scalar.activation(M1H[:, 4 * n:4 * n + 4, :], OB[:, 4 * n:4 * n + 4, :], ACT.Copy).then_inc(m1h_done, 1)

        for g in HIN_REST:
            a.splits(2)
            if g == 21:
                continue
            if g == HIN_REST[-1]:
                nc.scalar.activation(DA[:, 0, :], PV[:, V_ALOG:V_ALOG + SH], ACT.Exp)
                act.wait_ge(dt_abs, 1)
                nc.scalar.activation(DE[:], DE[:], ACT.Exp, scale=-1.0).then_inc(dt_exp, 1)
            if g < 16:
                silu_pair(("hin", g), ZS[:, 2 * (g - 12):2 * (g - 12) + 2, :])
                a.splits(2)
                if g == 13:
                    ret_high(0)
            else:
                wait_free(act, ("hin", g))
                if g == 16:
                    act.wait_ge(conv_loaded, 16)
                for m in range(2):
                    c = 2 * (g - 16) + m
                    w0 = PV[:, V_CONVW + c:V_CONVW + c + 1]
                    bias = PV[:, V_CONVB + c:V_CONVB + c + 1]
                    nc.scalar.activation(CACC[:, m, 0:NP_], CR[:, 2 * (g % 2) + m, 0:NP_], ACT.Identity, bias=bias, scale=w0)
                    nc.scalar.activation(CACC[:, m, NP_:T], SCI[:, c, 0, :], ACT.Identity, bias=bias,
                                         scale=w0).then_inc(tap_done, 1)
                for m in range(2):
                    a.splits(1)
                    c = 2 * (g - 16) + m
                    act.wait_ge(conv_done, c + 1)
                    dst = XS[:, c, :] if c < 8 else BC[:, c - 8, :]
                    nc.scalar.activation(dst, CACC[:, m, :], ACT.Silu).then_inc(convs_done, 1)
                if g == 16:
                    ret_high(1)
        step = "ssm BT"
        wait_full(act, step)
        nc.scalar.activation(BTOK[:].rearrange("p c n -> p (c n)"), PS[:, bank0(step), :], ACT.Copy).then_inc(free(step), 1)
        step = "ssm sums"
        wait_full(act, step)
        nc.scalar.activation(DX[:, 0, :], LA[:, 4, :], ACT.Exp)
        nc.scalar.activation(DEX[:].rearrange("p a b -> p (a b)"), PS[:, bank0(step), 0:128],
                             ACT.Exp).then_inc(free(step), 1)
        for c in range(NTT):
            step = ("ssm sc", c)
            wait_full(act, step)
            if c:
                wait_free(act, ("ssm sc", c - 1))
            b = bank0(step)
            nc.scalar.activation(CBE[:], PS[:, b + 2:b + 4, :].rearrange("p a b -> p (a b)"),
                                 ACT.Exp).then_inc(cbe_done, 1)
            step = ("ssm D", c)
            wait_full(act, step)
            if c:
                wait_full(act, ("ssm y", c - 1))
            b = bank0(step)
            for g in range(2):
                nc.scalar.activation(EM[:, 8 * g:8 * g + 8, :].rearrange("p h i -> p (h i)"),
                                     PS[:, b + 2 * g:b + 2 * g + 2, :].rearrange("p a b -> p (a b)"),
                                     ACT.Exp).then_inc(free(step) if g else em_done, 1)
        act.wait_ge(yg_done, 1)
        nc.scalar.activation(SQB[:], XS[:], ACT.Square).then_inc(ysq_done, 1)
        a.splits(2)
        for g in range(2):
            act.wait_ge(yv_done, g + 1)
            nc.scalar.activation(RT2[:, g], V2[:, g], ACT.Sqrt).then_inc(yr_done, 1)
        for t in range(8):
            if t == 2:
                a.splits(2)
            act.wait_ge(yn_done, t // 2 + 1)
            nc.scalar.activation(e.XH[:, t, :], XS[:, t, :], ACT.Copy,
                                 scale=PV[:, V_HNORM + t:V_HNORM + t + 1]).then_inc(yh_done, 1)
        for g in range(4):
            a.splits(6 if g else 2)
            if g == 3:
                wait_full(act, ("hout", 3))
                for p in range(3):
                    a.highs(nn + 1, p)
            wait_free(act, ("hout", g))
            a.squares(nn + 1, g)
            a.splits(2)
        a.highs(nn + 1, 3)

    def dve(dve, a):
        link = a.link

        def rstd_pair(step, out):
            wait_full(dve, step)
            for m in range(2):
                ins = nc.vector.tensor_tensor(halves(out[:, m, :]), acc(step)[:, 2 * m:2 * m + 2, :], halves(RSTD[:]), ALU.mult)
            ins.then_inc(free(step), 1)

        def rotate(g):
            step = ("hin", g)
            wait_full(dve, step)
            for m in range(2):
                t = 2 * g + m
                dst = (QT if t < 4 else KT)[:, t % 4, :]
                scale = 1.0 if t < 4 else RDK ** -0.5
                src = acc(step)[:, 2 * m:2 * m + 2, :]
                stt = lambda out, i0, i1: nc.vector.scalar_tensor_tensor(halves(out), i0, scale, halves(i1),
                                                                         ALU.mult, ALU.mult)
                if t >= 2:
                    dve.wait_ge(rot_done, t - 1)
                stt(dst, src, CT[:])
                stt(ROT[0:64, m, :], src[64:128], SN[64:128, :])
                ins = stt(ROT[64:128, m, :], src[0:64], SN[0:64, :])
                if m == 0:
                    link(ins)
                else:
                    ins.then_inc(free(step), 1)
                    wait_free(dve, step)
                nc.vector.tensor_tensor(dst, dst, ROT[:, m, :], ALU.add).then_inc(rot_done, 1)

        for g in range(8):
            a.splits(2 if g else 4)
            if g == 0:
                a.stats(("hin", 0), nn)
                dve.wait_ge(loaded, 16 * 3)
                nc.vector.tensor_tensor(CT[:], CT[:], RSTD[:], ALU.mult)
                link(nc.vector.tensor_tensor(SN[:], SN[:], RSTD[:], ALU.mult))
            if g < 4:
                rotate(g)
            else:
                rstd_pair(("hin", g), VTF[:, 2 * (g - 4):2 * (g - 4) + 2, :])
            if g:
                a.splits(2)
        step = "ret kT"
        wait_full(dve, step)
        b = bank0(step)
        nc.vector.tensor_tensor(KTOK[:], PS[:, b:b + 4, :].rearrange("p a (j d) -> p (a j) d", d=P),
                                PV[:, V_KEND:V_KEND + 16].unsqueeze(2).broadcast_to([P, 16, P]),
                                ALU.mult).then_inc(free(step), 1)
        for h in range(RH):
            step = ("ret S", h)
            wait_full(dve, step)
            if h >= 2:
                wait_full(dve, ("ret O", h - 2))
            b = bank0(step)
            for jt in range(NTT):
                n = NP_ - jt * P
                ins = nc.vector.tensor_tensor(ST[h % 2][:, soff[jt]:soff[jt] + n], PS[:, b + jt, 0:n],
                                              SEG[:, h, 0:n], ALU.mult)
            ins.then_inc(free(step), 1)
        step = "ret sT"
        wait_full(dve, step)
        b = bank0(step)
        for p in range(NS // 2):
            if p == NS // 2 - 1:
                dve.wait_ge(vs_done, 1)
            two = slice(2 * p, 2 * p + 2)
            nc.vector.tensor_tensor(KM[:, two], PS[0:NS, b, :].unsqueeze(1).broadcast_to([NS, 2, 512]),
                                    IDENT[0:NS, two].unsqueeze(2).broadcast_to([NS, 2, 512]),
                                    ALU.mult).then_inc(km_done if p < NS // 2 - 1 else free(step), 1)
        for p in range(NS // 2):
            step = ("ret outer", p)
            wait_full(dve, step)
            dve.wait_ge(s0_loaded[p % 2], 16 * (p // 2 + 1))
            b = bank0(step)
            for h in range(RH):
                s = S0[p % 2][:, :, h, :]
                ps = PS[:, b + h // 2:b + h // 2 + 3:2, (h % 2) * RDV:(h % 2 + 1) * RDV]
                ins = nc.vector.scalar_tensor_tensor(s, s, float(1.0 - 2.0 ** (-5 - h)), ps, ALU.mult, ALU.add)
            ins.then_inc(free(step), 1)
            a.splits(2)
            rstd_pair(("hin", 8 + p), GS[:, 2 * p:2 * p + 2, :])
            a.splits(2)
            step = ("ret y", p)
            wait_full(dve, step)
            b = bank0(step)
            nc.vector.tensor_copy(OB[:, :, NP_ + 2 * p:NP_ + 2 * p + 2],
                                  PS[:, b, 0:16].rearrange("p (j t) -> p t j", j=2)).then_inc(free(step), 1)
        for n in range(2):
            step = ("ret norm", n)
            wait_full(dve, step)
            v = QT[:, 2 * n:2 * n + 2, :]
            nc.vector.tensor_scalar(v.rearrange("p m (b t) -> p (m b) t", b=2), acc(step), 1.0 / RDV, EPS,
                                    ALU.mult, ALU.add).then_inc(free(step), 1)
            wait_free(dve, step)
            nc.vector.reciprocal(v, v).then_inc(v2_done, 1)

        def ret_gate(n):
            for hh in range(2):
                h = 2 * n + hh
                o = OB[:, 2 * h:2 * h + 2, :]
                ins = nc.vector.tensor_tensor(o, o, KT[:, h, :].unsqueeze(1).broadcast_to([P, 2, T]), ALU.mult)
            link(ins)
            if n == 0:
                dve.wait_ge(gs_done, 4)
            o = OB[:, 4 * n:4 * n + 4, :]
            nc.vector.tensor_tensor(o, o, GS[:, 4 * n:4 * n + 4, :], ALU.mult).then_inc(o_done, 1)

        def ret_low(n):
            dve.wait_ge(m1h_done, n + 1)
            nc.vector.tensor_tensor(M1L[:, 4 * n:4 * n + 4, :], OB[:, 4 * n:4 * n + 4, :],
                                    M1H[:, 4 * n:4 * n + 4, :].bitcast(F32), ALU.subtract).then_inc(m1l_done, 1)

        dve.wait_ge(rt_done, 2)
        for g in HIN_REST:
            a.splits(2)
            if g == 21:
                step = ("hin", 21)
                wait_full(dve, step)
                nc.vector.tensor_tensor(halves(DTR[:]), PS[0:SH, bank0(step):bank0(step) + 2, 0:TH], halves(RSTD[0:SH, :]),
                                        ALU.mult).then_inc(free(step), 1)
                continue
            if g == HIN_REST[-1]:
                step = "ssm dtT"
                link(nc.vector.memset(DX[:], 0.0))
                wait_full(dve, step)
                b = bank0(step)
                bias = PV[:, V_DTB:V_DTB + SH]
                nc.vector.tensor_tensor(DX[:, 0:NTT, :], PS[:, b, 0:64].rearrange("p (c h) -> p c h", c=NTT),
                                        bias.unsqueeze(1).broadcast_to([P, NTT, SH]), ALU.add)
                nc.vector.tensor_tensor(DX[0:NS, NTT, :], PS[0:NS, b, 64:80], bias[0:NS], ALU.add).then_inc(free(step), 1)
                wait_free(dve, step)
                nc.vector.scalar_tensor_tensor(DE[:], DX[:], -1.0, DX[:], ALU.mult, ALU.max).then_inc(dt_abs, 1)
                nc.vector.tensor_scalar(DP[:], DX[:], 0.0, None, ALU.max)
            if g < 16:
                rstd_pair(("hin", g), ZS[:, 2 * (g - 12):2 * (g - 12) + 2, :])
                if g == HIN_REST[-1]:
                    dve.wait_ge(dt_exp, 1)
                    link(nc.vector.tensor_scalar(DS_[:], DE[:], 2.0, None, ALU.add))
                    link(nc.vector.reciprocal(DS_[:], DS_[:]))
                    link(nc.vector.tensor_tensor(DS_[:], DS_[:], DE[:], ALU.mult))
                    link(nc.vector.tensor_tensor(DS2[:], DS_[:], DS_[:], ALU.mult))
                    link(nc.vector.tensor_scalar(DH[:], DS2[:], 1.0 / 17, None, ALU.mult))
                    for k in range(15, 1, -2):
                        link(nc.vector.scalar_tensor_tensor(DH[:], DH[:], 1.0 / k, DS2[:], ALU.add, ALU.mult))
                    link(nc.vector.scalar_tensor_tensor(DH[:], DH[:], 1.0, DS_[:], ALU.add, ALU.mult))
                    link(nc.vector.scalar_tensor_tensor(DT[:], DH[:], 2.0, DP[:], ALU.mult, ALU.add))
                    nc.vector.scalar_tensor_tensor(LA[:], DT[:], -1.0, DA[:, 0:1, :].broadcast_to([P, 5, SH]), ALU.mult,
                                                   ALU.mult).then_inc(dt_done, 1)
                a.splits(2)
                if g < 14:
                    ret_gate(g - 12)
                if g == 14:
                    ret_low(0)
                    ret_low(1)
                continue
            if g == 16:
                link(nc.vector.memset(CR[:, :, 0:3], 0.0))
            step = ("hin", g)
            wait_full(dve, step)
            for m in range(2):
                cr = CR[:, 2 * (g % 2) + m, 3:523]
                ins = nc.vector.tensor_tensor(halves(cr), acc(step)[:, 2 * m:2 * m + 2, :], halves(RSTD[:]), ALU.mult)
                if m == 0:
                    link(ins)
            ins.then_inc(free(step), 1)
            wait_free(dve, step)
            for m in range(2):
                c = 2 * (g - 16) + m
                cr = CR[:, 2 * (g % 2) + m, :]
                w = [PV[:, V_CONVW + XBC * k + c:V_CONVW + XBC * k + c + 1] for k in range(CONV_W)]
                dve.wait_ge(tap_done, c + 1)
                for k in range(1, CONV_W):
                    nc.vector.scalar_tensor_tensor(CACC[:, m, 0:NP_], cr[:, k:k + NP_], w[k], CACC[:, m, 0:NP_],
                                                   ALU.mult, ALU.add)
                    xs = SCI[:, c, k, :] if k < 3 else cr[:, 515:523]
                    ins = nc.vector.scalar_tensor_tensor(CACC[:, m, NP_:T], xs, w[k], CACC[:, m, NP_:T],
                                                         ALU.mult, ALU.add)
                    if k < 3:
                        link(ins)
                    else:
                        ins.then_inc(conv_done, 1)
                nc.vector.tensor_copy(CPO[:, c, :], cr[:, 512:515])
                ins = nc.vector.tensor_copy(CSO[:, c, 2, :], cr[:, 515:523])
                if g < 20 or m == 0:
                    a.splits(1)
            if g == 16:
                nc.vector.tensor_copy(CSO[:, :, 0:2, :], SCI[:, :, 1:3, :])
            if g == 20:
                ins.then_inc(out_ready, 1)
                a.splits(1)
        for v in range(2):
            step = f"ssm xT{v}"
            wait_full(dve, step)
            b = bank0(step)
            for jt in range(NTT):
                out = XTOK[:, jt, v * 512:(v + 1) * 512].rearrange("p (t h d) -> p t h d", t=4, h=2)
                ins = nc.vector.tensor_tensor(out, PS[:, b:b + 4, jt * P:(jt + 1) * P].rearrange("p t (h d) -> p t h d", h=2),
                                              DT[:, jt, 8 * v:8 * v + 8].rearrange("p (t h) -> p t h", t=4)
                                              .unsqueeze(3).broadcast_to([P, 4, 2, SHD]), ALU.mult)
            ins.then_inc(free(step), 1)
        wait_free(dve, "ssm sums")
        nc.vector.tensor_tensor(DECX[:], DX[0:NS, 0:1, :].broadcast_to([NS, NS, SH]),
                                IDENT[0:NS, 0:NS].unsqueeze(2).broadcast_to([NS, NS, SH]), ALU.mult).then_inc(dx_done, 1)
        step = "ssm dec"
        wait_full(dve, step)
        nc.vector.tensor_copy(DECB[:], PS[:, bank0(step), 0:64]).then_inc(free(step), 1)

        def ssm_values(c):
            tok = slice(c * P, (c + 1) * P)
            step = ("ssm y", c)
            b = bank0(step)
            for t in range(8):
                nc.vector.scalar_tensor_tensor(XS[:, t, tok], XS[:, t, tok], PV[:, V_DSKIP + t:V_DSKIP + t + 1],
                                               PS[:, b + t // 4, (t % 4) * P:(t % 4 + 1) * P], ALU.mult, ALU.add)
            if c == 0:
                nc.vector.tensor_copy(SST[:], PS[:, b + 2, :]).then_inc(free(step), 1)
            else:
                for g in range(2):
                    rows = slice(64 * g, 64 * g + 64)
                    s = SST[rows, :].rearrange("p (h d) -> p h d", h=8)
                    ins = nc.vector.tensor_tensor(s, s, DEX[rows, 1, c * SH + 8 * g:c * SH + 8 * g + 8]
                                                  .unsqueeze(2).broadcast_to([64, 8, SHD]), ALU.mult)
                link(ins)
                nc.vector.tensor_tensor(SST[:], SST[:], PS[:, b + 2, :], ALU.add).then_inc(free(step), 1)
            wait_free(dve, step)

        for c in range(NTT):
            tok = slice(c * P, (c + 1) * P)
            step = ("ssm sc", c)
            wait_full(dve, step)
            b = bank0(step)
            if c:
                dve.wait_ge(m_done, 2 * c)
            nc.vector.tensor_tensor(SM[:], PS[:, b:b + 2, 0:P], UPTO.unsqueeze(1).broadcast_to([P, 2, P]), ALU.mult)
            dve.wait_ge(cbe_done, c + 1)
            if c:
                wait_full(dve, ("ssm y", c - 1))
            nc.vector.tensor_tensor(CS[:], BC[:, 1, tok].unsqueeze(1).broadcast_to([P, 8, P]),
                                    CBE[:].rearrange("p (h i) -> p h i", h=8), ALU.mult).then_inc(free(step), 1)
            wait_free(dve, step)
            if c:
                ssm_values(c - 1)
            for g in range(2):
                if g:
                    wait_free(dve, ("ssm D", c))
                else:
                    dve.wait_ge(em_done, c + 1)
                em = EM[:, 8 * g:8 * g + 8, :]
                nc.vector.tensor_tensor(em, em, SM[:, g:g + 1, :].broadcast_to([P, 8, P]), ALU.mult).then_inc(m_done, 1)
        step = "ssm sT"
        wait_full(dve, step)
        b = bank0(step)
        nc.vector.tensor_tensor(BM[:], PS[0:NS, b + 2, 0:P].unsqueeze(1).broadcast_to([NS, NS, P]),
                                IDENT[0:NS, 0:NS].unsqueeze(2).broadcast_to([NS, NS, P]), ALU.mult)
        wait_full(dve, ("ssm y", NTT - 1))
        nc.vector.tensor_tensor(XDS[:].rearrange("p (h d) -> p h d", d=SHD),
                                PS[0:NS, b:b + 2, :].rearrange("p a (h d) -> p (a h) d", d=SHD),
                                DT[0:NS, NTT, :].unsqueeze(2).broadcast_to([NS, SH, SHD]), ALU.mult).then_inc(free(step), 1)
        link(nc.vector.memset(CM[:], 0.0))
        for g in range(2):
            rows = slice(64 * g, 64 * g + 64)
            ins = nc.vector.tensor_copy(CM[rows].rearrange("p s r -> p (s r)")[:, g::2 * NS + 2], BC[rows, 1, NP_:T])
        link(ins)
        ssm_values(NTT - 1)
        dve.wait_ge(sss_loaded, 16)
        for k in range(2):
            s = SSS[:, 4 * k:4 * k + 4, :].rearrange("p b (h d) -> p (b h) d", d=SHD)
            link(nc.vector.tensor_tensor(s, s, DECB[:, 32 * k:32 * k + 32].unsqueeze(2).broadcast_to([P, 32, SHD]), ALU.mult))
        for k in range(2):
            step = ("ssm outer", k)
            wait_full(dve, step)
            s = SSS[:, 4 * k:4 * k + 4, :]
            nc.vector.tensor_tensor(s, s, PS[:, bank0(step):bank0(step) + 4, :], ALU.add).then_inc(free(step), 1)
        step = "ssm ys"
        wait_full(dve, step)
        nc.vector.tensor_copy(YB[:], PS[0:2 * NS, bank0(step), :]).then_inc(free(step), 1)
        step = "ssm yT"
        wait_full(dve, step)
        b = bank0(step)
        for t in range(8):
            ins = nc.vector.scalar_tensor_tensor(XS[:, t, NP_:T], XS[:, t, NP_:T], PV[:, V_DSKIP + t:V_DSKIP + t + 1],
                                                 PS[:, b, 2 * NS * (t % 4) + t // 4:2 * NS * (t % 4 + 1):2],
                                                 ALU.mult, ALU.add)
        ins.then_inc(free(step), 1)
        wait_free(dve, step)
        dve.wait_ge(gs_done, 8)
        nc.vector.tensor_tensor(XS[:], XS[:], ZS[:], ALU.mult).then_inc(yg_done, 1)
        a.splits(2)
        step = "ssm norm"
        wait_full(dve, step)
        nc.vector.tensor_scalar(V2[:].rearrange("p m (b t) -> p (m b) t", b=2), acc(step), 1.0 / 512, EPS, ALU.mult,
                                ALU.add).then_inc(free(step), 1)
        wait_free(dve, step)
        for g in range(2):
            nc.vector.reciprocal(V2[:, g], V2[:, g]).then_inc(yv_done, 1)
        for t in range(0, 8, 2):
            if t % 4 == 0:
                dve.wait_ge(yr_done, t // 4 + 1)
            y = XS[:, t:t + 2, :]
            nc.vector.tensor_tensor(y, y, RT2[:, t // 4:t // 4 + 1, :].broadcast_to([P, 2, T]), ALU.mult).then_inc(yn_done, 1)
            for u in (t, t + 1):
                dve.wait_ge(yh_done, u + 1)
                nc.vector.scalar_tensor_tensor(e.XL[:, u, :], XS[:, u, :], PV[:, V_HNORM + u:V_HNORM + u + 1],
                                               e.XH[:, u, :].bitcast(F32), ALU.mult, ALU.subtract).then_inc(yl_done, 1)
            if t == 0:
                a.splits(2)
        for g in range(4):
            a.splits(6 if g else 2)
            if g == 3:
                wait_full(dve, ("hout", 3))
                a.lows(nn + 1, 0)
                a.lows(nn + 1, 1)
            a.residual(("hout", g), g, 1.0)
            a.splits(2)
        for g in range(2, 4):
            a.lows(nn + 1, g)

    def pool(pool, a):
        def store(dst, src):
            pool.dma_start(dst, src).then_inc(e.out_stored, 16)
            a.stores[0] += 1

        if before:
            wait_full(pool, (before, "out", 3))
        pool.dma_start(CT[:], io["ret_cos"]).then_inc(loaded, 16)
        pool.dma_start(SN[:], io["ret_sin"]).then_inc(loaded, 16)
        pool.dma_start(SEG[:], io["ret_decays"]).then_inc(loaded, 16)
        wait_free(pool, ("ret S", 3))
        pool.dma_start(S0[0][:], io["state_ret"][:, 0:2]).then_inc(s0_loaded[0], 16)
        wait_free(pool, ("ret O", 3))
        pool.dma_start(S0[1][:], io["state_ret"][:, 2:4]).then_inc(s0_loaded[1], 16)
        store(io["ret_p"], RST[:])
        for p in range(NS // 2):
            wait_free(pool, ("ret outer", p))
            pool.dma_start(io["ret_s"][:, 2 * p:2 * p + 2], S0[p % 2][:]).then_inc(s0_stored[p % 2], 16)
            if p < 2:
                pool.wait_ge(s0_stored[p % 2], 16)
                wait_full(pool, ("ret y", p))
                pool.dma_start(S0[p % 2][:], io["state_ret"][:, 2 * p + 4:2 * p + 6]).then_inc(s0_loaded[p % 2], 16)
        for s in range(2):
            pool.wait_ge(s0_stored[s], 32)
        wait_full(pool, ("ret norm", 1))
        pool.dma_start(SCI[:], io["state_conv"]).then_inc(conv_loaded, 16)
        pool.wait_ge(out_ready, 1)
        store(io["conv_p"], CPO[:])
        store(io["conv_s"], CSO[:])
        pool.wait_ge(e.out_stored, 16 * a.stores[0])
        pool.wait_ge(dt_done, 1)
        for c in range(NTT):
            if c:
                wait_full(pool, ("ssm sc", c - 1))
            nc.gpsimd.tensor_copy(LAW[:], LA[:, c, :].rearrange("p (g h) -> p h g", g=2).unsqueeze(3)
                                  .broadcast_to([P, 8, 2, 64])).then_inc(law_done, 1)
            if c:
                wait_full(pool, ("ssm D", c - 1))
            else:
                pool.wait_ge(convs_done, XBC)
            nc.gpsimd.tensor_tensor(LM[:], AFTER.unsqueeze(1).broadcast_to([P, SH, P]),
                                    LA[:, c, :].unsqueeze(2).broadcast_to([P, SH, P]), ALU.mult).then_inc(l_done, 1)
            if c:
                wait_full(pool, ("ssm y", c - 1))
            else:
                wait_free(pool, "ssm xT1")
                wait_free(pool, "ssm sums")
            nc.gpsimd.tensor_tensor(XEND[:].rearrange("p (h d) -> p h d", d=SHD),
                                    XTOK[:, c, :].rearrange("p (h d) -> p h d", d=SHD),
                                    DEX[:, 0, c * SH:(c + 1) * SH].unsqueeze(2).broadcast_to([P, SH, SHD]),
                                    ALU.mult).then_inc(xend_done, 1)
        wait_full(pool, ("ssm y", 3))
        pool.dma_start(SSS[:], io["state_ssm"]).then_inc(sss_loaded, 16)
        wait_free(pool, ("ssm y", 3))
        store(io["ssm_p"], SST[:])
        wait_free(pool, ("ssm outer", 1))
        store(io["ssm_s"], SSS[:])
        a.norm_sums(nn + 1)
        pool.wait_ge(e.out_stored, 16 * a.stores[0])

    parts = Shared()
    parts.pe, parts.act, parts.dve, parts.pool = pe, act, dve, pool
    return parts


def lay_out_hyb(a, tile, gamma):
    f = np.float32
    i = np.arange(P)
    dist = np.arange(NP_)[None, :] - i[:, None]
    decays = np.stack([np.where(dist >= 0, np.exp(g * np.maximum(dist, 0)), 0.0) for g in gamma], 1).astype(f)
    pos = np.concatenate([np.arange(NP_), np.full(NS, PAST)]).astype(f)
    inv = (np.float32(10000.0) ** (-np.arange(64, dtype=f) / 64)).astype(f)
    ang = (inv[:, None] * pos[None]).astype(f)
    cos, sin = np.cos(ang.astype(np.float64)), np.sin(ang.astype(np.float64))
    return {
        "ret_decays": decays,
        "ret_cos": np.concatenate([cos, cos], 0).astype(f),
        "ret_sin": np.concatenate([sin, -sin], 0).astype(f),
        "state_ret": a["state_ret"][0].transpose(2, 0, 1, 3),
        "state_conv": a["state_conv"][0].reshape(NS, 3, XBC, P).transpose(3, 2, 1, 0),
        "state_ssm": a["state_ssm"][0].reshape(NS, 2, 8, SST_N, SHD).transpose(1, 3, 0, 2, 4).reshape(P, NS, 512),
    }


SST_N = 64
OUT_HYB = {"ret_p": (P, RH, RDV), "ret_s": (P, NS, RH, RDV), "conv_p": (P, XBC, 3), "conv_s": (P, XBC, 3, NS),
           "ssm_p": (P, 512), "ssm_s": (P, NS, 512)}


def hyb_results(o):
    ssm = lambda s, n: s.reshape(2, SST_N, n, 8, SHD).transpose(2, 0, 3, 1, 4).reshape(1, n, SH, SST_N, SHD)
    return (o["ret_p"].transpose(1, 0, 2)[None, None], o["ret_s"].transpose(1, 2, 0, 3)[None],
            ssm(o["ssm_p"], 1), ssm(o["ssm_s"], NS),
            o["conv_p"].transpose(2, 1, 0).reshape(1, 1, 3, XBC * P),
            o["conv_s"].transpose(3, 2, 1, 0).reshape(1, NS, 3, XBC * P))


def mla_parts(e):
    nc, io, plan, at, sem, PS = e.nc, e.io, e.plan, e.at, e.sem, e.PS
    REGION, GU_OFF = e.REGION, e.GU_OFF
    IDENT, ONES, NEGM, PV, RSTD = e.IDENT, e.ONES, e.NEGM, e.PV, e.RSTD
    acc, bank0, halves = e.acc, e.bank0, e.halves
    wait_full, wait_free, acquire = e.wait_full, e.wait_free, e.acquire
    full = lambda step: e.acc_full[plan.set_of[step]]
    free = lambda step: e.acc_free[plan.set_of[step]]
    nn = e.nn_of["mla"]
    before = e.phases[nn - 1] if nn else None
    XH, XL = e.XH, e.XL

    CQF = at("q_latent", [P, 4, T], REGION)
    XQH = at("q_latent_high", [P, 4, T], REGION + 8320, F32R)
    XQL = at("q_latent_low", [P, 4, T], REGION + 16640, F32R)
    OTOK = at("attention_tokens", [P, NTT, MH * VD], REGION)
    CKF = at("kv_latent", [P, 2, T], REGION + 24960)
    CKH = at("kv_latent_high", [P, 2, T], REGION + 29120, F32R)
    CKL = at("kv_latent_low", [P, 2, T], REGION + 33280, F32R)
    KRT = at("rotary_key", [P, T], REGION + 37440)
    Q = at("queries", [P, MH, T], REGION + 39520)
    TAB = at("query_scale", [P, T], REGION + 72800)
    TABR = at("rope_table", [P, T], REGION + 74880)
    V = at("values", [P, NTT, MH * VD], REGION + 72800)
    KRX = at("rotary_parts", [P, T], REGION + 89184)
    KRB = at("rotary_second", [P, T], REGION + 91264)
    TABK = at("key_table", [P, T], REGION + 93344)
    WUKT = at("w_uk_by_head", [NOPE, MH, KVL], e.XH_OFF)
    KTT = at("keys", [P, MH, NP_], e.XH_OFF)
    HALF = NPG // 2
    TB = [at("cache_features0", [P, HALF, 3 * P], REGION + 89184), at("cache_features1", [P, HALF, 3 * P], e.WH_OFF)]
    TB_FIRST = at("cache_features_first", [P, HALF, 3 * P], REGION)
    NAT = [at("cache_rows0", [P, HALF, KVL], REGION + 16384), at("cache_rows1", [P, HALF, KVL], REGION + 29120)]
    WUV = at("w_uv_f32", [P, 2, MH * VD], REGION + 89184)
    PGT = at("page_numbers", [1, NS * NPG], REGION + 103584, I32)
    PB = [at(f"probs{i}", [P, 1280], e.SQS_OFF + 5120 * i) for i in range(2)]
    PT = at("probs_by_key", [P, 1280], GU_OFF)
    SQC = at("latent_squares", [P, 6, T], GU_OFF)
    V2 = at("latent_variance", [P, 2, T], GU_OFF + 12480)
    R2 = at("latent_rstd", [P, 2, T], e.SQT_OFF)
    small = [GU_OFF + 5120]

    def little(name, shape):
        small[0] += int(np.prod(shape[1:])) * 4
        return at(name, shape, small[0] - int(np.prod(shape[1:])) * 4)

    SSB = [little(f"sample_scores{i}", [P, (NPG + 1) * MH]) for i in range(2)]
    SPB = [little(f"sample_probs{i}", [P, NPG + 1, MH]) for i in range(2)]
    MXP = little("sample_max", [P, MH])
    MXA = little("sample_max_all", [P, MH])
    LSUM = little("sample_sum", [P, MH])
    LPN = little("sample_sum_all", [P, 2 * MH])
    O2 = little("sample_out_part", [P, 2, MH])
    QLAT = little("sample_q_latent", [P, 2, NS, MH])
    OBH = little("sample_out_by_head", [MH, KVL])
    OLAT = little("sample_out_latent", [P, 2, MH, NS])
    OTS = little("sample_out", [P, 8, NS])
    MX = little("row_max", [P, 2, NTT])
    LS = little("row_sum", [P, 2, NTT])
    RL = little("row_rcp", [P, 2, NTT])

    loaded, wuk_loaded, wuv_loaded = sem("mla_tables_loaded"), sem("w_uk_loaded"), sem("w_uv_loaded")
    t_loaded = [sem("cache_features_loaded0"), sem("cache_features_loaded1")]
    n_loaded = [sem("cache_rows_loaded0"), sem("cache_rows_loaded1")]
    lsq_done, xqh_done, xq_done = sem("latent_squares_done"), sem("q_high_done"), sem("q_low_done")
    lv_done, lr_done = sem("latent_rcp_done"), sem("latent_rstd_done")
    ckn_done, ckh_done, ck_done = sem("kv_normed_done"), sem("kv_high_done"), sem("kv_low_done")
    kr_done, krr_done = sem("rotary_key_done"), sem("keys_rotary_done")
    smx_done, sall_done, sd_done, sp_done, sl_done = (sem(n) for n in (
        "sample_max_done", "sample_max_all_done", "sample_scores_less_max", "sample_probs_done", "sample_sum_done"))
    mx_done, oh_done, ol_done = sem("row_max_done"), sem("out_high_done"), sem("out_low_done")
    SC0, SV0 = NTT * VD, NTT * VD + (HALF + 1) * MH
    block_of = lambda it, jt: it * (it + 1) // 2 + jt

    def sp(sp, weight_chunks):
        def load(what, q, pages=range(HALF), i=None, wait=None):
            n, k = q * HALF + pages[0], len(pages)
            at_ = PGT[0:1, n:n + k] if i is None else PGT[0:1, bass.ds(NPG * i + n, k)]
            numbers = nc.values_load_multi_w_load_instructions(at_, [mybir.EngineType.SP], min_val=0,
                                                               max_val=N_PHYS - 1)[1]
            for pg, idx in zip(pages, numbers):
                if wait and pg == 0:
                    wait()
                if what == "rows":
                    sp.dma_start(NAT[q % 2][:, pg, :], io["cache_rows"][bass.ds(idx, 1)]
                                 .rearrange("a p n -> (a p) n")).then_inc(n_loaded[q % 2], 16)
                else:
                    tb = TB_FIRST if q == 1 else TB[q % 2]
                    sp.dma_start(tb[:, pg, :], io["cache_features"][bass.ds(idx, 1)]
                                 .rearrange("a p n -> (a p) n")).then_inc(t_loaded[q % 2], 16)

        n = plan.first[("uq", 2)]
        weight_chunks(0, n)
        sp.wait_ge(loaded, 32)
        if before:
            wait_full(sp, (before, "out", 3))
        sp.wait_ge(kr_done, 2)
        for pg in range(HALF):
            weight_chunks(n + pg, n + pg + 1)
            load("features", 0, [pg])
        n += HALF
        weight_chunks(n, plan.first[("uv", 0)])
        wait_full(sp, ("uq", 7))
        n = plan.first[("uv", 0)]
        for c in range(R):
            weight_chunks(n + c, n + c + 1)
            load("features", 1, range(2 * c, 2 * c + 2))
        weight_chunks(n + R, n + 2 * R)
        load("rows", 0)
        load("features", 2, wait=lambda: wait_full(sp, ("smp S", 0)))
        load("rows", 1, wait=lambda: wait_full(sp, ("uv", 1)))
        load("features", 3, wait=lambda: wait_full(sp, ("smp S", 1)))
        with sp.Fori(0, (2 * NS - 4) // 2) as i:
            for q in (2, 3):
                load("features", q + 2, i=i, wait=lambda: wait_full(sp, ("att TO", q - 1), 2 * i))
                load("rows", q, i=i)
        for q in (2 * NS - 2, 2 * NS - 1):
            load("rows", q, wait=lambda: wait_full(sp, ("att TO", q - 1)))
        weight_chunks(n + 2 * R, None)

    def pe(pe):
        def transposes(step, items, waits=()):
            acquire(pe, step)
            for w in waits:
                w()
            for out, src in items:
                k = src.shape[0]
                mm = nc.tensor.transpose(out, src, IDENT[0:k, 0:k])
            mm.then_inc(full(step), 1)

        e.gemm(pe, ("min", 0), 2, KD, e.x_rhs, before_k=e.first_wait(pe, nn))
        e.pe_stats(pe, ("min", 0), nn)
        e.gemm(pe, ("min", 1), 2, KD, e.x_rhs)
        e.gemm(pe, ("min", 2), 2, KD, e.x_rhs)
        e.gemm(pe, ("min", 3), 1, KD, e.x_rhs)
        step = "mla cnorm"
        acquire(pe, step)
        pe.wait_ge(lsq_done, 3)
        b = bank0(step)
        for which, tiles in enumerate((range(4), range(4, 6))):
            for half in range(2):
                for t in tiles:
                    mm = nc.tensor.matmul(PS[:, b + 2 * which + half, 0:TH], ONES, SQC[:, t, half * TH:(half + 1) * TH],
                                          start=t == tiles[0], stop=t == tiles[-1])
        mm.then_inc(full(step), 1)
        for g in range(8):
            e.gemm(pe, ("uq", g), 2, 4, lambda k: (XQH[:, k, :], XQL[:, k, :]),
                   before_k=(lambda k: pe.wait_ge(xq_done, k + 1)) if g == 0 else None)
        step = "smp qlat"
        acquire(pe, step)
        wait_free(pe, ("uq", 7))
        pe.wait_ge(wuk_loaded, 16)
        b = bank0(step)
        for h in range(MH):
            for ct in range(2):
                mm = nc.tensor.matmul(PS[:, b + ct, h * NS:(h + 1) * NS], WUKT[:, h, ct * P:(ct + 1) * P],
                                      Q[0:NOPE, h, NP_:T], start=True, stop=True)
        mm.then_inc(full(step), 1)

        def smp_scores_page(bank, q, pg):
            s, u = divmod(q, 2)
            tb = TB_FIRST if q == 1 else TB[u]
            if pg == 0:
                pe.wait_ge(t_loaded[u], 16 * HALF * (s + 1))
            out = bank[:, SC0 + pg * MH:SC0 + (pg + 1) * MH]
            for ct in range(2):
                nc.tensor.matmul(out, tb[:, pg, ct * P:(ct + 1) * P], QLAT[:, ct, s, :], start=ct == 0, stop=False)
            return nc.tensor.matmul(out, tb[64:128, pg, 2 * P:3 * P], Q[64:128, :, NP_ + s], start=False, stop=True)

        def smp_new_row(bank, s):
            out = bank[0:1, SC0 + HALF * MH:SC0 + (HALF + 1) * MH]
            for ct in range(2):
                nc.tensor.matmul(out, CKF[:, ct, NP_ + s:NP_ + s + 1], QLAT[:, ct, s, :], start=ct == 0, stop=False)
            return nc.tensor.matmul(out, KRT[64:128, NP_ + s:NP_ + s + 1], Q[64:128, :, NP_ + s], start=False, stop=True)

        def smp_sum(bank, s, k):
            out = bank[:, SV0 + (2 + k) * MH:SV0 + (3 + k) * MH]
            if k == 0:
                pe.wait_ge(sl_done, s + 1)
                return nc.tensor.matmul(out, ONES, LSUM[:], start=True, stop=True)
            return nc.tensor.matmul(out, ONES[0:1, :], SPB[s % 2][0:1, NPG, :], start=True, stop=True)

        def smp_values_page(b, q, pg):
            s, u = divmod(q, 2)
            if pg == 0:
                pe.wait_ge(sp_done, s + 1)
                pe.wait_ge(n_loaded[u], 16 * HALF * (s + 1))
            return nc.tensor.matmul(PS[0:MH, b + 2, KVL:2 * KVL], SPB[s % 2][:, HALF * u + pg, :], NAT[u][:, pg, :],
                                    start=pg == 0, stop=pg == HALF - 1)

        def smp_turned(bank, ct):
            return nc.tensor.transpose(bank[:, SV0 + ct * MH:SV0 + (ct + 1) * MH], OBH[:, ct * P:(ct + 1) * P],
                                       IDENT[0:MH, 0:MH])

        def smp_extra(bank, h, k):
            if h % 2 == 0 and h + 1 < 2 * NS and k == 3:
                return smp_new_row(bank, h // 2)
            if h % 2 and k < 2 and h > 1:
                return smp_turned(bank, k)
            if h % 2 and k >= 2:
                return smp_sum(bank, h // 2, k - 2)
            return None

        def first_scores(q):
            step = ("smp S", q)
            acquire(pe, step)
            bank = PS[:, bank0(step) + 3, :]
            for pg in range(HALF):
                mm = smp_scores_page(bank, q, pg)
            if q:
                mm = smp_new_row(bank, 0)
            mm.then_inc(full(step), 1)

        for g in range(4):
            e.gemm(pe, ("uk", g), 2, 2, lambda k: (CKH[:, k, :], CKL[:, k, :]), cols=NP_ // 2,
                   before_k=(lambda k: pe.wait_ge(ck_done, k + 1)) if g == 0 else None)
        wait_free(pe, "smp qlat")
        first_scores(0)
        for g in range(2):
            step = ("uv", g)
            acquire(pe, step)
            b = bank0(step)
            for ct in range(2):
                n = plan.first[step] + ct
                pe.wait_ge(e.w_split, n + 1)
                for tt in range(NTT):
                    kh, kl = (k[:, ct, tt * P:(tt + 1) * P] for k in (CKH, CKL))
                    wh, wl = e.WH[:, n % R, :], e.WL[:, n % R, :]
                    for k, w, st, sp_ in ((kh, wh, ct == 0, False), (kh, wl, False, False), (kl, wh, False, ct == 1)):
                        mm = nc.tensor.matmul(PS[:, b + tt, :], k, w, start=st, stop=sp_)
                mm.then_inc(e.w_used if ct == 0 else full(step), 1)
        first_scores(1)

        def scores(h):
            step = ("att S", h)
            acquire(pe, step)
            if h == 0:
                wait_free(pe, ("uk", 3))
                pe.wait_ge(krr_done, 1)
            b = bank0(step)
            for it in range(NTT):
                n = (it + 1) * P
                nc.tensor.matmul(PS[:, b + it, 0:n], Q[:, h, it * P:n], KTT[:, h, 0:n], start=True, stop=False)
                mm = nc.tensor.matmul(PS[:, b + it, it * P:n], IDENT, NEGM, start=False, stop=True)
            mm.then_inc(full(step), 1)

        scores(0)
        for h in range(MH + 1):
            if h + 1 < MH:
                scores(h + 1)
            step = ("att TO", h)
            acquire(pe, step)
            b = bank0(step)
            bank = PS[:, b + 3, :]
            if h == 1:
                wait_free(pe, ("uv", 1))
            if h:
                wait_free(pe, ("att TO", h - 1))
            if h < MH:
                wait_free(pe, ("att S", h))

            def turn(n):
                return nc.tensor.transpose(PS[:, b + n // 4, (n % 4) * P:(n % 4 + 1) * P],
                                           PB[h % 2][:, n * P:(n + 1) * P], IDENT)

            for it in range(NTT):
                for jt in range(it + 1):
                    n = block_of(it, jt)
                    if h:
                        nc.tensor.matmul(bank[:, it * VD:(it + 1) * VD], PT[:, n * P:(n + 1) * P],
                                         V[:, jt, (h - 1) * VD:h * VD], start=jt == 0, stop=jt == it)
                    if h < MH and n < 8:
                        turn(n)
            if h:
                for pg in range(HALF):
                    if h + 1 < 2 * NS:
                        smp_scores_page(bank, h + 1, pg)
                    mm = smp_values_page(b, h - 1, pg)
                    if pg % 2:
                        mm = smp_extra(bank, h, pg // 2) or mm
            if h < MH:
                turn(8)
                mm = turn(9)
            mm.then_inc(full(step), 1)

        def out_transposes(v):
            b = bank0(f"att OT{v}")
            transposes(f"att OT{v}", [(PS[:, b + t, it * P:(it + 1) * P], OTOK[:, it, (4 * v + t) * P:(4 * v + t + 1) * P])
                                      for t in range(4) for it in range(NTT)],
                       [lambda: wait_free(pe, ("att TO", MH))])

        step = "smp T"
        acquire(pe, step)
        wait_free(pe, ("att TO", MH))
        for ct in range(2):
            mm = smp_turned(PS[:, bank0(step) + 3, :], ct)
        mm.then_inc(full(step), 1)
        out_transposes(0)
        step = "smp O"
        acquire(pe, step)
        wait_free(pe, "smp T")
        pe.wait_ge(wuv_loaded, 16)
        b = bank0(step)
        for h in range(MH):
            for ct in range(2):
                mm = nc.tensor.matmul(PS[64 * (h % 2):64 * (h % 2) + 64, b, (h // 2) * NS:(h // 2 + 1) * NS],
                                      WUV[:, ct, h * VD:(h + 1) * VD], OLAT[:, ct, h, :], start=ct == 0, stop=ct == 1)
        mm.then_inc(full(step), 1)
        out_transposes(1)
        for g in range(4):
            e.gemm(pe, ("wo", g), 2, KD, e.x_rhs,
                   before_k=(lambda k: pe.wait_ge(ol_done, 1) if k < 4 else wait_free(pe, "att OT1")) if g == 0 else None)

    def act(act, a):
        for g in range(2):
            a.splits(2 if g else 4)
            if g == 0:
                a.stats(nn)
            wait_free(act, ("min", g))
            nc.scalar.activation(SQC[:, 2 * g:2 * g + 2, :], CQF[:, 2 * g:2 * g + 2, :], ACT.Square).then_inc(lsq_done, 1)
            for m in range(2):
                t = 2 * g + m
                nc.scalar.activation(XQH[:, t, :], CQF[:, t, :], ACT.Copy,
                                     scale=PV[:, V_QNORM + t:V_QNORM + t + 1]).then_inc(xqh_done, 1)
            if g:
                a.splits(2)
        a.splits(2)
        wait_free(act, ("min", 2))
        nc.scalar.activation(SQC[:, 4:6, :], CKF[:], ACT.Square).then_inc(lsq_done, 1)
        a.splits(2)
        a.splits(2)
        act.wait_ge(lv_done, 1)
        nc.scalar.activation(R2[:, 0], V2[:, 0], ACT.Sqrt).then_inc(lr_done, 1)
        a.splits(2)
        act.wait_ge(lv_done, 2)
        nc.scalar.activation(R2[:, 1], V2[:, 1], ACT.Sqrt).then_inc(lr_done, 1)
        a.splits(2)
        act.wait_ge(ckn_done, 2)
        for t in range(2):
            nc.scalar.activation(CKH[:, t, :], CKF[:, t, :], ACT.Copy).then_inc(ckh_done, 1)
        for g in range(6):
            a.splits(2)
        for g in range(4):
            a.splits(1)
        for g in range(2):
            step = ("uv", g)
            wait_full(act, step)
            b = bank0(step)
            nc.scalar.activation(V[:, :, g * 512:(g + 1) * 512], PS[:, b:b + 4, :], ACT.Copy).then_inc(free(step), 1)

        def exps(h):
            step = ("att S", h)
            act.wait_ge(mx_done, h + 1)
            if h >= 2:
                wait_full(act, ("att TO", h - 2))
                wait_free(act, ("att TO", h - 2))
            b = bank0(step)
            for it in range(NTT):
                n0 = block_of(it, 0) * P
                ins = nc.scalar.activation(PB[h % 2][:, n0:n0 + (it + 1) * P], PS[:, b + it, 0:(it + 1) * P], ACT.Exp,
                                           bias=MX[:, h % 2, it:it + 1], scale=MLA_SCALE,
                                           accum_out=LS[:, h % 2, it:it + 1])
            ins.then_inc(free(step), 1)

        exps(0)
        for h in range(MH + 1):
            if h % 2:
                s = h // 2
                act.wait_ge(sd_done, s + 1)
                nc.scalar.activation(SPB[s % 2][:], SPB[s % 2][:], ACT.Exp, scale=MLA_SCALE).then_inc(sp_done, 1)
            if h + 1 < MH:
                exps(h + 1)
        wait_full(act, ("att TO", MH - 2))
        a.splits(R)
        for v in range(2):
            step = f"att OT{v}"
            wait_full(act, step)
            b = bank0(step)
            nc.scalar.activation(XH[:, 4 * v:4 * v + 4, 0:NP_], PS[:, b:b + 4, :], ACT.Copy).then_inc(oh_done, 1)
            if v == 0:
                wait_free(act, "smp O")
                nc.scalar.activation(XH[:, :, NP_:T], OTS[:], ACT.Copy).then_inc(oh_done, 1)
        for g in range(4):
            a.splits(2)
            if g == 3:
                wait_full(act, ("wo", 3))
                for p in range(3):
                    a.highs(nn + 1, p)
            wait_free(act, ("wo", g))
            a.squares(nn + 1, g)
            a.splits(2)
        a.highs(nn + 1, 3)

    def dve(dve, a):
        link = a.link

        def latent(g, out):
            step = ("min", g)
            wait_full(dve, step)
            nc.vector.tensor_tensor(halves(out[:, 0, :]), acc(step)[:, 0:2, :], halves(RSTD[:]), ALU.mult)
            nc.vector.tensor_tensor(halves(out[:, 1, :]), acc(step)[:, 2:4, :], halves(RSTD[:]),
                                    ALU.mult).then_inc(free(step), 1)
            wait_free(dve, step)

        def uq(g):
            step = ("uq", g)
            wait_full(dve, step)
            for m in range(2):
                ins = nc.vector.tensor_tensor(halves(Q[:, 2 * g + m, :]), acc(step)[:, 2 * m:2 * m + 2, :], halves(TAB[:]),
                                              ALU.mult)
            ins.then_inc(free(step), 1)
            a.splits(2)

        for g in range(2):
            a.splits(2 if g else 4)
            if g == 0:
                a.stats(("min", 0), nn)
                dve.wait_ge(loaded, 32)
                link(nc.vector.tensor_tensor(TABK[64:128, :], TABR[64:128, :], RSTD[64:128, :], ALU.mult))
            latent(g, CQF[:, 2 * g:2 * g + 2, :])
            for m in range(2):
                t = 2 * g + m
                dve.wait_ge(xqh_done, t + 1)
                nc.vector.scalar_tensor_tensor(XQL[:, t, :], CQF[:, t, :], PV[:, V_QNORM + t:V_QNORM + t + 1],
                                               XQH[:, t, :].bitcast(F32), ALU.mult, ALU.subtract).then_inc(
                                                   xq_done, 1)
            if g:
                a.splits(2)
        a.splits(2)
        latent(2, CKF)
        a.splits(2)
        step = ("min", 3)
        wait_full(dve, step)
        nc.vector.tensor_tensor(halves(KRX[64:128, :]), PS[64:128, bank0(step):bank0(step) + 2, 0:TH],
                                halves(TABK[64:128, :]), ALU.mult).then_inc(free(step), 1)
        wait_free(dve, step)
        link(nc.vector.tensor_copy(KRB[64:96, :], KRX[96:128, :]))
        nc.vector.tensor_tensor(KRT[64:96, :], KRX[64:96, :], KRB[64:96, :], ALU.add).then_inc(kr_done, 1)
        dve.wait_ge(kr_done, 1)
        nc.vector.tensor_copy(KRT[96:128, :], KRT[64:96, :]).then_inc(kr_done, 1)
        a.splits(2)
        step = "mla cnorm"
        wait_full(dve, step)
        b = bank0(step)
        nc.vector.tensor_scalar(halves(V2[:, 0, :]), PS[:, b:b + 2, 0:TH], 1.0 / QL, EPS, ALU.mult, ALU.add)
        nc.vector.tensor_scalar(halves(V2[:, 1, :]), PS[:, b + 2:b + 4, 0:TH], 1.0 / KVL, EPS, ALU.mult,
                                ALU.add).then_inc(free(step), 1)
        wait_free(dve, step)
        nc.vector.reciprocal(V2[:, 0], V2[:, 0]).then_inc(lv_done, 1)
        dve.wait_ge(lr_done, 1)
        link(nc.vector.tensor_tensor(TAB[:], TABR[:], R2[:, 0, :], ALU.mult))
        uq(0)
        nc.vector.reciprocal(V2[:, 1], V2[:, 1]).then_inc(lv_done, 1)
        uq(1)
        dve.wait_ge(lr_done, 2)
        for t in range(2):
            nc.vector.scalar_tensor_tensor(CKF[:, t, :], CKF[:, t, :], PV[:, V_KVNORM + t:V_KVNORM + t + 1], R2[:, 1, :],
                                           ALU.mult, ALU.mult).then_inc(ckn_done, 1)
        for t in range(2):
            dve.wait_ge(ckh_done, t + 1)
            nc.vector.tensor_tensor(CKL[:, t, :], CKF[:, t, :], CKH[:, t, :].bitcast(F32), ALU.subtract).then_inc(ck_done, 1)
        for g in range(2, 8):
            uq(g)
        step = "smp qlat"
        nc.vector.memset(SSB[0][:, NPG * MH:], NEG)
        link(nc.vector.memset(SSB[1][:, NPG * MH:], NEG))
        wait_full(dve, step)
        b = bank0(step)
        for ct in range(2):
            ins = nc.vector.tensor_copy(QLAT[:, ct], PS[:, b + ct, 0:MH * NS].rearrange("p (h b) -> p b h", b=NS))
        ins.then_inc(free(step), 1)
        def smp_scores(bank, q, done):
            s, u = divmod(q, 2)
            ss = SSB[s % 2]
            ins = nc.vector.tensor_copy(ss[:, u * HALF * MH:(u + 1) * HALF * MH], bank[:, SC0:SC0 + HALF * MH])
            if u == 0:
                done(ins)
                return
            done(nc.vector.tensor_copy(ss[0:1, NPG * MH:], bank[0:1, SC0 + HALF * MH:SC0 + (HALF + 1) * MH]))
            by_head = ss[:].rearrange("p (g h) -> p h g", h=MH)
            nc.vector.tensor_reduce(MXP[:], by_head, AX.X, ALU.max).then_inc(smx_done, 1)

        def less_max(s):
            dve.wait_ge(sall_done, s + 1)
            nc.vector.tensor_tensor(SPB[s % 2][:], SSB[s % 2][:].rearrange("p (g h) -> p g h", h=MH),
                                    MXA[:].unsqueeze(1).broadcast_to([P, NPG + 1, MH]), ALU.subtract).then_inc(sd_done, 1)
            dve.wait_ge(sp_done, s + 1)
            nc.vector.tensor_reduce(LSUM[:], SPB[s % 2][:].rearrange("p g h -> p h g"), AX.X, ALU.add).then_inc(sl_done, 1)

        def smp_out(bank, s):
            for ct in range(2):
                ins = nc.vector.scalar_tensor_tensor(O2[:, ct, :], LPN[:, MH:2 * MH], CKF[:, ct, NP_ + s:NP_ + s + 1],
                                                     bank[:, SV0 + ct * MH:SV0 + (ct + 1) * MH], ALU.mult, ALU.add)
            link(ins)
            return nc.vector.tensor_tensor(OLAT[:, :, :, s], O2[:], LPN[:, 0:MH].unsqueeze(1).broadcast_to([P, 2, MH]),
                                           ALU.mult)

        def smp_values(b, q):
            s, u = divmod(q, 2)
            bank, out = PS[:, b + 3, :], PS[0:MH, b + 2, KVL:2 * KVL]
            if u == 0:
                if s:
                    link(smp_out(bank, s - 1))
                nc.vector.tensor_copy(OBH[:], out)
                link(nc.vector.tensor_copy(LPN[:], bank[:, SV0 + 2 * MH:SV0 + 4 * MH]))
                return nc.vector.reciprocal(LPN[:, 0:MH], LPN[:, 0:MH])
            else:
                return nc.vector.tensor_tensor(OBH[:], OBH[:], out, ALU.add)

        def first_scores(q):
            step = ("smp S", q)
            wait_full(dve, step)

            def done(ins):
                ins.then_inc(free(step), 1)
                wait_free(dve, step)

            smp_scores(PS[:, bank0(step) + 3, :], q, done)

        for g in range(4):
            step = ("uk", g)
            wait_full(dve, step)
            b = bank0(step)
            for m in range(2):
                for hh in range(2):
                    ins = nc.vector.tensor_copy(KTT[0:64, 4 * g + 2 * m + hh, :].rearrange("p (a t) -> p a t", a=2),
                                                PS[64 * hh:64 * hh + 64, b + 2 * m:b + 2 * m + 2, 0:NP_ // 2])
            ins.then_inc(free(step), 1)
            a.splits(1)
        first_scores(0)
        first_scores(1)

        def maxima(h):
            step = ("att S", h)
            wait_full(dve, step)
            if h >= 2:
                wait_free(dve, ("att S", h - 2))
            b = bank0(step)
            for it in range(NTT):
                ins = nc.vector.tensor_reduce(MX[:, h % 2, it:it + 1], PS[:, b + it, 0:(it + 1) * P], AX.X, ALU.max)
            link(ins)
            nc.vector.tensor_scalar(MX[:, h % 2, :], MX[:, h % 2, :], -MLA_SCALE, None, ALU.mult).then_inc(mx_done, 1)

        maxima(0)
        for h in range(MH + 1):
            if h % 2:
                less_max(h // 2)
            if h + 1 < MH:
                maxima(h + 1)
            if h < MH:
                wait_free(dve, ("att S", h))
                link(nc.vector.reciprocal(RL[:, h % 2, :], LS[:, h % 2, :]))
            step = ("att TO", h)
            wait_full(dve, step)
            b = bank0(step)
            bank = PS[:, b + 3, :]
            if h:
                nc.vector.tensor_tensor(OTOK[:, :, (h - 1) * VD:h * VD], bank[:, 0:NTT * VD].rearrange("p (i d) -> p i d", i=NTT),
                                        RL[:, (h - 1) % 2, :].unsqueeze(2).broadcast_to([P, NTT, VD]), ALU.mult)
                if h + 1 < 2 * NS:
                    smp_scores(bank, h + 1, link)
                ins = smp_values(b, h - 1)
            if 0 < h < MH:
                link(ins)
            if h < MH:
                ins = nc.vector.tensor_copy(PT[:], PS[:, b:b + 3, :].rearrange("p a n -> p (a n)")[:, 0:1280])
            ins.then_inc(free(step), 1)
            wait_free(dve, step)
        step = "smp T"
        wait_full(dve, step)
        smp_out(PS[:, bank0(step) + 3, :], NS - 1).then_inc(free(step), 1)
        a.splits(R)
        for v in range(2):
            step = f"att OT{v}"
            dve.wait_ge(oh_done, 2 * v + 1)
            b = bank0(step)
            nc.vector.tensor_tensor(XL[:, 4 * v:4 * v + 4, 0:NP_], PS[:, b:b + 4, :], XH[:, 4 * v:4 * v + 4, 0:NP_].bitcast(F32),
                                    ALU.subtract).then_inc(free(step), 1)
            if v == 0:
                step = "smp O"
                wait_full(dve, step)
                nc.vector.tensor_copy(OTS[:].rearrange("p t b -> p (t b)"), PS[:, bank0(step), 0:64]).then_inc(free(step), 1)
                dve.wait_ge(oh_done, 2)
                wait_free(dve, "att OT0")
                nc.vector.tensor_tensor(XL[:, :, NP_:T], OTS[:], XH[:, :, NP_:T].bitcast(F32),
                                        ALU.subtract).then_inc(ol_done, 1)
        for g in range(4):
            a.splits(2)
            if g == 3:
                wait_full(dve, ("wo", 3))
                a.lows(nn + 1, 0)
                a.lows(nn + 1, 1)
            a.residual(("wo", g), g, 1.0)
            a.splits(2)
        for g in range(2, 4):
            a.lows(nn + 1, g)

    def pool(pool, a):
        def store(dst, src):
            pool.dma_start(dst, src).then_inc(e.out_stored, 16)
            a.stores[0] += 1

        if before:
            wait_full(pool, (before, "out", 3))
            wait_free(pool, (before, "out", 3))
        pool.dma_start(TABR[:], io["mla_rope"]).then_inc(loaded, 16)
        pool.dma_start(PGT[:], io["page_table"]).then_inc(loaded, 16)
        wait_full(pool, ("min", 3))
        pool.dma_start(WUKT[:], io["w_uk_by_head"]).then_inc(wuk_loaded, 16)
        pool.wait_ge(kr_done, 2)
        nc.gpsimd.tensor_copy(KTT[64:128, :, :], KRT[64:128, 0:NP_].unsqueeze(1).broadcast_to([64, MH, NP_])).then_inc(krr_done, 1)
        store(io["kr"], KRT[64:96, :])
        pool.wait_ge(ckn_done, 2)
        store(io["ckv"], CKF[:])
        pool.wait_ge(krr_done, 1)
        for s in range(NS):
            pool.wait_ge(smx_done, s + 1)
            nc.gpsimd.partition_all_reduce(MXA[:], MXP[:], P, RMAX).then_inc(sall_done, 1)
        wait_full(pool, ("att TO", 2 * NS - 3))
        pool.dma_start(WUV[:], io["w_uv"]).then_inc(wuv_loaded, 16)
        a.norm_sums(nn + 1)
        pool.wait_ge(e.out_stored, 16 * a.stores[0])

    parts = Shared()
    parts.pe, parts.act, parts.dve, parts.pool, parts.sp = pe, act, dve, pool, sp
    return parts


def lay_out_mla(a, tile):
    f = np.float32
    pos = np.concatenate([np.arange(NP_), np.full(NS, PAST)]).astype(f)
    half = ROPE // 2
    inv = (np.float32(10000.0) ** (-np.arange(half, dtype=f) / half)).astype(f)
    ang = (inv[:, None] * pos[None]).astype(f).astype(np.float64)
    cos, sin = np.cos(ang), np.sin(ang)
    ckv, kr = a["cache_ckv"][0], a["cache_krope"][0]
    krt = kr.transpose(0, 2, 1)
    features = np.concatenate([ckv.reshape(N_PHYS, PAGE, 2, P).transpose(0, 3, 2, 1).reshape(N_PHYS, P, 2 * PAGE),
                               np.concatenate([np.zeros((N_PHYS, 64, PAGE), f), krt, krt], 1)], 2)
    return {
        "mla_rope": np.concatenate([np.ones((64, T)), cos, cos, -sin, sin], 0).astype(f),
        "cache_rows": ckv,
        "cache_features": features,
        "page_table": a["page_table"].reshape(1, NS * NPG),
        "w_uk_by_head": a["mla_w_uk"][0].transpose(2, 1, 0),
        "w_uv": a["mla_w_uv"][0].reshape(2, P, MH * VD).transpose(1, 0, 2),
    }


OUT_MLA = {"ckv": (P, 2, T), "kr": (ROPE, T)}


def mla_results(o):
    ckv = o["ckv"].transpose(1, 0, 2).reshape(KVL, T).T
    kr = o["kr"].T
    return (ckv[None, None, :NP_], ckv[None, NP_:, None], kr[None, None, :NP_], kr[None, NP_:, None])


def kernel(**inputs):
    import concourse.bacc as bacc
    from concourse.bass_utils import run_bass_kernel_spmd

    nc = bacc.Bacc("TRN2", target_bir_lowering=False, num_devices=1)
    arrays, io = {}, {}
    for name, a in lay_out(inputs).items():
        arrays[f"in_{name}_dram"] = a
        io[name] = nc.dram_tensor(f"in_{name}_dram", a.shape, mybir.dt.from_np(a.dtype), kind="ExternalInput").ap()
    shapes = outputs()
    for name, shape in shapes.items():
        io[name] = nc.dram_tensor(f"out_{name}_dram", shape, F32, kind="ExternalOutput").ap()
    program(nc, io)
    r = run_bass_kernel_spmd(nc, [arrays], core_ids=[0])
    o = {name: np.asarray(r.results[0][f"out_{name}_dram"]) for name in shapes}
    y = o["y"].transpose(1, 0, 2).reshape(D, T).T
    got = (y[None, :NP_], y[NP_:, None]) + tuple(hyb_results(o)) + tuple(mla_results(o))
    return tuple(np.ascontiguousarray(g) for g in got)
```
